# Optimizing a Trainium2 kernel written in Bass

```python
import math
import jax
import jax.numpy as jnp
from jax import lax
import numpy as np

D_MODEL = 2048
BATCH = 1
SEQ = 128
DEPTH = 2
DEC_BATCH = 1
DEC_SEQ = 512
PAST_LEN = 128

GRID_W = 64
EPS = 1e-6
CHUNK = 64
Q_BLOCK = 128
H_A = 4
DK_A = 128
DV_A = 128
W_A = H_A * DV_A
CONV_K = 5
H_B = 8
Q_LORA = 512
KV_LORA = 256
NOPE_DIM = 128
ROPE_DIM = 64
AXIS_ROPE = ROPE_DIM // 2
DV_B = 128
W_B = H_B * DV_B
ROPE_THETA = 10000.0
SM_SCALE = (NOPE_DIM + ROPE_DIM) ** -0.5
H_C = 4
DK_C = 128
DV_C = 128
W_C = H_C * DV_C
MIX_W = W_A + W_B + W_C
SPLIT_SIZES = (H_A * DK_A, H_A * DK_A, W_A, W_A, 2 * H_A, 2 * H_A,
               Q_LORA, KV_LORA, ROPE_DIM, W_B,
               H_C * DK_C, H_C * DK_C, W_C, W_C, W_C, 2 * H_C, 2 * H_C)
N_IN = sum(SPLIT_SIZES)

kernel_name = 'hybrid_gdn_mla_mlstm_diffusion_step'

def _rmsnorm(x, g):
    xf = x.astype(jnp.float32)
    y = xf * lax.rsqrt(jnp.mean(xf * xf, axis=-1, keepdims=True) + EPS)
    return (y * g.astype(jnp.float32)).astype(x.dtype)

def _l2norm(x):
    return x * lax.rsqrt(jnp.sum(x * x, axis=-1, keepdims=True) + EPS)

def _heads(x, h):
    b, l, _ = x.shape
    return x.reshape(b, l, h, -1).transpose(0, 2, 1, 3)

def _unheads(x):
    b, h, l, d = x.shape
    return x.transpose(0, 2, 1, 3).reshape(b, l, h * d)

def _flip(t):
    return jnp.flip(t, axis=2)

def _centred_dwconv(x, w):
    k = w.shape[0]
    return lax.conv_general_dilated(x, w[:, None, :].astype(x.dtype), (1,), [(k // 2, k // 2)],
                                    dimension_numbers=('NWC', 'WIO', 'NWC'),
                                    feature_group_count=x.shape[-1])

def _axial_angles(rows):
    row = jnp.repeat(jnp.arange(rows, dtype=jnp.float32), GRID_W)
    col = jnp.tile(jnp.arange(GRID_W, dtype=jnp.float32), rows)
    inv = ROPE_THETA ** (-jnp.arange(0, AXIS_ROPE, 2, dtype=jnp.float32) / AXIS_ROPE)
    return row[:, None] * inv, col[:, None] * inv

def _rope_half(x, ang):
    x1, x2 = jnp.split(x, 2, axis=-1)
    cos = jnp.cos(ang).astype(x.dtype)
    sin = jnp.sin(ang).astype(x.dtype)
    return jnp.concatenate([x1 * cos - x2 * sin, x1 * sin + x2 * cos], axis=-1)

def _axial_rope(x, ang_row, ang_col):
    xr, xc = jnp.split(x, 2, axis=-1)
    return jnp.concatenate([_rope_half(xr, ang_row), _rope_half(xc, ang_col)], axis=-1)

def _modulate(x, cond, p):
    mod = jax.nn.silu(cond) @ p['w_ada'] + p['b_ada']
    shift, scale, gate = jnp.split(mod[:, None, :], 3, axis=-1)
    h = _rmsnorm(x, p['g_pre']) * (1 + scale) + shift
    return h, gate

def _split_proj(h, w_in):
    points = np.cumsum(SPLIT_SIZES)[:-1].tolist()
    return jnp.split(h @ w_in, points, axis=-1)

def _gdn_chunked(q, k, v, g, beta, s0):
    b, h, l, dk = q.shape
    n = l // CHUNK

    def chunks(t):
        return t.reshape(b, h, n, CHUNK, *t.shape[3:])

    q = chunks(q * dk ** -0.5)
    k = chunks(k)
    v = chunks(v)
    beta = chunks(beta)
    g = jnp.cumsum(chunks(g), axis=-1)
    incl = jnp.tril(jnp.ones((CHUNK, CHUNK), dtype=bool))
    strict = jnp.tril(jnp.ones((CHUNK, CHUNK), dtype=bool), -1)
    decay = jnp.exp(jnp.where(incl, g[..., :, None] - g[..., None, :], -jnp.inf))
    kb = k * beta[..., None]
    vb = v * beta[..., None]
    a = jnp.where(strict, jnp.einsum('bhncd,bhnsd->bhncs', kb, k) * decay, 0.0)
    eye = jnp.eye(CHUNK, dtype=a.dtype)
    t = lax.linalg.triangular_solve(a + eye, jnp.broadcast_to(eye, a.shape),
                                    left_side=True, lower=True, unit_diagonal=True)
    u = jnp.einsum('bhncs,bhnsv->bhncv', t, vb)
    w = jnp.einsum('bhncs,bhnsk->bhnck', t, kb * jnp.exp(g)[..., None])
    qk = jnp.einsum('bhncd,bhnsd->bhncs', q, k) * decay
    g_last = g[..., -1]
    q_dec = q * jnp.exp(g)[..., None]
    k_dec = k * jnp.exp(g_last[..., None] - g)[..., None]

    def step(s, xs):
        qd, kd, uc, wc, qkc, gl = xs
        v_new = uc - jnp.einsum('bhck,bhkv->bhcv', wc, s)
        o = jnp.einsum('bhck,bhkv->bhcv', qd, s) + jnp.einsum('bhcs,bhsv->bhcv', qkc, v_new)
        s = s * jnp.exp(gl)[..., None, None] + jnp.einsum('bhck,bhcv->bhkv', kd, v_new)
        return s, o

    xs = tuple(jnp.moveaxis(z, 2, 0) for z in (q_dec, k_dec, u, w, qk, g_last))
    s_fin, o = lax.scan(step, s0, xs)
    return jnp.moveaxis(o, 0, 2).reshape(b, h, l, -1), s_fin

def _mlstm_chunked(q, k, v, i_pre, logf, c0, n0, m0):
    b, h, l, dk = q.shape
    n = l // CHUNK

    def chunks(t):
        return t.reshape(b, h, n, CHUNK, *t.shape[3:])

    q = chunks(q * dk ** -0.5)
    k = chunks(k)
    v = chunks(v)
    i_pre = chunks(i_pre)
    bcum = jnp.cumsum(chunks(logf), axis=-1)
    incl = jnp.tril(jnp.ones((CHUNK, CHUNK), dtype=bool))
    logd = jnp.where(incl, bcum[..., :, None] - bcum[..., None, :] + i_pre[..., None, :], -jnp.inf)
    qk = jnp.einsum('bhncd,bhnsd->bhncs', q, k)
    b_last = bcum[..., -1]
    logw = b_last[..., None] - bcum + i_pre

    def step(carry, xs):
        cm, nm, m = carry
        qc, kc, vc, bc, ld, qkc, bl, lw = xs
        m_inter = bc + m[..., None]
        m_t = jnp.maximum(m_inter, jnp.max(ld, axis=-1))
        w_inter = jnp.exp(m_inter - m_t)
        s = qkc * jnp.exp(ld - m_t[..., None])
        num = (w_inter[..., None] * jnp.einsum('bhck,bhkv->bhcv', qc, cm)
               + jnp.einsum('bhcs,bhsv->bhcv', s, vc))
        den = w_inter * jnp.einsum('bhck,bhk->bhc', qc, nm) + jnp.sum(s, axis=-1)
        hc = num / jnp.maximum(jnp.abs(den), jnp.exp(-m_t))[..., None]
        m_new = jnp.maximum(bl + m, jnp.max(lw, axis=-1))
        dec = jnp.exp(bl + m - m_new)
        wk = kc * jnp.exp(lw - m_new[..., None])[..., None]
        cm = dec[..., None, None] * cm + jnp.einsum('bhck,bhcv->bhkv', wk, vc)
        nm = dec[..., None] * nm + jnp.sum(wk, axis=2)
        return (cm, nm, m_new), hc

    xs = tuple(jnp.moveaxis(z, 2, 0) for z in (q, k, v, bcum, logd, qk, b_last, logw))
    (cf, nf, mf), hs = lax.scan(step, (c0, n0, m0), xs)
    return jnp.moveaxis(hs, 0, 2).reshape(b, h, l, -1), cf, nf, mf

def _gdn_branch(qa, ka, va, za, ga, ba, p, s0):
    f32 = jnp.float32
    b, l, _ = qa.shape
    qkv = jax.nn.silu(_centred_dwconv(jnp.concatenate([qa, ka, va], axis=-1), p['gdn_conv']).astype(f32))
    q, k, v = jnp.split(qkv, [H_A * DK_A, 2 * H_A * DK_A], axis=-1)
    q = _l2norm(_heads(q, H_A))
    k = _l2norm(_heads(k, H_A))
    v = _heads(v, H_A)
    ga = ga.astype(f32).reshape(b, l, 2, H_A).transpose(2, 0, 3, 1)
    ba = ba.astype(f32).reshape(b, l, 2, H_A).transpose(2, 0, 3, 1)
    g = -jnp.exp(p['gdn_a_log'].astype(f32))[:, None, :, None] * jax.nn.softplus(
        ga + p['gdn_dt_bias'].astype(f32)[:, None, :, None])
    beta = jax.nn.sigmoid(ba)
    s0 = s0.astype(f32)
    o_f, s_f = _gdn_chunked(q, k, v, g[0], beta[0], s0[:, 0])
    o_b, s_b = _gdn_chunked(_flip(q), _flip(k), _flip(v), _flip(g[1]), _flip(beta[1]), s0[:, 1])
    o = _rmsnorm(o_f + _flip(o_b), p['gdn_norm'])
    out = _unheads(o) * jax.nn.silu(za.astype(f32))
    return out.astype(za.dtype), jnp.stack([s_f, s_b], axis=1)

def _mlstm_branch(qc, kc, vc, oc, zc, ic, fc, p, c0, n0, m0):
    f32 = jnp.float32
    b, l, _ = qc.shape
    q = _heads(qc.astype(f32), H_C)
    k = _heads(kc.astype(f32), H_C)
    v = _heads(vc.astype(f32), H_C)
    i_pre = (ic.astype(f32).reshape(b, l, 2, H_C).transpose(2, 0, 3, 1)
             + p['mlstm_b_i'].astype(f32)[:, None, :, None])
    logf = jax.nn.log_sigmoid(fc.astype(f32).reshape(b, l, 2, H_C).transpose(2, 0, 3, 1)
                              + p['mlstm_b_f'].astype(f32)[:, None, :, None])
    c0 = c0.astype(f32)
    n0 = n0.astype(f32)
    m0 = m0.astype(f32)
    h_f, c_f, n_f, m_f = _mlstm_chunked(q, k, v, i_pre[0], logf[0], c0[:, 0], n0[:, 0], m0[:, 0])
    h_b, c_b, n_b, m_b = _mlstm_chunked(_flip(q), _flip(k), _flip(v), _flip(i_pre[1]), _flip(logf[1]),
                                        c0[:, 1], n0[:, 1], m0[:, 1])
    hh = _rmsnorm(h_f + _flip(h_b), p['mlstm_norm'])
    out = _unheads(hh) * jax.nn.sigmoid(oc.astype(f32)) * jax.nn.silu(zc.astype(f32))
    states = (jnp.stack([c_f, c_b], axis=1), jnp.stack([n_f, n_b], axis=1), jnp.stack([m_f, m_b], axis=1))
    return out.astype(zc.dtype), states

def _mla_queries(cq, p, ang_row=None, ang_col=None):
    b, l, _ = cq.shape
    q = (_rmsnorm(cq, p['mla_q_norm']) @ p['mla_w_uq']).reshape(b, l, H_B, NOPE_DIM + ROPE_DIM)
    q_pe = q[..., NOPE_DIM:]
    if ang_row is not None:
        q_pe = _axial_rope(q_pe, ang_row, ang_col)
    return jnp.concatenate([q[..., :NOPE_DIM], q_pe], axis=-1) * SM_SCALE

def _mla_keys_values(ckv_n, k_rope, p):
    b, l, _ = ckv_n.shape
    kv = (ckv_n @ p['mla_w_ukv']).reshape(b, l, H_B, NOPE_DIM + DV_B)
    k_pe = jnp.broadcast_to(k_rope[:, :, None, :], (b, l, H_B, ROPE_DIM))
    return jnp.concatenate([kv[..., :NOPE_DIM], k_pe], axis=-1), kv[..., NOPE_DIM:]

def _block_attention(q, k, v):
    b, lq, h, dqk = q.shape
    nb = lq // Q_BLOCK
    qb = jnp.moveaxis(q.reshape(b, nb, Q_BLOCK, h, dqk), 1, 0)

    def one_block(qi):
        s = jnp.einsum('bqhd,bkhd->bhqk', qi, k).astype(jnp.float32)
        pr = jax.nn.softmax(s, axis=-1).astype(v.dtype)
        return jnp.einsum('bhqk,bkhd->bqhd', pr, v)

    o = lax.map(one_block, qb)
    return jnp.moveaxis(o, 0, 1).reshape(b, lq, h, v.shape[-1])

def _context_layer(x, c_ctx, p):
    b, l, _ = x.shape
    f32 = jnp.float32
    h, gate = _modulate(x, c_ctx[None, :], p)
    (qa, ka, va, za, ga, ba, cq, ckv, kr, zb,
     qc, kc, vc, oc, zc, ic, fc) = _split_proj(h, p['w_in'])
    out_a, s_gdn = _gdn_branch(qa, ka, va, za, ga, ba, p, jnp.zeros((b, 2, H_A, DK_A, DV_A), f32))
    ckv_n = _rmsnorm(ckv, p['mla_kv_norm'])
    k, v = _mla_keys_values(ckv_n, kr, p)
    att = _block_attention(_mla_queries(cq, p), k, v)
    out_b = att.reshape(b, l, W_B) * jax.nn.silu(zb)
    out_c, (cm, nm, mm) = _mlstm_branch(qc, kc, vc, oc, zc, ic, fc, p,
                                        jnp.zeros((b, 2, H_C, DK_C, DV_C), f32),
                                        jnp.zeros((b, 2, H_C, DK_C), f32),
                                        jnp.zeros((b, 2, H_C), f32))
    y = jnp.concatenate([out_a, out_b, out_c], axis=-1) @ p['w_out']
    x = x + gate * _rmsnorm(y, p['g_post'])
    return x, (ckv_n, kr, s_gdn, cm, nm, mm)

def _latent_layer(x, c, cache, p, ang_row, ang_col):
    ckv_ctx, kr_ctx, s_gdn0, c0, n0, m0 = cache
    b, l, _ = x.shape
    h, gate = _modulate(x, c, p)
    (qa, ka, va, za, ga, ba, cq, ckv, kr, zb,
     qc, kc, vc, oc, zc, ic, fc) = _split_proj(h, p['w_in'])
    out_a, _ = _gdn_branch(qa, ka, va, za, ga, ba, p, s_gdn0)
    q = _mla_queries(cq, p, ang_row[:, None, :], ang_col[:, None, :])
    k_ctx, v_ctx = _mla_keys_values(ckv_ctx.astype(x.dtype), kr_ctx.astype(x.dtype), p)
    k_lat, v_lat = _mla_keys_values(_rmsnorm(ckv, p['mla_kv_norm']), _axial_rope(kr, ang_row, ang_col), p)
    att = _block_attention(q, jnp.concatenate([k_ctx, k_lat], axis=1), jnp.concatenate([v_ctx, v_lat], axis=1))
    out_b = att.reshape(b, l, W_B) * jax.nn.silu(zb)
    out_c, _ = _mlstm_branch(qc, kc, vc, oc, zc, ic, fc, p, c0, n0, m0)
    y = jnp.concatenate([out_a, out_b, out_c], axis=-1) @ p['w_out']
    return x + gate * _rmsnorm(y, p['g_post'])

def setup_inputs(seed: int = 0) -> dict:
    key = jax.random.key(seed)
    ks = iter(jax.random.split(key, 32))
    f32 = jnp.float32

    def nrm(shape, scale=1.0):
        return scale * jax.random.normal(next(ks), shape, f32)

    def gain(shape):
        return 1.0 + 0.01 * jax.random.normal(next(ks), shape, f32)

    x_prompt = nrm((BATCH, SEQ, D_MODEL))
    x_sample = nrm((DEC_BATCH, DEC_SEQ, D_MODEL))
    cache_mla_ckv = nrm((DEC_BATCH, DEPTH, PAST_LEN, KV_LORA))
    cache_mla_krope = nrm((DEC_BATCH, DEPTH, PAST_LEN, ROPE_DIM))
    state_gdn = nrm((DEC_BATCH, DEPTH, 2, H_A, DK_A, DV_A), 0.1)
    state_mlstm_c = nrm((DEC_BATCH, DEPTH, 2, H_C, DK_C, DV_C), 0.1)
    state_mlstm_n = nrm((DEC_BATCH, DEPTH, 2, H_C, DK_C), 0.1)
    state_mlstm_m = nrm((DEC_BATCH, DEPTH, 2, H_C))
    c = nrm((DEC_BATCH, D_MODEL))
    c_ctx = nrm((D_MODEL,))
    w_ada = nrm((DEPTH, D_MODEL, 3 * D_MODEL), 0.5 * D_MODEL ** -0.5)
    b_ada = nrm((DEPTH, 3 * D_MODEL), 0.01)
    g_pre = gain((DEPTH, D_MODEL))
    g_post = gain((DEPTH, D_MODEL))
    w_in = nrm((DEPTH, D_MODEL, N_IN), D_MODEL ** -0.5)
    gdn_conv = nrm((DEPTH, CONV_K, 2 * H_A * DK_A + W_A), CONV_K ** -0.5)
    gdn_a_log = jnp.log(jax.random.uniform(next(ks), (DEPTH, 2, H_A), f32, 1.0, 16.0))
    dt = jnp.exp(jax.random.uniform(next(ks), (DEPTH, 2, H_A), f32, math.log(1e-3), math.log(1e-1)))
    gdn_dt_bias = dt + jnp.log(-jnp.expm1(-dt))
    gdn_norm = gain((DEPTH, DV_A))
    mla_q_norm = gain((DEPTH, Q_LORA))
    mla_kv_norm = gain((DEPTH, KV_LORA))
    mla_w_uq = nrm((DEPTH, Q_LORA, H_B * (NOPE_DIM + ROPE_DIM)), Q_LORA ** -0.5)
    mla_w_ukv = nrm((DEPTH, KV_LORA, H_B * (NOPE_DIM + DV_B)), KV_LORA ** -0.5)
    mlstm_b_i = nrm((DEPTH, 2, H_C), 0.1)
    mlstm_b_f = 3.0 + 3.0 * jax.random.uniform(next(ks), (DEPTH, 2, H_C), f32)
    mlstm_norm = gain((DEPTH, DV_C))
    w_out = nrm((DEPTH, MIX_W, D_MODEL), MIX_W ** -0.5)
    return {'x_prompt': x_prompt, 'x_sample': x_sample,
            'cache_mla_ckv': cache_mla_ckv, 'cache_mla_krope': cache_mla_krope,
            'state_gdn': state_gdn, 'state_mlstm_c': state_mlstm_c,
            'state_mlstm_n': state_mlstm_n, 'state_mlstm_m': state_mlstm_m,
            'c': c, 'c_ctx': c_ctx, 'w_ada': w_ada, 'b_ada': b_ada,
            'g_pre': g_pre, 'g_post': g_post, 'w_in': w_in,
            'gdn_conv': gdn_conv, 'gdn_a_log': gdn_a_log, 'gdn_dt_bias': gdn_dt_bias,
            'gdn_norm': gdn_norm, 'mla_q_norm': mla_q_norm, 'mla_kv_norm': mla_kv_norm,
            'mla_w_uq': mla_w_uq, 'mla_w_ukv': mla_w_ukv,
            'mlstm_b_i': mlstm_b_i, 'mlstm_b_f': mlstm_b_f, 'mlstm_norm': mlstm_norm,
            'w_out': w_out}

def reference(x_prompt, x_sample, cache_mla_ckv, cache_mla_krope, state_gdn, state_mlstm_c,
              state_mlstm_n, state_mlstm_m, c, c_ctx, w_ada, b_ada, g_pre, g_post, w_in,
              gdn_conv, gdn_a_log, gdn_dt_bias, gdn_norm, mla_q_norm, mla_kv_norm,
              mla_w_uq, mla_w_ukv, mlstm_b_i, mlstm_b_f, mlstm_norm, w_out):
    rows = x_sample.shape[1] // GRID_W
    ang_row, ang_col = _axial_angles(rows)
    xp = x_prompt
    xs = x_sample
    ctx_states = []
    for l in range(DEPTH):
        p = {'w_ada': w_ada[l], 'b_ada': b_ada[l], 'g_pre': g_pre[l], 'g_post': g_post[l],
             'w_in': w_in[l], 'gdn_conv': gdn_conv[l], 'gdn_a_log': gdn_a_log[l],
             'gdn_dt_bias': gdn_dt_bias[l], 'gdn_norm': gdn_norm[l],
             'mla_q_norm': mla_q_norm[l], 'mla_kv_norm': mla_kv_norm[l],
             'mla_w_uq': mla_w_uq[l], 'mla_w_ukv': mla_w_ukv[l],
             'mlstm_b_i': mlstm_b_i[l], 'mlstm_b_f': mlstm_b_f[l], 'mlstm_norm': mlstm_norm[l],
             'w_out': w_out[l]}
        xp, st = _context_layer(xp, c_ctx, p)
        ctx_states.append(st)
        cache_l = (cache_mla_ckv[:, l], cache_mla_krope[:, l], state_gdn[:, l],
                   state_mlstm_c[:, l], state_mlstm_n[:, l], state_mlstm_m[:, l])
        xs = _latent_layer(xs, c, cache_l, p, ang_row, ang_col)
    new_mla_ckv = jnp.stack([s[0] for s in ctx_states], axis=1)
    new_mla_krope = jnp.stack([s[1] for s in ctx_states], axis=1)
    new_gdn = jnp.stack([s[2] for s in ctx_states], axis=1)
    new_mlstm_c = jnp.stack([s[3] for s in ctx_states], axis=1)
    new_mlstm_n = jnp.stack([s[4] for s in ctx_states], axis=1)
    new_mlstm_m = jnp.stack([s[5] for s in ctx_states], axis=1)
    return (xp, xs, new_mla_ckv, new_mla_krope, new_gdn, new_mlstm_c, new_mlstm_n, new_mlstm_m)


_drawn_inputs = setup_inputs


def setup_inputs(seed=0):
    import zlib

    import numpy as np

    out = dict(_drawn_inputs(seed))
    spreads = {}
    factors = {'cache_mla_ckv': 3.491,
     'cache_mla_krope': 6.565,
     'state_mlstm_c': 8.0,
     'state_mlstm_n': 8.0,
     'state_mlstm_m': 8.0,
     'g_pre': 2.952,
     'g_post': 8.0,
     'gdn_norm': 8.0,
     'mla_q_norm': 8.0,
     'mla_kv_norm': 5.887,
     'mlstm_norm': 24.4,
     'mlstm_b_i': 5.978}
    for name, (base, spread) in spreads.items():
        noise = np.random.default_rng([zlib.crc32(name.encode()), seed]).standard_normal(out[name].shape)
        drawn = base * np.exp(spread * noise) if base else spread * noise
        out[name] = jnp.asarray(drawn.astype(out[name].dtype))
    for name, factor in factors.items():
        out[name] = (out[name] * factor).astype(out[name].dtype)
    return out
```

```python
import math
from contextlib import ExitStack

import numpy as np
import concourse.bass as bass
from concourse import mybir

F32 = mybir.dt.float32
F32R = mybir.dt.float32r
F16 = mybir.dt.float16
ACT = mybir.ActivationFunctionType
ALU = mybir.AluOpType
AX = mybir.AxisListType.X

P = 128
DEPTH, D_MODEL, CTX, LAT = 2, 2048, 128, 512
TOK = CTX + LAT
TILES = TOK // P
HALF = TOK // 2
KT = D_MODEL // P
H_A, H_B, H_C = 4, 8, 4
Q_TILES, KV_TILES = 4, 2
PAST = 128
KEYS = TOK + PAST
EPS = 1e-6
CONV_K = 5
PADW = TOK + 8
CONVW = TOK + 4
SM_SCALE = float((128 + 64) ** -0.5)
DK_SCALE = float(P ** -0.5)
NEG = -1.0e30
LEVELS = 7
GATE_COLS = 104

ADA_HALVES = 2 * 3 * KT
STREAM = dict(gates=2, gdn=8 * H_A, mlstm=10 * H_C, mla_in=30, mla=2 * H_B, out=2 * KT)
STREAM_HALVES = sum(STREAM.values())
CELLS = 8
RAW_SLOTS = 4

C_ID, C_ONE, C_NEG, C_FOLD, C_ROPE = 0, 128, 256, 512, 640
C_WIDTH = C_ROPE + TOK
PRM = {}
_at = 0
for _n, _w in (("b_ada", 48), ("g_pre", 16), ("g_post", 16), ("conv", 12 * CONV_K), ("gdn_norm", 1),
               ("q_norm", 4), ("kv_norm", 2), ("mlstm_norm", 1), ("gates", 4)):
    PRM[_n] = _at
    _at += _w
PRM_WIDTH = _at


class Stage:

    def __init__(self, name, sems, passed, book):
        self.name, self.sems, self.passed = name, sems, passed
        self.book = book.setdefault(name, {e: {} for e in sems})
        self.total = {e: self.book[e].get("", 1) for e in sems}

    def body(self, me, eng, turn):
        return Body(self, me, eng, turn)


class Body:

    def __init__(self, stage, me, eng, turn):
        self.stage, self.me, self.eng, self.n = stage, me, eng, 0
        self.base = {e: 0 if turn is None else eng.snap(turn * stage.total[e]) for e in stage.sems}
        self.seen = {}

    def value(self, who, n):
        return self.base[who] + n

    def did(self, ins, label=None):
        ins.then_inc(self.stage.sems[self.me], 1)
        self.n += 1
        if label:
            self.stage.book[self.me][label] = self.n
        return ins

    def link(self, ins, label=None):
        self.did(ins, label)
        self.eng.wait_ge(self.stage.sems[self.me], self.value(self.me, self.n))

    def wait(self, who, label):
        n = self.stage.book[who].get(label, 1)
        if self.seen.get(who, 0) < n:
            self.seen[who] = n
            self.eng.wait_ge(self.stage.sems[who], self.value(who, n))

    def end(self):
        self.stage.book[self.me][""] = self.n
        for who in self.stage.sems:
            n = self.n if who == self.me else self.stage.total[who]
            self.eng.wait_ge(self.stage.sems[who], self.value(who, n))
        self.eng.sem_inc(self.stage.passed, 1)


def build(nc, io, book):
    ctx = ExitStack()
    with ctx:
        def sb(name, shape, dt=F32):
            return ctx.enter_context(nc.sbuf_tensor(name, shape, dt))

        def ps(name, shape):
            return ctx.enter_context(nc.psum_tensor(name, shape, F32))

        def sem(name):
            return ctx.enter_context(nc.semaphore(name))

        def stage(name, engines="pe act dve"):
            return Stage(name, {e: sem(f"{name}_{e}_steps") for e in engines.split()}, sem(f"{name}_passed"), book)

        h_hi = sb("h_hi", [P, KT, TOK], F32R)
        h_lo = sb("h_lo", [P, KT, TOK], F32R)
        xo = sb("xo", [P, KT, TOK])
        raw = sb("raw", [P, RAW_SLOTS, CELLS, P])
        w_hi = sb("w_hi", [P, 2, CELLS, P], F32R)
        w_lo = sb("w_lo", [P, 2, CELLS, P], F32R)
        W = sb("work", [P, 17, TOK])
        con = sb("constants", [P, C_WIDTH])
        lvl = sb("level_masks", [P, 2, LEVELS, P], F16)
        prm = sb("parameters", [P, PRM_WIDTH])
        cond = sb("cond", [P, KT, 2])
        cond_t = sb("cond_t", [P, KT, 2])
        mod = sb("mod", [P, 3 * KT, 2])
        mul = sb("mul", [P, KT, 2])
        tokc = sb("token_columns", [P, 5, TILES, 8])
        colt = sb("column_temps", [P, 12, TILES])
        hcw = sb("head_conv", [P, 3, CONV_K])
        state = sb("state", [P, 2, 2 * P])
        mxs = sb("row_sums", [P, 4, TILES])
        mprev = sb("m_prev", [8, 2, TILES])
        m0 = sb("m0", [8, 1])
        mout = sb("m_out", [8, 2])
        n0 = sb("n0", [P, 1])
        cst = sb("small_constants", [P, 3])

        pj = [ps(f"projection{i}", [P, 2, 512]) for i in range(2)]
        wa = ps("wa", [P, 1024])
        wb = ps("wb", [P, 1024])

        rows = nc.dram_tensor("rows", [5, 8, TOK], F32, kind="Internal").ap()
        x_kept = nc.dram_tensor("x_kept", [P, KT, TOK], F32, kind="Internal").ap()

        ident = con[:, C_ID:C_ID + P]
        ones = con[:, C_ONE:C_ONE + P]

        def neg(d):
            return con[:, C_NEG + d * P:C_NEG + (d + 1) * P]

        def tiled(ap):
            return ap.rearrange("p (t c) -> p t c", c=P)

        def over_tiles(ap):
            return ap.unsqueeze(1).to_broadcast([P, TILES, P])

        def over_cols(ap):
            return ap.unsqueeze(2).to_broadcast([P, TILES, P])

        def halves(ap):
            return ap.rearrange("p (a n) -> p a n", a=2)

        def wt(i):
            return W[:, i, :]

        def T(ap, t):
            return ap[:, t * P:(t + 1) * P]

        def flat(i, n):
            return W[:, i:i + 2, :].rearrange("p a n -> p (a n)")[:, 0:n]

        raw_full = [sem(f"raw_full{s}") for s in range(RAW_SLOTS)]
        raw_free = [sem(f"raw_free{s}") for s in range(RAW_SLOTS)]
        split_done = sem("split_done")
        split_part = sem("split_part")
        split_used = sem("split_used")
        const_in = sem("const_in")
        x_in = sem("x_in")
        params_in = sem("params_in")
        x_saved = sem("x_saved")
        x_back = [sem(f"x_back{i}") for i in range(2)]
        rows_out = sem("rows_out")
        m0_in = sem("m0_in")
        m_out = sem("m_out_stored")
        rows_in = [sem(f"rows_in{d}") for d in range(2)]
        state_in = [sem(f"state_in{d}") for d in range(2)]
        state_out = [sem(f"state_out{d}") for d in range(2)]
        crows_in = [sem(f"mlstm_rows_in{d}") for d in range(2)]
        cstate_in = [sem(f"mlstm_state_in{d}") for d in range(2)]
        cstate_out = [sem(f"mlstm_state_out{d}") for d in range(2)]
        cache_in = sem("cache_in")
        latent_out = sem("latent_out")
        y_out = sem("y_out")

        s_init = stage("init", "act dve")
        s_ada = stage("ada", "pe dve")
        s_norm = stage("norm")
        s_gate = stage("gates")
        s_gdn = stage("gdn")
        s_mls = stage("mlstm")
        s_min = stage("mla_in")
        s_mla = stage("mla")
        s_spl = stage("out_split", "dve pe")
        s_out = stage("out", "pe dve")
        s_res = stage("residual")

        block = ctx.enter_context(nc.Block())

        @block.sync
        def _(sp):
            sp.dma_start(con[:, :], io["constants"]).then_inc(const_in, 16)
            sp.dma_start(lvl[:, :, :, :], io["levels"]).then_inc(const_in, 16)
            sp.dma_start(cond_t[:, :, :], io["cond"]).then_inc(const_in, 16)
            sp.dma_start(xo[:, :, :], io["x"]).then_inc(x_in, 16)
            for s in range(RAW_SLOTS):
                sp.sem_inc(raw_free[s], 1)
            per_layer = (ADA_HALVES + STREAM_HALVES) // RAW_SLOTS
            with sp.Fori(0, DEPTH) as l:
                for n, first, src in ((ADA_HALVES, 0, io["w_ada"]),
                                      (STREAM_HALVES, ADA_HALVES // RAW_SLOTS, io["w_stream"])):
                    with sp.Fori(0, n // RAW_SLOTS) as i:
                        turn = sp.snap(l * per_layer + i + first + 1)
                        for s in range(RAW_SLOTS):
                            sp.wait_ge(raw_free[s], turn)
                            sp.dma_start(raw[:, s, :, :].rearrange("p c n -> p (c n)"),
                                         src[l, i * RAW_SLOTS + s, :, :]).then_inc(raw_full[s], 16)

        @block.gpsimd
        def _(pool):
            once = ones.unsqueeze(1).to_broadcast([P, CELLS, P])
            pool.wait_ge(const_in, 48)
            pool.sem_inc(split_used, 2)
            per_layer = (ADA_HALVES + STREAM_HALVES) // RAW_SLOTS
            with pool.Fori(0, DEPTH) as l:
                with pool.Fori(0, STREAM_HALVES // RAW_SLOTS) as i:
                    turn = pool.snap((l * per_layer + i + (ADA_HALVES // RAW_SLOTS + 1)) * 16)
                    done = pool.snap((l * (STREAM_HALVES // RAW_SLOTS) + i) * RAW_SLOTS)
                    for s in range(RAW_SLOTS):
                        pool.wait_ge(split_used, done + s + 1)
                        pool.wait_ge(raw_full[s], turn)
                        nc.gpsimd.tensor_tensor(w_hi[:, s % 2, :, :], raw[:, s, :, :], once, ALU.mult).then_inc(split_part, 1)
                        pool.wait_ge(split_part, done * 2 + 2 * s + 1)
                        nc.gpsimd.tensor_tensor(w_lo[:, s % 2, :, :], raw[:, s, :, :],
                                                w_hi[:, s % 2, :, :].bitcast(F32), ALU.subtract)\
                            .then_inc(split_part, 1)
                        pool.wait_ge(split_part, done * 2 + 2 * s + 2)
                        pool.sem_inc(raw_free[s], 1)
                        pool.sem_inc(split_done, 1)

        @block.tensor
        def _(pe):
            mm = nc.tensor.matmul

            def parts_ready(n):
                pe.wait_ge(split_done, n + 1)

            def project(out, n):
                last = None
                for half in range(2):
                    parts_ready(n + half)
                    for c in range(CELLS):
                        k = half * CELLS + c
                        for a in range(2):
                            hs = slice(a * HALF, (a + 1) * HALF)
                            o = out[:, a, 0:HALF]
                            mm(o, w_hi[:, half, c, :], h_hi[:, k, hs], start=(k == 0), stop=False)
                            mm(o, w_hi[:, half, c, :], h_lo[:, k, hs], start=False, stop=False)
                            last = mm(o, w_lo[:, half, c, :], h_hi[:, k, hs], start=False, stop=(k == KT - 1))
                    if half == 0:
                        last.then_inc(split_used, 1)
                return last

            def used_and(B, last, n, label):
                last.then_inc(split_used, 1)
                pe.wait_ge(split_used, n + 2)
                B.did(pe.nop(), label)

            def each_tile(out, lhs, rhs):
                last = None
                for t in range(TILES):
                    last = mm(T(out, t), T(lhs, t), T(rhs, t), start=True, stop=True)
                return last

            def transposed(out, src):
                last = None
                for t in range(TILES):
                    last = nc.tensor.transpose(T(out, t), T(src, t), ident)
                return last

            def column_sums(out, src, first=True, last=True):
                mm(out[:, 0:512], ones, src[:, 0:512], start=first, stop=last)
                return mm(out[:, 512:TOK], ones, src[:, 512:TOK], start=first, stop=last)

            pe.wait_ge(const_in, 48)
            with pe.Fori(0, DEPTH) as l:
                per_layer = (ADA_HALVES + STREAM_HALVES) // RAW_SLOTS
                with pe.Fori(0, ADA_HALVES // RAW_SLOTS) as i:
                    B = s_ada.body("pe", pe, l * (ADA_HALVES // RAW_SLOTS) + i)
                    turn = pe.snap((l * per_layer + i + 1) * 16)
                    if True:
                        pe.wait_ge(s_init.sems["dve"], s_init.total["dve"])
                    for s in range(RAW_SLOTS):
                        pe.wait_ge(raw_full[s], turn)
                        j = s // 2
                        for c in range(CELLS):
                            k = (s % 2) * CELLS + c
                            last = mm(wa[:, 2 * j:2 * j + 2], raw[:, s, c, :], cond[:, k, :],
                                      start=(k == 0), stop=(k == KT - 1))
                        last.then_inc(raw_free[s], 1)
                    pe.wait_ge(raw_free[RAW_SLOTS - 1], l * per_layer + i + 2)
                    B.did(pe.nop(), "two tiles")
                    B.end()

                B = s_norm.body("pe", pe, l)
                for k in range(KT):
                    B.wait("act", f"square{k}")
                    B.did(column_sums(wa, wt(k % 4), k == 0, k == KT - 1), f"sum{k}")
                B.end()

                layer0 = pe.snap(l * STREAM_HALVES)
                B = s_gate.body("pe", pe, l)
                used_and(B, project(pj[0], layer0), layer0 + 2, "gates")
                for n, (label, src) in enumerate((("cum", 10), ("cum", 12), ("beta", 14), ("aF", 0), ("aB", 1))):
                    B.wait("dve", label)
                    if n in (0, 2, 3, 4):
                        B.did(pe.nop())
                    for t in range(TILES):
                        last = nc.tensor.transpose(wb[:, (n * TILES + t) * 8:(n * TILES + t + 1) * 8],
                                                   W[0:8, src, t * P:(t + 1) * P], con[0:8, 0:8])
                    B.did(last, f"columns{n}")
                B.end()

                with pe.Fori(0, H_A) as h:
                    B = s_gdn.body("pe", pe, l * H_A + h)
                    n0_ = pe.snap(l * STREAM_HALVES + h * 8 + STREAM["gates"])
                    used_and(B, project(pj[0], n0_), n0_ + 2, "q")
                    used_and(B, project(pj[1], n0_ + 2), n0_ + 2 + 2, "k")
                    B.wait("act", "q taken")
                    used_and(B, project(pj[0], n0_ + 4), n0_ + 4 + 2, "v")
                    B.wait("act", "q squared")
                    B.did(column_sums(wa, wt(16)), "q sum")
                    B.wait("act", "k squared")
                    B.did(column_sums(wb, wt(16)), "k sum")
                    B.wait("dve", "k normed")
                    B.did(transposed(wa, wt(1)), "k turned")
                    B.wait("dve", "v silu")
                    B.did(transposed(wb, wt(15)), "v turned")
                    for d in range(2):
                        B.wait("dve", f"kb{d}")
                        B.wait("act", "v turned taken")
                        B.did(each_tile(wa, wt(1), wt(14)), f"kk{d}")
                        B.did(each_tile(wb, wt(1), wt(0)), f"qk{d}")
                        for v in range(LEVELS):
                            B.wait("dve", f"level{d}{v}")
                            last = None
                            for t in range(TILES):
                                last = mm(T(wa, t), T(wt(12), t), ident if v == 0 else T(wt(10), t),
                                          start=True, stop=True)
                            B.did(last, f"ld{d}{v}")
                            if v:
                                B.wait("act", f"ld taken{d}{v}")
                                if v < LEVELS - 1:
                                    B.did(each_tile(wb, wt(11), wt(13)), f"dld{d}{v}")
                                B.did(each_tile(wa, wt(13), wt(11)), f"dldT{d}{v}")
                        B.wait("dve", f"inverse{d}")
                        B.wait("dve", f"kbg{d}")
                        B.did(each_tile(wa, wt(15), wt(11)), f"wT{d}")
                        B.wait("act", f"wT taken{d}")
                        B.wait("dve", f"kdec{d}")
                        order = [0, 1, 2, 3, 4] if d == 0 else [0, 4, 3, 2, 1]
                        for n, t in enumerate(order):
                            st = state[:, min(n, 1), 0:P]
                            last = mm(wa[:, 0:P], T(wt(11), t), T(wt(14), t), start=True, stop=(n == 0))
                            if n == 1:
                                pe.wait_ge(state_in[d], (l * H_A + h + 1) * 16)
                            if n:
                                if n > 1:
                                    B.wait("dve", f"state{d}{n - 1}")
                                last = mm(wa[:, 0:P], T(wt(12), t), st, start=False, stop=True)
                            B.did(last, f"vnew{d}{n}")
                            if n:
                                mm(wa[:, 512:512 + P], st, T(wt(13), t), start=True, stop=False)
                            B.wait("act", f"vnew taken{d}{n}")
                            last = mm(wa[:, 512:512 + P], T(wt(9), t), T(wt(16), t), start=(n == 0), stop=True)
                            B.did(last, f"o{d}{n}")
                            B.did(mm(wb[:, 0:P], T(wt(10), t), T(wt(9), t), start=True, stop=True), f"kv{d}{n}")
                            B.wait("dve", f"o taken{d}{n}")
                    used_and(B, project(pj[1], n0_ + 6), n0_ + 6 + 2, "z")
                    B.wait("act", "o squared")
                    B.did(column_sums(wa, wt(6)), "o sum")
                    B.end()

                with pe.Fori(0, H_C) as h:
                    B = s_mls.body("pe", pe, l * H_C + h)
                    n0_ = pe.snap(l * STREAM_HALVES + h * 10 + (STREAM["gates"] + STREAM["gdn"]))
                    for j, name in enumerate(("q", "k", "v", "o", "z")):
                        if j >= 2:
                            B.wait("act", ("q taken", "k taken", "v taken")[j - 2])
                        used_and(B, project(pj[j % 2], n0_ + 2 * j), n0_ + 2 * j + 2, name)
                        if j == 3:
                            B.did(transposed(wa, wt(1)), "k turned")
                            B.wait("act", "v taken")
                            B.did(transposed(wb, wt(2)), "v turned")
                    for d in range(2):
                        B.wait("dve", "v turned taken")
                        B.wait("act", "k turned taken")
                        if d:
                            B.wait("dve", "hB ready")
                        B.did(each_tile(wa, wt(1), wt(0)), f"qk{d}")
                        B.wait("dve", f"s{d}")
                        order = [0, 1, 2, 3, 4] if d == 0 else [0, 4, 3, 2, 1]
                        for n, t in enumerate(order):
                            if n:
                                if n == 1:
                                    B.wait("dve", f"n rep{d}")
                                else:
                                    B.wait("dve", f"state{d}{n - 1}")
                                mm(wa[:, 0:P], state[:, 1, 0:P], T(wt(10), t), start=True, stop=False)
                            mm(wa[:, 0:P], T(wt(4), t), T(wt(9), t), start=(n == 0), stop=True)
                            if n:
                                mm(wa[:, 512:512 + P], state[:, 1, P:2 * P], T(wt(10), t), start=True, stop=False)
                            B.did(mm(wa[:, 512:512 + P], ones, T(wt(9), t), start=(n == 0), stop=True), f"numden{d}{n}")
                            mm(wb[:, 0:P], T(wt(11), t), T(wt(4), t), start=True, stop=True)
                            B.did(mm(wb[:, P:2 * P], T(wt(11), t), ones, start=True, stop=True), f"kv{d}{n}")
                            B.wait("dve", f"h taken{d}{n}")
                    B.wait("act", "h squared")
                    B.did(column_sums(wa, wt(6)), "h sum")
                    B.end()

                B = s_min.body("pe", pe, l)
                n0_ = pe.snap(l * STREAM_HALVES + (STREAM["gates"] + STREAM["gdn"] + STREAM["mlstm"]))
                for j in range(15):
                    if j >= 2:
                        B.wait("act", f"taken{j - 2}")
                    used_and(B, project(pj[j % 2], n0_ + 2 * j), n0_ + 2 * j + 2, f"tile{j}")
                for k in range(Q_TILES):
                    B.wait("act", f"cq squared{k}")
                    B.did(column_sums(wa, wt(10 + k), k == 0, k == Q_TILES - 1), f"cq sum{k}")
                for k in range(KV_TILES):
                    B.wait("act", f"ckv squared{k}")
                    B.did(column_sums(wb, wt(14 + k), k == 0, k == KV_TILES - 1), f"ckv sum{k}")
                B.wait("dve", "roped")
                B.wait("act", "cq logged")
                mm(wa[:, 0:512], con[:, C_FOLD:C_FOLD + P], W[:, 7, 0:512], start=True, stop=True)
                B.did(mm(wa[:, 512:TOK], con[:, C_FOLD:C_FOLD + P], W[:, 7, 512:TOK], start=True, stop=True), "key pe")
                B.end()

                with pe.Fori(0, H_B) as h:
                    B = s_mla.body("pe", pe, l * H_B + h)
                    n0_ = pe.snap(l * STREAM_HALVES + h * 2
                                  + (STREAM["gates"] + STREAM["gdn"] + STREAM["mlstm"] + STREAM["mla_in"]))
                    cqn = [(h_hi[:, k, :], h_lo[:, k, :]) for k in range(Q_TILES)]
                    kvh = h_hi[:, 4:7, :].rearrange("p a n -> p (a n)")
                    kvl = h_lo[:, 4:7, :].rearrange("p a n -> p (a n)")

                    def three(out, hi, lo, xh, xl, first, last):
                        mm(out, hi, xh, start=first, stop=False)
                        mm(out, hi, xl, start=False, stop=False)
                        return mm(out, lo, xh, start=False, stop=last)

                    parts_ready(n0_)
                    for which in range(2):
                        for k in range(Q_TILES):
                            for a in range(2):
                                hs = slice(a * HALF, (a + 1) * HALF)
                                last = three(pj[which][:, a, 0:HALF], w_hi[:, 0, 2 * k + which, :],
                                             w_lo[:, 0, 2 * k + which, :], cqn[k][0][:, hs], cqn[k][1][:, hs],
                                             k == 0, k == Q_TILES - 1)
                        if which == 0:
                            B.did(last, "q nope")
                    used_and(B, last, n0_ + 1, "q pe")
                    parts_ready(n0_ + 1)
                    B.wait("act", "q nope taken")
                    for k in range(KV_TILES):
                        for a in range(2):
                            at = k * KEYS + a * (KEYS // 2)
                            last = three(pj[0][:, a, 0:KEYS // 2], w_hi[:, 1, 2 * k, :], w_lo[:, 1, 2 * k, :],
                                         kvh[:, at:at + KEYS // 2], kvl[:, at:at + KEYS // 2],
                                         k == 0, k == KV_TILES - 1)
                    B.did(last, "k nope")
                    B.wait("dve", "q pe roped")
                    for t in range(KEYS // P):
                        o = pj[1][:, t // 3, (t % 3) * P:(t % 3 + 1) * P]
                        for k in range(KV_TILES):
                            at = k * KEYS + t * P
                            last = three(o, kvh[:, at:at + P], kvl[:, at:at + P], w_hi[:, 1, 2 * k + 1, :],
                                         w_lo[:, 1, 2 * k + 1, :], k == 0, k == KV_TILES - 1)
                    used_and(B, last, n0_ + 2, "v")
                    qn, qp, kn, kp, vt = wt(0), wt(1), flat(2, KEYS), flat(8, KEYS), flat(4, KEYS)
                    B.wait("act", "v taken")
                    for t in range(TILES):
                        spans = [(0, CTX, 0)] if t == 0 else [(CTX, TOK, 0), (TOK, KEYS, 512)]
                        for a, b, o in spans:
                            mm(wa[:, o:o + b - a], T(qn, t), kn[:, a:b], start=True, stop=False)
                            last = mm(wa[:, o:o + b - a], T(qp, t), kp[:, a:b], start=False, stop=True)
                        B.did(last, f"scores{t}")
                        B.wait("dve", f"normed{t}")
                        nk = 1 if t == 0 else TILES
                        for j in range(nk):
                            last = nc.tensor.transpose(T(wb, j), T(wt(6), j), ident)
                        B.did(last, f"turned{t}")
                        B.wait("act", f"turned taken{t}")
                        k0 = 0 if t == 0 else 1
                        for j in range(nk):
                            last = mm(wa[:, 0:P], T(vt, k0 + j), T(wt(7), j), start=(j == 0), stop=(j == nk - 1))
                        B.did(last, f"o{t}")
                        B.wait("dve", f"o taken{t}")
                    B.end()

                B = s_spl.body("pe", pe, l)
                B.did(pe.nop())
                B.end()
                with pe.Fori(0, KT // 2) as f:
                    B = s_out.body("pe", pe, l * (KT // 2) + f)
                    n0_ = pe.snap(l * STREAM_HALVES + f * 4 + (STREAM_HALVES - STREAM["out"]))
                    used_and(B, project(pj[0], n0_), n0_ + 2, "first")
                    used_and(B, project(pj[1], n0_ + 2), n0_ + 2 + 2, "second")
                    B.end()
                B = s_res.body("pe", pe, l)
                for k in range(KT):
                    B.wait("act", f"square{k}")
                    B.did(column_sums(wa, wt(k % 4), k == 0, k == KT - 1), f"sum{k}")
                B.end()

        @block.scalar
        def _(act):
            A = nc.scalar.activation
            act.preload_act_table_set("natural_log_exp_and_others")
            def rsqrt(B, out, src, tmp, scale, label, post=1.0, mid=None):
                B.link(A(tmp, src, ACT.Ln, bias=cst[:, 0:1], scale=scale), mid)
                B.link(A(out, tmp, ACT.Exp, scale=-0.5, bias=(cst[:, 1:2] if post != 1.0 else 0.0)), label)

            act.wait_ge(const_in, 48)
            B = s_init.body("act", act, None)
            B.wait("dve", "eps")
            B.link(A(cond[:, :, :], cond_t[:, :, :], ACT.Exp, scale=-1.0), "cond exp")
            B.end()
            with act.Fori(0, DEPTH) as l:
                act.dma_start(prm[:, :], io["params"][l, :, :]).then_inc(params_in, 16)
                act.dma_start(m0[:, :], io["m0"][l, :, :]).then_inc(m0_in, 16)
                act.wait_ge(x_in, 16)
                act.dma_start(x_kept, xo[:, :, :]).then_inc(x_saved, 16)

                B = s_norm.body("act", act, l)
                for k in range(KT):
                    if k >= 4:
                        B.wait("pe", f"sum{k - 4}")
                    B.did(A(wt(k % 4), xo[:, k, :], ACT.Square), f"square{k}")
                B.wait("pe", f"sum{KT - 1}")
                rsqrt(B, wt(5), wa[:, 0:TOK], wt(4), 1.0 / D_MODEL, "rstd")
                B.end()

                B = s_gate.body("act", act, l)
                g = PRM["gates"]
                act.wait_ge(params_in, (l + 1) * 16)
                xx = W[0:8, 0:2, :]
                B.link(A(colt[0:8, 0, 0:1], prm[0:8, g:g + 1], ACT.Exp), "exp a_log")
                B.wait("pe", "gates")

                def gate(at):
                    return pj[0][at:at + 8, :, 0:HALF]
                B.did(A(halves(W[0:8, 0, :]), gate(0), ACT.Identity, bias=prm[0:8, g + 1:g + 2]))
                B.did(A(halves(W[0:8, 1, :]), gate(96), ACT.Identity, bias=prm[0:8, g + 3:g + 4]))
                B.did(A(halves(W[0:8, 15, :]), gate(64), ACT.Identity, bias=prm[0:8, g + 2:g + 3]), "i")
                B.link(A(halves(W[0:8, 14, :]), gate(32), ACT.Exp, scale=-1.0), "beta exp")
                B.link(A(W[0:8, 1, :], W[0:8, 1, :], ACT.Copy, scale=-1.0), "x")
                B.link(A(W[0:8, 2:4, :], xx, ACT.Abs))
                B.link(A(W[0:8, 2:4, :], W[0:8, 2:4, :], ACT.Exp, scale=-1.0))
                B.link(A(W[0:8, 2:4, :], W[0:8, 2:4, :], ACT.Ln, bias=1.0), "log")
                B.wait("dve", "wi")
                B.link(A(W[0:8, 6:8, :], W[0:8, 6:8, :], ACT.Exp), "wi exp")
                B.wait("dve", "em")
                B.link(A(W[0:8, 8:10, :], W[0:8, 8:10, :], ACT.Exp, scale=-1.0), "em exp")
                for d in range(2):
                    hs = slice(4 * d, 4 * d + 4)
                    act.dma_start(rows[0, hs, :], W[hs, 10 + 2 * d, :]).then_inc(rows_out, 16)
                    act.dma_start(rows[1, hs, :], W[hs, 14, :]).then_inc(rows_out, 16)
                    act.dma_start(rows[2, hs, :], W[hs, 2 + d, :]).then_inc(rows_out, 16)
                    act.dma_start(rows[3, hs, :], W[hs, 6 + d, :]).then_inc(rows_out, 16)
                    act.dma_start(rows[4, hs, :], W[hs, 8 + d, :]).then_inc(rows_out, 16)
                    act.dma_start(io["new_m"][l, d, :, :], mout[hs, d:d + 1]).then_inc(rows_out, 16)
                B.wait("pe", "columns4")
                B.link(A(tokc[:, :, :, :].rearrange("p k t h -> p (k t h)"), wb[:, 0:5 * TILES * 8], ACT.Copy))
                act.wait_ge(rows_out, (l + 1) * (12 * 16))
                B.did(act.nop())
                B.end()

                with act.Fori(0, H_A) as h:
                    B = s_gdn.body("act", act, l * H_A + h)
                    now = act.snap((l * H_A + h + 1) * 16)
                    act.dma_start(state[:, 1, 0:P], io["state_gdn"][l, 0, h, :, :]).then_inc(state_in[0], 16)
                    for j, kind in ((5, 0), (6, 1)):
                        act.dma_start(wt(j), rows[kind, bass.ds(h, 1), :].partition_broadcast(P)).then_inc(rows_in[0], 16)

                    def padded(src, i):
                        B.did(A(flat(9, PADW)[:, 2:2 + CTX], src[:, 0, 0:CTX], ACT.Copy))
                        B.did(A(flat(9, PADW)[:, 6 + CTX:6 + HALF], src[:, 0, CTX:HALF], ACT.Copy))
                        B.did(A(flat(9, PADW)[:, 6 + HALF:6 + TOK], src[:, 1, 0:HALF], ACT.Copy), f"{'qkv'[i]} taken")
                    B.wait("dve", "zeros")
                    for i, x in enumerate("qkv"):
                        B.wait("pe", x)
                        if i:
                            B.wait("dve", f"{'qkv'[i - 1]} conv")
                        padded(pj[i % 2], i)
                        B.wait("dve", f"{x} conv")
                        B.did(A(flat(13, CONVW), flat(11, CONVW), ACT.Exp, scale=-1.0), f"{x} exp")
                        if i < 2:
                            B.wait("dve", f"{x} silu")
                            B.did(A(wt(16), wt(15), ACT.Square), f"{x} squared")
                            B.wait("pe", f"{x} sum")
                            rsqrt(B, wt(16), (wa if i == 0 else wb)[:, 0:TOK], wt(16), 1.0, f"{x} rstd",
                                  DK_SCALE if i == 0 else 1.0)
                    B.wait("pe", "k turned")
                    B.did(A(wt(2), wa[:, 0:TOK], ACT.Copy))
                    B.wait("pe", "v turned")
                    B.did(A(wt(3), wb[:, 0:TOK], ACT.Copy), "v turned taken")
                    for d in range(2):
                        act.wait_ge(rows_in[d], (l * H_A + h + 1) * 32)
                        B.wait("dve", f"cols{d}")
                        B.did(A(wt(8), wt(5), ACT.Exp), f"eg{d}")
                        B.did(A(colt[:, 2, :], colt[:, 0, :], ACT.Exp), f"eg col{d}")
                        B.did(A(colt[:, 5, :], colt[:, 4, :], ACT.Exp), f"kdec col{d}")
                        B.wait("dve", f"gap{d}")
                        B.did(A(wt(7), wt(7), ACT.Exp), f"decay{d}")
                        for v in range(1, LEVELS):
                            B.wait("pe", f"ld{d}{v}")
                            B.did(A(wt(13), wa[:, 0:TOK], ACT.Copy), f"ld taken{d}{v}")
                        B.wait("pe", f"wT{d}")
                        B.did(A(wt(12), wa[:, 0:TOK], ACT.Copy, scale=-1.0), f"wT taken{d}")
                        if d == 0:
                            B.wait("dve", "rows free")
                            for j, kind in ((5, 0), (6, 1)):
                                act.dma_start(wt(j), rows[kind, bass.ds(h + 4, 1), :].partition_broadcast(P))\
                                    .then_inc(rows_in[1], 16)
                        for n in range(TILES):
                            t = n if d == 0 or n == 0 else TILES - n
                            B.wait("pe", f"vnew{d}{n}")
                            B.did(A(T(wt(9), t), wa[:, 0:P], ACT.Copy), f"vnew taken{d}{n}")
                            if n == 0:
                                B.wait("dve", f"state{d}0")
                                act.dma_start(io["new_gdn"][l, d, h, :, :], state[:, 0, 0:P]).then_inc(state_out[d], 16)
                        if d == 0:
                            B.wait("dve", f"state0{TILES - 1}")
                            act.dma_start(state[:, 1, 0:P], io["state_gdn"][l, 1, h, :, :]).then_inc(state_in[1], 16)
                    B.wait("dve", "o whole")
                    B.did(A(wt(6), wt(4), ACT.Square), "o squared")
                    B.wait("pe", "z")
                    B.did(A(halves(wt(8)), pj[1][:, :, 0:HALF], ACT.Copy))
                    B.did(A(halves(wt(9)), pj[1][:, :, 0:HALF], ACT.Exp, scale=-1.0), "z exp")
                    B.wait("pe", "o sum")
                    rsqrt(B, wt(7), wa[:, 0:TOK], wt(7), 1.0 / P, "o rstd")
                    for d in range(2):
                        act.wait_ge(state_out[d], now)
                    B.did(act.nop())
                    B.end()

                with act.Fori(0, H_C) as h:
                    B = s_mls.body("act", act, l * H_C + h)
                    now = act.snap((l * H_C + h + 1) * 16)
                    for d in range(1):
                        act.dma_start(state[:, 1, 0:P], io["state_c"][l, d, h, :, :]).then_inc(cstate_in[d], 16)
                        act.dma_start(n0[:, :], io["state_n"][l, d, h, :, :]).then_inc(cstate_in[d], 16)
                        for j in range(3):
                            act.dma_start(wt(5 + j), rows[2 + j, bass.ds(h + 4 * d, 1), :].partition_broadcast(P))\
                                .then_inc(crows_in[d], 16)
                    B.wait("pe", "q")
                    B.did(A(halves(wt(0)), pj[0][:, :, 0:HALF], ACT.Copy, scale=DK_SCALE), "q taken")
                    B.wait("pe", "k")
                    B.did(A(halves(wt(1)), pj[1][:, :, 0:HALF], ACT.Copy), "k taken")
                    B.wait("pe", "v")
                    B.did(A(halves(wt(2)), pj[0][:, :, 0:HALF], ACT.Copy), "v taken")
                    B.wait("pe", "k turned")
                    B.did(A(wt(3), wa[:, 0:TOK], ACT.Copy), "k turned taken")
                    B.wait("pe", "o")
                    B.did(A(halves(wt(13)), pj[1][:, :, 0:HALF], ACT.Exp, scale=-1.0), "o exp")
                    B.wait("pe", "z")
                    B.did(A(halves(wt(14)), pj[0][:, :, 0:HALF], ACT.Copy))
                    B.did(A(halves(wt(15)), pj[0][:, :, 0:HALF], ACT.Exp, scale=-1.0), "z exp")
                    for d in range(2):
                        B.wait("dve", f"gap{d}")
                        B.did(A(wt(8), wt(8), ACT.Exp), f"decay{d}")
                        B.did(A(colt[:, 5, :], colt[:, 4, :], ACT.Exp), f"wk col{d}")
                        B.wait("dve", f"state{d}0")
                        act.dma_start(io["new_c"][l, d, h, :, :], state[:, 0, 0:P]).then_inc(cstate_out[d], 16)
                        act.dma_start(io["new_n"][l, d, h, :, :], state[:, 0, P:P + 1]).then_inc(cstate_out[d], 16)
                        if d == 0:
                            B.wait("dve", "hB ready")
                            act.dma_start(state[:, 1, 0:P], io["state_c"][l, 1, h, :, :]).then_inc(cstate_in[1], 16)
                            act.dma_start(n0[:, :], io["state_n"][l, 1, h, :, :]).then_inc(cstate_in[1], 16)
                            for j in range(3):
                                act.dma_start(wt(5 + j), rows[2 + j, bass.ds(h + 4, 1), :].partition_broadcast(P))\
                                    .then_inc(crows_in[1], 16)
                    B.wait("dve", "h whole")
                    B.did(A(wt(6), wt(12), ACT.Square), "h squared")
                    B.wait("pe", "h sum")
                    rsqrt(B, wt(7), wa[:, 0:TOK], wt(7), 1.0 / P, "h rstd")
                    for d in range(2):
                        act.wait_ge(cstate_out[d], (l * H_C + h + 1) * 32)
                    B.did(act.nop())
                    B.end()

                B = s_min.body("act", act, l)
                act.dma_start(flat(15, 2 * P), io["cache_ckv"][l, :, :]).then_inc(cache_in, 16)
                kp = flat(8, KEYS)
                for a in range(2):
                    act.dma_start(kp[64 * a:64 * a + 64, TOK:KEYS], io["cache_kr"][l, :, :]).then_inc(cache_in, 16)
                for j in range(15):
                    B.wait("pe", f"tile{j}")
                    if j < 7:
                        B.did(A(halves(wt(j)), pj[j % 2][:, :, 0:HALF], ACT.Copy), f"taken{j}")
                    else:
                        if j >= 9:
                            B.wait("dve", f"zb{j - 2}")
                        B.did(A(halves(wt(10 + 2 * (j % 2))), pj[j % 2][:, :, 0:HALF], ACT.Exp, scale=-1.0))
                        B.did(A(halves(wt(11 + 2 * (j % 2))), pj[j % 2][:, :, 0:HALF], ACT.Copy), f"taken{j}")
                act.dma_start(io["new_kr"][l, :, :], W[0:64, 6, 0:CTX]).then_inc(latent_out, 16)
                act.wait_ge(cache_in, (l + 1) * 48)
                B.wait("dve", "zb14")
                B.wait("dve", "cache split")
                for k in range(Q_TILES):
                    B.did(A(wt(10 + k), wt(k), ACT.Square), f"cq squared{k}")
                for k in range(KV_TILES):
                    B.did(A(wt(14 + k), wt(4 + k), ACT.Square), f"ckv squared{k}")
                B.wait("pe", f"cq sum{Q_TILES - 1}")
                rsqrt(B, wt(10), wa[:, 0:TOK], wt(10), 1.0 / (Q_TILES * P), "cq rstd", mid="cq logged")
                B.wait("pe", f"ckv sum{KV_TILES - 1}")
                rsqrt(B, wt(11), wb[:, 0:TOK], wt(11), 1.0 / (KV_TILES * P), "ckv rstd")
                B.wait("pe", "key pe")
                B.did(A(kp[:, 0:TOK], wa[:, 0:TOK], ACT.Copy), "key pe taken")
                B.wait("dve", "ckv normed")
                act.dma_start(io["new_ckv"][l, :, :, :], W[:, 4:6, 0:CTX]).then_inc(latent_out, 16)
                act.wait_ge(latent_out, (l + 1) * 32)
                B.did(act.nop())
                B.end()

                with act.Fori(0, H_B) as h:
                    B = s_mla.body("act", act, l * H_B + h)
                    B.wait("pe", "q nope")
                    B.did(A(halves(wt(0)), pj[0][:, :, 0:HALF], ACT.Copy), "q nope taken")
                    B.wait("pe", "k nope")
                    B.did(A(halves(flat(2, KEYS)), pj[0][:, :, 0:KEYS // 2], ACT.Copy), "k nope taken")
                    B.wait("pe", "v")
                    B.did(A(halves(flat(4, KEYS)), pj[1][:, :, 0:KEYS // 2], ACT.Copy), "v taken")
                    for t in range(TILES):
                        nk = P if t == 0 else TOK
                        B.wait("dve", f"max{t}")
                        B.did(A(W[:, 6, 0:nk], wa[:, 0:nk], ACT.Exp, bias=mxs[:, 1, t:t + 1], scale=SM_SCALE,
                                accum_out=mxs[:, 2, t:t + 1]), f"exp{t}")
                        B.wait("pe", f"turned{t}")
                        B.did(A(W[:, 7, 0:nk], wb[:, 0:nk], ACT.Copy), f"turned taken{t}")
                    B.end()

                act.wait_ge(s_out.sems["dve"], (l + 1) * (KT // 2 * s_out.total["dve"]))
                B = s_res.body("act", act, l)
                for k in range(KT):
                    if k >= 4:
                        B.wait("pe", f"sum{k - 4}")
                    B.did(A(wt(k % 4), xo[:, k, :], ACT.Square), f"square{k}")
                B.wait("pe", f"sum{KT - 1}")
                rsqrt(B, wt(5), wa[:, 0:TOK], wt(4), 1.0 / D_MODEL, "rstd")
                act.wait_ge(x_saved, (l + 1) * 16)
                for k in range(KT):
                    if k >= 2:
                        B.wait("dve", f"added{k - 2}")
                    act.dma_start(wt(6 + k % 2), x_kept[:, k, :]).then_inc(x_back[k % 2], 16)
                B.end()
            act.dma_start(io["y"], xo[:, :, :]).then_inc(y_out, 16)
            act.wait_ge(y_out, 16)

        @block.vector
        def _(dve):
            V = nc.vector
            tt, ts, stt = V.tensor_tensor, V.tensor_scalar, V.scalar_tensor_tensor

            def sigmoid_from_exp(B, ap, label=None):
                B.link(ts(ap, ap, 1.0, None, ALU.add))
                B.link(V.reciprocal(ap, ap), label)

            B = s_init.body("dve", dve, None)
            B.did(V.memset(cst[:, 0:1], EPS))
            B.did(V.memset(cst[:, 1:2], math.log(DK_SCALE)), "eps")
            dve.wait_ge(const_in, 48)
            B.wait("act", "cond exp")
            sigmoid_from_exp(B, cond[:, :, :])
            B.link(tt(cond[:, :, :], cond[:, :, :], cond_t[:, :, :], ALU.mult))
            B.end()
            with dve.Fori(0, DEPTH) as l:
                dve.wait_ge(params_in, (l + 1) * 16)
                dve.sem_inc(s_init.passed, 1)
                with dve.Fori(0, ADA_HALVES // RAW_SLOTS) as i:
                    B = s_ada.body("dve", dve, l * (ADA_HALVES // RAW_SLOTS) + i)
                    B.wait("pe", "two tiles")
                    b = PRM["b_ada"]
                    B.did(tt(mod[:, bass.ds(2 * i, 2), :], wa[:, 0:4].rearrange("p (a b) -> p a b", b=2),
                             prm[:, bass.ds(2 * i + b, 2)].unsqueeze(2).to_broadcast([P, 2, 2]), ALU.add))
                    B.end()

                B = s_norm.body("dve", dve, l)

                def par(name, n):
                    return prm[:, PRM[name]:PRM[name] + n]
                B.link(stt(mul[:, :, :], mod[:, KT:2 * KT, :], 1.0,
                           par("g_pre", KT).unsqueeze(2).to_broadcast([P, KT, 2]), ALU.add, ALU.mult))
                B.wait("act", "rstd")
                for k in range(KT):
                    u = wt(6 + k % 4)
                    B.link(tt(u, xo[:, k, :], wt(5), ALU.mult))
                    B.did(ts(u[:, 0:CTX], u[:, 0:CTX], mul[:, k, 0:1], mod[:, k, 0:1], ALU.mult, ALU.add))
                    B.link(ts(u[:, CTX:TOK], u[:, CTX:TOK], mul[:, k, 1:2], mod[:, k, 1:2], ALU.mult, ALU.add))
                    B.link(V.tensor_copy(h_hi[:, k, :], u))
                    B.did(tt(h_lo[:, k, :], u, h_hi[:, k, :].bitcast(F32), ALU.subtract))
                dve.wait_ge(x_saved, (l + 1) * 16)
                B.did(V.memset(cst[:, 2:3], 0.0))
                B.end()

                B = s_gate.body("dve", dve, l)
                resF, resB = W[0:8, 6:8, :], W[0:8, 8:10, :]
                B.did(V.memset(resF, 1.0))
                B.link(V.memset(resB, 1.0))
                B.did(V.memset(resF.rearrange("p a (t c) -> p (a t) c", c=P)[:, :, 0:1], 0.0))
                B.link(V.memset(resB.rearrange("p a (t c) -> p (a t) c", c=P)[:, :, P - 1:P], 0.0))
                B.wait("act", "exp a_log")
                B.link(ts(colt[0:8, 1, 0:1], colt[0:8, 0, 0:1], -1.0, None, ALU.mult))
                B.wait("act", "beta exp")
                sigmoid_from_exp(B, W[0:8, 14, :], "beta")
                B.wait("act", "log")
                B.link(stt(W[0:8, 4:6, :], W[0:8, 0:2, :], 0.0, W[0:8, 2:4, :], ALU.max, ALU.add))
                B.did(ts(W[0:8, 4, :], W[0:8, 4, :], colt[0:8, 1, 0:1], None, ALU.mult))
                B.link(ts(W[0:8, 5, :], W[0:8, 5, :], -1.0, None, ALU.mult))

                def fl(a):
                    return W[0:8, a:a + 2, :].rearrange("p a n -> p (a n)")
                B.did(V.tensor_tensor_scan(fl(10), fl(6), fl(4), 0.0, ALU.mult, ALU.add))
                B.link(V.tensor_tensor_scan(fl(12)[:, ::-1], fl(8)[:, ::-1], fl(4)[:, ::-1], 0.0,
                                            ALU.mult, ALU.add), "cum")
                B.did(tt(W[0:8, 0, :], W[0:8, 15, :], W[0:8, 11, :], ALU.subtract), "aF")
                B.did(tt(W[0:8, 1, :], W[0:8, 15, :], W[0:8, 13, :], ALU.subtract), "aB")
                B.link(V.memset(W[0:8, 4:6, :], 0.0))
                d0F, d0B = W[0:8, 4, :], W[0:8, 5, :]
                B.did(V.tensor_copy(tiled(d0F)[:, 2:5, 0:1], tiled(W[0:8, 11, :])[:, 1:4, P - 1:P]))
                B.link(V.tensor_copy(tiled(d0B)[:, 1:4, P - 1:P], tiled(W[0:8, 13, :])[:, 2:5, 0:1]))
                dve.wait_ge(m0_in, (l + 1) * 16)
                MF, MB = W[0:8, 2, :], W[0:8, 3, :]
                scan = V.tensor_tensor_scan
                B.did(scan(MF[:, 0:CTX], d0F[:, 0:CTX], W[0:8, 0, 0:CTX], 0.0, ALU.add, ALU.max))
                B.did(scan(MF[:, CTX:TOK], d0F[:, CTX:TOK], W[0:8, 0, CTX:TOK], m0[:, 0:1], ALU.add, ALU.max))
                B.did(scan(MB[:, 0:CTX][:, ::-1], d0B[:, 0:CTX][:, ::-1], W[0:8, 1, 0:CTX][:, ::-1], 0.0,
                           ALU.add, ALU.max))
                B.link(scan(MB[:, CTX:TOK][:, ::-1], d0B[:, CTX:TOK][:, ::-1], W[0:8, 1, CTX:TOK][:, ::-1],
                            m0[:, 0:1], ALU.add, ALU.max))
                B.did(V.memset(mprev[:, :, 0:1], 0.0))
                B.did(V.tensor_copy(mprev[:, 0, 1:2], m0[:, :]))
                B.did(V.tensor_copy(mprev[:, 1, 4:5], m0[:, :]))
                B.did(tt(mprev[:, 0, 2:5].unsqueeze(2), tiled(MF)[:, 1:4, P - 1:P],
                         tiled(W[0:8, 11, :])[:, 1:4, P - 1:P], ALU.add))
                B.did(tt(mprev[:, 1, 1:4].unsqueeze(2), tiled(MB)[:, 2:5, 0:1],
                         tiled(W[0:8, 13, :])[:, 2:5, 0:1], ALU.add))
                B.did(tt(mout[:, 0:1], MF[:, P - 1:P], W[0:8, 11, P - 1:P], ALU.add))
                B.link(tt(mout[:, 1:2], MB[:, 0:1], W[0:8, 13, 0:1], ALU.add))
                for d, M in ((0, MF), (1, MB)):
                    B.did(tt(tiled(W[0:8, 6 + d, :]), mprev[:, d, :].unsqueeze(2).to_broadcast([8, TILES, P]),
                             tiled(M), ALU.subtract), "wi")
                for d, M in ((0, MF), (1, MB)):
                    B.did(tt(W[0:8, 8 + d, :], M, W[0:8, 11 + 2 * d, :], ALU.add), "em")
                B.end()

                with dve.Fori(0, H_A) as h:
                    B = s_gdn.body("dve", dve, l * H_A + h)
                    pad, cv, sg = flat(9, PADW), flat(11, CONVW), flat(13, CONVW)
                    B.did(V.memset(pad[:, 0:2], 0.0))
                    B.did(V.memset(pad[:, 2 + CTX:6 + CTX], 0.0))
                    B.did(V.memset(pad[:, 6 + TOK:8 + TOK], 0.0), "zeros")
                    cw = PRM["conv"]
                    for i in range(3):
                        ins = ts(hcw[:, i, :], prm[:, bass.ds(h * CONV_K + (cw + i * H_A * CONV_K), CONV_K)],
                                 1.0, None, ALU.mult)
                        B.link(ins)
                    for i, x in enumerate("qkv"):
                        B.wait("act", f"{x} taken")
                        B.link(ts(cv, pad[:, 0:CONVW], hcw[:, i, 0:1], None, ALU.mult))
                        for j in range(1, CONV_K):
                            B.link(stt(cv, pad[:, j:j + CONVW], hcw[:, i, j:j + 1], cv, ALU.mult, ALU.add),
                                   f"{x} conv" if j == CONV_K - 1 else None)
                        B.wait("act", f"{x} exp")
                        sigmoid_from_exp(B, sg)
                        y = wt(15)
                        B.did(tt(y[:, 0:CTX], cv[:, 0:CTX], sg[:, 0:CTX], ALU.mult))
                        B.link(tt(y[:, CTX:TOK], cv[:, CTX + 4:CONVW], sg[:, CTX + 4:CONVW], ALU.mult), f"{x} silu")
                        if i < 2:
                            B.wait("act", f"{x} rstd")
                            B.link(tt(wt(i), y, wt(16), ALU.mult), f"{x} normed")
                    B.wait("act", "v turned taken")
                    for d in range(2):
                        dve.wait_ge(rows_in[d], (l * H_A + h + 1) * 32)
                        last_at = P - 1 if d == 0 else 0
                        B.did(ts(colt[:, 0, :], tokc[:, d, :, bass.ds(h + 4 * d, 1)].rearrange("p t o -> p (t o)"), 1.0, None, ALU.mult))
                        B.link(ts(colt[:, 1, :], tokc[:, 2, :, bass.ds(h + 4 * d, 1)].rearrange("p t o -> p (t o)"), 1.0, None, ALU.mult))
                        B.link(tt(colt[:, 4, :].unsqueeze(2), tiled(wt(5))[:, :, last_at:last_at + 1],
                                  colt[:, 0, :].unsqueeze(2), ALU.subtract), f"cols{d}")
                        B.did(tt(wt(14), wt(1), wt(6), ALU.mult), f"kb{d}")
                        B.link(tt(tiled(wt(7)), tiled(wt(5)), over_cols(colt[:, 0, :]), ALU.subtract))
                        B.link(tt(tiled(wt(7)), tiled(wt(7)), over_tiles(neg(d)), ALU.add), f"gap{d}")
                        B.wait("act", f"decay{d}")
                        B.wait("pe", f"kk{d}")
                        B.link(tt(wt(9), wa[:, 0:TOK], wt(7), ALU.mult))
                        B.wait("pe", f"qk{d}")
                        B.link(tt(wt(16), wb[:, 0:TOK], wt(7), ALU.mult))
                        D, DT, L = wt(10), wt(11), wt(12)
                        for v in range(LEVELS):
                            if v > 0:
                                B.wait("pe", f"ld{d}{v - 1}")
                            B.link(tt(tiled(L), tiled(wt(9)), over_tiles(lvl[:, d, v, :]), ALU.mult), f"level{d}{v}")
                            if v == 0:
                                B.link(tt(tiled(DT), over_tiles(ident), tiled(L), ALU.subtract))
                                B.wait("pe", f"ld{d}0")
                                B.link(tt(tiled(D), over_tiles(ident), tiled(wa[:, 0:TOK]), ALU.subtract))
                            else:
                                if v < LEVELS - 1:
                                    B.wait("pe", f"dld{d}{v}")
                                    B.did(tt(D, D, wb[:, 0:TOK], ALU.subtract))
                                B.wait("pe", f"dldT{d}{v}")
                                B.link(tt(DT, DT, wa[:, 0:TOK], ALU.subtract),
                                       f"inverse{d}" if v == LEVELS - 1 else None)
                        B.wait("act", f"kdec col{d}")
                        B.link(tt(colt[:, 3, :], colt[:, 1, :], colt[:, 2, :], ALU.mult))
                        B.did(tt(tiled(wt(14)), tiled(wt(3)), over_cols(colt[:, 1, :]), ALU.mult))
                        B.did(tt(tiled(wt(15)), tiled(wt(2)), over_cols(colt[:, 3, :]), ALU.mult), f"kbg{d}")
                        B.wait("act", f"wT taken{d}")
                        B.did(tt(wt(13), wt(0), wt(8), ALU.mult))
                        B.did(tt(tiled(wt(10)), tiled(wt(2)), over_cols(colt[:, 5, :]), ALU.mult), f"kdec{d}")
                        if d == 0:
                            B.did(V.memset(cst[:, 2:3], 0.0), "rows free")
                        for n in range(TILES):
                            t = n if d == 0 or n == 0 else TILES - n
                            B.wait("pe", f"kv{d}{n}")
                            if n == 0:
                                B.link(V.tensor_copy(state[:, 0, 0:P], wb[:, 0:P]), f"state{d}0")
                            else:
                                e = t * P + last_at
                                B.link(stt(state[:, 1, 0:P], state[:, 1, 0:P], W[:, 8, e:e + 1], wb[:, 0:P],
                                           ALU.mult, ALU.add), f"state{d}{n}")
                            if d == 0:
                                B.link(V.tensor_copy(T(wt(4), t), wa[:, 512:512 + P]), f"o taken{d}{n}")
                            else:
                                B.link(tt(T(wt(4), t), T(wt(4), t), wa[:, 512:512 + P], ALU.add), f"o taken{d}{n}")
                        if d == 0:
                            dve.wait_ge(state_out[0], (l * H_A + h + 1) * 16)
                    B.did(V.memset(cst[:, 2:3], 0.0), "o whole")
                    B.wait("act", "z exp")
                    sigmoid_from_exp(B, wt(9))
                    B.link(tt(wt(8), wt(8), wt(9), ALU.mult))
                    B.wait("act", "o rstd")
                    B.link(stt(wt(4), wt(4), par("gdn_norm", 1), wt(7), ALU.mult, ALU.mult))
                    B.did(tt(xo[:, bass.ds(h, 1), :].rearrange("p a n -> p (a n)"), wt(4), wt(8), ALU.mult))
                    B.end()

                with dve.Fori(0, H_C) as h:
                    B = s_mls.body("dve", dve, l * H_C + h)
                    B.wait("pe", "v turned")
                    B.did(V.tensor_copy(wt(4), wb[:, 0:TOK]), "v turned taken")
                    for d in range(2):
                        last_at = P - 1 if d == 0 else 0
                        dve.wait_ge(crows_in[d], (l * H_C + h + 1) * 48)
                        dve.wait_ge(cstate_in[d], (l * H_C + h + 1) * 32)
                        B.did(ts(state[:, 1, P:2 * P], ones, n0[:, 0:1], None, ALU.mult), f"n rep{d}")
                        B.link(ts(colt[:, 0, :], tokc[:, 3 + d, :, bass.ds(h + 4 * d, 1)].rearrange("p t o -> p (t o)"), 1.0, None, ALU.mult))
                        B.did(tt(colt[:, 4, :].unsqueeze(2), colt[:, 0, :].unsqueeze(2),
                                 tiled(wt(5))[:, :, last_at:last_at + 1], ALU.subtract))
                        B.link(tt(tiled(wt(8)), over_cols(colt[:, 0, :]), tiled(wt(5)), ALU.subtract))
                        B.link(tt(tiled(wt(8)), tiled(wt(8)), over_tiles(neg(d)), ALU.add), f"gap{d}")
                        B.did(tt(wt(10), wt(0), wt(6), ALU.mult))
                        B.wait("act", f"wk col{d}")
                        B.did(tt(tiled(wt(11)), tiled(wt(3)), over_cols(colt[:, 5, :]), ALU.mult))
                        B.wait("pe", f"qk{d}")
                        B.link(tt(wt(9), wa[:, 0:TOK], wt(8), ALU.mult), f"s{d}")
                        for n in range(TILES):
                            t = n if d == 0 or n == 0 else TILES - n
                            B.wait("pe", f"kv{d}{n}")
                            if n == 0:
                                B.link(V.tensor_copy(state[:, 0, :], wb[:, 0:2 * P]), f"state{d}0")
                            else:
                                e = t * P + last_at
                                B.link(stt(state[:, 1, :], state[:, 1, :], W[:, 6, e:e + 1], wb[:, 0:2 * P],
                                           ALU.mult, ALU.add), f"state{d}{n}")
                            q = W[:, 16, 0:P]
                            B.link(stt(q, wa[:, 512:512 + P], -1.0, T(wt(7), t), ALU.mult, ALU.max))
                            B.link(tt(q, q, wa[:, 512:512 + P], ALU.max))
                            B.link(V.reciprocal(q, q))
                            if d == 0:
                                B.link(tt(T(wt(12), t), wa[:, 0:P], q, ALU.mult), f"h taken{d}{n}")
                            else:
                                B.link(tt(q, wa[:, 0:P], q, ALU.mult), f"h taken{d}{n}")
                                B.link(tt(T(wt(12), t), T(wt(12), t), q, ALU.add))
                        if d == 0:
                            dve.wait_ge(cstate_out[0], (l * H_C + h + 1) * 32)
                            B.did(V.memset(cst[:, 2:3], 0.0), "hB ready")
                    B.did(V.memset(cst[:, 2:3], 0.0), "h whole")
                    sigmoid_from_exp(B, wt(13))
                    sigmoid_from_exp(B, wt(15))
                    B.link(tt(wt(14), wt(14), wt(15), ALU.mult))
                    B.link(tt(wt(14), wt(14), wt(13), ALU.mult))
                    B.wait("act", "h rstd")
                    B.link(stt(wt(12), wt(12), par("mlstm_norm", 1), wt(7), ALU.mult, ALU.mult))
                    B.did(tt(xo[:, bass.ds(h + (H_A + H_B), 1), :].rearrange("p a n -> p (a n)"), wt(12), wt(14), ALU.mult))
                    B.end()

                B = s_min.body("dve", dve, l)
                kvh = h_hi[:, 4:7, :].rearrange("p a n -> p (a n)")
                kvl = h_lo[:, 4:7, :].rearrange("p a n -> p (a n)")
                for j in range(7, 15):
                    e, x = wt(10 + 2 * (j % 2)), wt(11 + 2 * (j % 2))
                    B.wait("act", f"taken{j}")
                    sigmoid_from_exp(B, e)
                    B.did(tt(xo[:, H_A + j - 7, :], x, e, ALU.mult), f"zb{j}")
                B.wait("pe", "tile14")
                dve.wait_ge(cache_in, (l + 1) * 48)
                for k in range(KV_TILES):
                    s = slice(k * KEYS + TOK, (k + 1) * KEYS)
                    c = flat(15, 2 * P)[:, k * P:(k + 1) * P]
                    B.link(V.tensor_copy(kvh[:, s], c))
                    B.did(tt(kvl[:, s], c, kvh[:, s].bitcast(F32), ALU.subtract), "cache split")
                B.link(tt(wt(7), wt(6), con[:, C_ROPE:C_ROPE + TOK], ALU.mult), "roped")
                B.wait("act", "cq rstd")
                for k in range(Q_TILES):
                    B.link(stt(wt(k), wt(k), par("q_norm", 4)[:, k:k + 1], wt(10), ALU.mult, ALU.mult))
                    B.link(V.tensor_copy(h_hi[:, k, :], wt(k)))
                    B.did(tt(h_lo[:, k, :], wt(k), h_hi[:, k, :].bitcast(F32), ALU.subtract))
                B.wait("act", "ckv rstd")
                for k in range(KV_TILES):
                    B.link(stt(wt(4 + k), wt(4 + k), par("kv_norm", 2)[:, k:k + 1], wt(11), ALU.mult, ALU.mult),
                           "ckv normed")
                for k in range(KV_TILES):
                    s = slice(k * KEYS, k * KEYS + TOK)
                    B.link(V.tensor_copy(kvh[:, s], wt(4 + k)))
                    B.did(tt(kvl[:, s], wt(4 + k), kvh[:, s].bitcast(F32), ALU.subtract))
                B.end()

                with dve.Fori(0, H_B) as h:
                    B = s_mla.body("dve", dve, l * H_B + h)
                    B.wait("pe", "q pe")
                    B.did(tt(halves(wt(1)), pj[1][:, :, 0:HALF], halves(con[:, C_ROPE:C_ROPE + TOK]), ALU.mult), "q pe roped")
                    for t in range(TILES):
                        nk = P if t == 0 else TOK
                        B.wait("pe", f"scores{t}")
                        B.link(V.reduce_max(mxs[:, 0, t:t + 1], wa[:, 0:nk], AX))
                        B.link(ts(mxs[:, 1, t:t + 1], mxs[:, 0, t:t + 1], -SM_SCALE, None, ALU.mult), f"max{t}")
                        B.wait("act", f"exp{t}")
                        B.link(V.reciprocal(mxs[:, 3, t:t + 1], mxs[:, 2, t:t + 1]))
                        B.link(ts(W[:, 6, 0:nk], W[:, 6, 0:nk], mxs[:, 3, t:t + 1], None, ALU.mult), f"normed{t}")
                        B.wait("pe", f"o{t}")
                        o = xo[:, bass.ds(h + H_A, 1), t * P:(t + 1) * P].rearrange("p a n -> p (a n)")
                        B.link(tt(o, o, wa[:, 0:P], ALU.mult), f"o taken{t}")
                    B.end()

                B = s_spl.body("dve", dve, l)
                for k in range(KT):
                    B.link(V.tensor_copy(h_hi[:, k, :], xo[:, k, :]))
                    B.did(tt(h_lo[:, k, :], xo[:, k, :], h_hi[:, k, :].bitcast(F32), ALU.subtract))
                B.end()
                with dve.Fori(0, KT // 2) as f:
                    B = s_out.body("dve", dve, l * (KT // 2) + f)
                    for j, name in enumerate(("first", "second")):
                        B.wait("pe", name)
                        B.did(ts(xo[:, bass.ds(2 * f + j, 1), :].rearrange("p a (b n) -> p (a b) n", b=2),
                                 pj[j][:, :, 0:HALF], 1.0, None, ALU.mult))
                    B.end()

                B = s_res.body("dve", dve, l)
                B.link(tt(mul[:, :, :], mod[:, 2 * KT:3 * KT, :],
                          par("g_post", KT).unsqueeze(2).to_broadcast([P, KT, 2]), ALU.mult))
                B.wait("act", "rstd")
                for k in range(KT):
                    u, x = wt(8 + k % 2), wt(6 + k % 2)
                    B.link(tt(u, xo[:, k, :], wt(5), ALU.mult))
                    dve.wait_ge(x_back[k % 2], (l * (KT // 2) + (k // 2 + 1)) * 16)
                    B.did(stt(xo[:, k, 0:CTX], u[:, 0:CTX], mul[:, k, 0:1], x[:, 0:CTX], ALU.mult, ALU.add))
                    B.did(stt(xo[:, k, CTX:TOK], u[:, CTX:TOK], mul[:, k, 1:2], x[:, CTX:TOK], ALU.mult, ALU.add),
                          f"added{k}")
                B.end()


def column_tiles(w, picks):
    depth, rows_, _ = w.shape
    w = np.concatenate([w, np.zeros((depth, rows_, 1), w.dtype)], axis=2)
    w = w[:, :, np.concatenate(picks)]
    w = w.reshape(depth, rows_ // (CELLS * P), CELLS, P, len(picks), P)
    return w.transpose(0, 4, 1, 3, 2, 5).reshape(depth, -1, P, CELLS * P)


def small_cells(w, picks):
    depth, rows_, _ = w.shape
    w = w[:, :, np.concatenate(picks)].reshape(depth, rows_ // P, P, len(picks) // 2, 2, P)
    w = w.transpose(0, 3, 2, 1, 4, 5).reshape(depth, len(picks) // 2, P, -1)
    fill = np.zeros(w.shape[:3] + (CELLS * P - w.shape[3],), w.dtype)
    return np.concatenate([w, fill], axis=3)


def swapped(first):
    at = np.arange(64)
    return np.concatenate([first + at, first + (at // 32) * 32 + (at % 32 + 16) % 32])


def constants():
    con = np.zeros((P, C_WIDTH), np.float32)
    j, i = np.arange(P)[:, None], np.arange(P)[None, :]
    con[:, C_ID:C_ID + P] = np.eye(P)
    con[:, C_ONE:C_ONE + P] = 1
    con[:, C_NEG:C_NEG + P] = np.where(i >= j, 0, NEG)
    con[:, C_NEG + P:C_NEG + 2 * P] = np.where(i <= j, 0, NEG)
    con[:, C_FOLD:C_FOLD + P] = i % 64 == j % 64
    inv = np.float32(10000.0) ** (-np.arange(0, 32, 2, dtype=np.float32) / np.float32(32))
    at = np.arange(LAT)
    angle = np.concatenate([(at // 64).astype(np.float32)[None] * np.tile(inv, 2)[:, None],
                            (at % 64).astype(np.float32)[None] * np.tile(inv, 2)[:, None]])
    sign = np.where(np.arange(64) % 32 < 16, -1, 1)[:, None]
    con[:64, C_ROPE:C_ROPE + CTX] = 1
    con[:64, C_ROPE + CTX:] = np.cos(angle)
    con[64:, C_ROPE + CTX:] = np.sin(angle) * sign
    lvl = np.zeros((P, 2, LEVELS, P), np.float32)
    for v in range(LEVELS):
        b = 1 << v
        pair = i // (2 * b) == j // (2 * b)
        lvl[:, 0, v] = pair & (i // b % 2 == 1) & (j // b % 2 == 0)
        lvl[:, 1, v] = pair & (i // b % 2 == 0) & (j // b % 2 == 1)
    return con, lvl.astype(np.float16)


def features_first(x):
    return x.T.reshape(-1, P, x.shape[0]).transpose(1, 0, 2)


def kernel(x_prompt, x_sample, cache_mla_ckv, cache_mla_krope, state_gdn, state_mlstm_c,
           state_mlstm_n, state_mlstm_m, c, c_ctx, w_ada, b_ada, g_pre, g_post, w_in,
           gdn_conv, gdn_a_log, gdn_dt_bias, gdn_norm, mla_q_norm, mla_kv_norm,
           mla_w_uq, mla_w_ukv, mlstm_b_i, mlstm_b_f, mlstm_norm, w_out):
    import concourse.bacc as bacc
    from concourse.bass_utils import run_bass_kernel_spmd

    con, lvl = constants()
    L = DEPTH

    def cols(a, n):
        return a.reshape(L, n, P).transpose(0, 2, 1)

    at = np.cumsum([0, 512, 512, 512, 512, 8, 8, 512, 256, 64, 1024, 512, 512, 512, 512, 512, 8, 8])
    qa, ka, va, za, ga, ba, cq, ckv, kr, zb, qc, kc, vc, oc, zc, ic, fc = at[:17]

    def tile(first, n=0):
        return first + n * P + np.arange(P)
    gates = np.full(P, -1)
    for quadrant, first in enumerate((ga, ba, ic, fc)):
        gates[32 * quadrant:32 * quadrant + 8] = first + np.arange(8)
    picks = [gates]
    for h in range(H_A):
        picks += [tile(x, h) for x in (qa, ka, va, za)]
    for h in range(H_C):
        picks += [tile(x, h) for x in (qc, kc, vc, oc, zc)]
    picks += [tile(cq, n) for n in range(4)] + [tile(ckv, n) for n in range(2)] + [swapped(kr)]
    picks += [tile(zb, n) for n in range(8)]
    uq = small_cells(mla_w_uq, sum([[h * 192 + np.arange(P), swapped(h * 192 + P)] for h in range(H_B)], []))
    ukv = small_cells(mla_w_ukv, sum([[h * 256 + np.arange(P), h * 256 + P + np.arange(P)] for h in range(H_B)], []))
    heads = np.stack([uq, ukv], axis=2).reshape(L, 2 * H_B, P, CELLS * P)
    stream = np.concatenate([column_tiles(w_in, picks), heads,
                             column_tiles(w_out, [tile(0, f) for f in range(KT)])], axis=1)
    params = np.zeros((L, P, PRM_WIDTH), np.float32)

    def put(name, a):
        params[:, :a.shape[1], PRM[name]:PRM[name] + a.shape[2]] = a
    put("b_ada", cols(b_ada, 48))
    put("g_pre", cols(g_pre, KT))
    put("g_post", cols(g_post, KT))
    put("conv", gdn_conv.reshape(L, CONV_K, 12, P).transpose(0, 3, 2, 1).reshape(L, P, 12 * CONV_K))
    put("gdn_norm", gdn_norm[:, :, None])
    put("q_norm", cols(mla_q_norm, 4))
    put("kv_norm", cols(mla_kv_norm, 2))
    put("mlstm_norm", mlstm_norm[:, :, None])
    put("gates", np.stack([a.reshape(L, 8) for a in (gdn_a_log, gdn_dt_bias, mlstm_b_i, mlstm_b_f)], axis=2))

    arrays = {
        "constants": con, "levels": lvl, "params": params,
        "x": features_first(np.concatenate([x_prompt[0], x_sample[0]], axis=0)),
        "cond": np.stack([c_ctx.reshape(KT, P).T, c[0].reshape(KT, P).T], axis=2),
        "w_ada": column_tiles(w_ada, [tile(0, m) for m in range(3 * KT)]),
        "w_stream": stream,
        "state_gdn": state_gdn[0], "state_c": state_mlstm_c[0], "state_n": state_mlstm_n[0][..., None],
        "m0": state_mlstm_m[0].reshape(L, 8, 1),
        "cache_ckv": cache_mla_ckv[0].transpose(0, 2, 1).reshape(L, 2, P, PAST).transpose(0, 2, 1, 3).reshape(L, P, 2 * PAST),
        "cache_kr": cache_mla_krope[0].transpose(0, 2, 1),
    }
    arrays = {n: np.ascontiguousarray(a) for n, a in arrays.items()}
    outs = {"y": (P, KT, TOK), "new_ckv": (L, P, 2, CTX), "new_kr": (L, 64, CTX),
            "new_gdn": (L, 2, H_A, P, P), "new_c": (L, 2, H_C, P, P), "new_n": (L, 2, H_C, P, 1),
            "new_m": (L, 2, H_C, 1)}

    book = {}
    for _ in range(2):
        nc = bacc.Bacc("TRN2", target_bir_lowering=False, num_devices=1)
        io = {n: nc.dram_tensor(f"in_{n}", a.shape, F16 if n == "levels" else F32, kind="ExternalInput").ap()
              for n, a in arrays.items()}
        io.update({n: nc.dram_tensor(f"out_{n}", s, F32, kind="ExternalOutput").ap() for n, s in outs.items()})
        build(nc, io, book)
    r = run_bass_kernel_spmd(nc, [{f"in_{n}": a for n, a in arrays.items()}], core_ids=[0])
    got = {n: r.results[0][f"out_{n}"] for n in outs}
    y = got["y"].transpose(2, 1, 0).reshape(TOK, D_MODEL)
    return (y[None, :CTX], y[None, CTX:],
            got["new_ckv"].transpose(0, 3, 2, 1).reshape(1, L, CTX, 2 * P),
            got["new_kr"].transpose(0, 2, 1)[None],
            got["new_gdn"][None], got["new_c"][None], got["new_n"][None, ..., 0], got["new_m"][None, ..., 0])
```

```python
import math
from contextlib import ExitStack

import numpy as np
import concourse.bass as bass
from concourse import mybir

F32 = mybir.dt.float32
F32R = mybir.dt.float32r
F16 = mybir.dt.float16
ACT = mybir.ActivationFunctionType
ALU = mybir.AluOpType
AX = mybir.AxisListType.X

P = 128
DEPTH, D_MODEL, CTX, LAT = 2, 2048, 128, 512
TOK = CTX + LAT
TILES = TOK // P
STRIP = TOK // 8
HALF = TOK // 2
KT = D_MODEL // P
H_A, H_B, H_C = 4, 8, 4
Q_TILES, KV_TILES = 4, 2
PAST = 128
KEYS = TOK + PAST
EPS = 1e-6
CONV_K = 5
PADW = TOK + 8
CONVW = TOK + 4
SM_SCALE = float((128 + 64) ** -0.5)
DK_SCALE = float(P ** -0.5)
NEG = -1.0e30
LEVELS = 7
GATE_COLS = 104

ADA_COLS = 1024
ADA_GROUPS = 3 * D_MODEL // ADA_COLS
ADA_HALVES = ADA_GROUPS * KT
ADA_PAIRS = ADA_GROUPS // 2
ADA_TILES = ADA_COLS // P
STREAM = dict(gates=2, gdn=8 * H_A, mlstm=10 * H_C, mla_in=30, mla=2 * H_B, out=2 * KT)
STREAM_HALVES = sum(STREAM.values())
CELLS = 8
RAW_SLOTS = 4

C_ID, C_ONE, C_NEG, C_FOLD, C_ROPE = 0, 128, 256, 512, 640
C_WIDTH = C_ROPE + TOK
PRM = {}
_at = 0
for _n, _w in (("b_ada", 48), ("g_pre", 16), ("g_post", 16), ("conv", 12 * CONV_K), ("gdn_norm", 1),
               ("q_norm", 4), ("kv_norm", 2), ("mlstm_norm", 1), ("gates", 4)):
    PRM[_n] = _at
    _at += _w
PRM_WIDTH = _at


class Stage:

    def __init__(self, name, sems, passed, book):
        self.name, self.sems, self.passed = name, sems, passed
        self.book = book.setdefault(name, {e: {} for e in sems})
        self.total = {e: self.book[e].get("", 1) for e in sems}

    def body(self, me, eng, turn):
        return Body(self, me, eng, turn)


class Body:

    def __init__(self, stage, me, eng, turn):
        self.stage, self.me, self.eng, self.n = stage, me, eng, 0
        self.base = {e: 0 if turn is None else eng.snap(turn * stage.total[e]) for e in stage.sems}
        self.seen = {}

    def value(self, who, n):
        return self.base[who] + n

    def did(self, ins, label=None):
        ins.then_inc(self.stage.sems[self.me], 1)
        self.n += 1
        if label:
            self.stage.book[self.me][label] = self.n
        return ins

    def link(self, ins, label=None):
        self.did(ins, label)
        self.eng.wait_ge(self.stage.sems[self.me], self.value(self.me, self.n))

    def wait(self, who, label):
        n = self.stage.book[who].get(label, 1)
        if self.seen.get(who, 0) < n:
            self.seen[who] = n
            self.eng.wait_ge(self.stage.sems[who], self.value(who, n))

    def leave(self):
        self.stage.book[self.me][""] = self.n

    def end(self):
        self.leave()
        for who in self.stage.sems:
            n = self.n if who == self.me else self.stage.total[who]
            self.eng.wait_ge(self.stage.sems[who], self.value(who, n))
        self.eng.sem_inc(self.stage.passed, 1)


def build(nc, io, book):
    ctx = ExitStack()
    with ctx:
        def sb(name, shape, dt=F32):
            return ctx.enter_context(nc.sbuf_tensor(name, shape, dt))

        def ps(name, shape):
            return ctx.enter_context(nc.psum_tensor(name, shape, F32))

        def sem(name):
            return ctx.enter_context(nc.semaphore(name))

        def stage(name, engines="pe act dve"):
            return Stage(name, {e: sem(f"{name}_{e}_steps") for e in engines.split()}, sem(f"{name}_passed"), book)

        h_hi = sb("h_hi", [P, KT, TOK], F32R)
        h_lo = sb("h_lo", [P, KT, TOK], F32R)
        xo = sb("xo", [P, KT, TOK])
        raw = sb("raw", [P, RAW_SLOTS, CELLS, P])
        w_hi = sb("w_hi", [P, 2, CELLS, P], F32R)
        w_lo = sb("w_lo", [P, 2, CELLS, P], F32R)
        W = sb("work", [P, 17, TOK])
        con = sb("constants", [P, C_WIDTH])
        lvl = sb("level_masks", [P, 2, LEVELS, P], F16)
        prm = sb("parameters", [P, PRM_WIDTH])
        cond = sb("cond", [P, KT, 2])
        cond_t = sb("cond_t", [P, KT, 2])
        mod = sb("mod", [P, 3 * KT, 2])
        mul = sb("mul", [P, KT, 2])
        tokc = sb("token_columns", [P, 5, TILES, 8])
        colt = sb("column_temps", [P, 12, TILES])
        hcw = sb("head_conv", [P, 3, CONV_K])
        state = sb("state", [P, 2, 2 * P])
        mxs = sb("row_sums", [P, 4, TILES])
        mprev = sb("m_prev", [8, 2, TILES])
        m0 = sb("m0", [8, 1])
        mout = sb("m_out", [8, 2])
        n0 = sb("n0", [P, 1])
        cst = sb("small_constants", [P, 3])

        pj = [ps(f"projection{i}", [P, 2, 512]) for i in range(2)]
        wa = ps("wa", [P, 1024])
        wb = ps("wb", [P, 1024])

        rows = nc.dram_tensor("rows", [5, 8, TOK], F32, kind="Internal").ap()
        x_kept = nc.dram_tensor("x_kept", [P, KT, TOK], F32, kind="Internal").ap()

        ident = con[:, C_ID:C_ID + P]
        ones = con[:, C_ONE:C_ONE + P]

        def neg(d):
            return con[:, C_NEG + d * P:C_NEG + (d + 1) * P]

        def tiled(ap):
            return ap.rearrange("p (t c) -> p t c", c=P)

        def over_tiles(ap):
            return ap.unsqueeze(1).to_broadcast([P, TILES, P])

        def over_cols(ap):
            return ap.unsqueeze(2).to_broadcast([P, TILES, P])

        def halves(ap):
            return ap.rearrange("p (a n) -> p a n", a=2)

        def wt(i):
            return W[:, i, :]

        def xt(i):
            return xo[:, i, :]

        lvt = [wt(12), xt(9)]
        row_g, row_beta = [wt(5), xt(10)], [wt(6), xt(11)]

        def T(ap, t):
            return ap[:, t * P:(t + 1) * P]

        def flat(i, n, of=W):
            return of[:, i:i + 2, :].rearrange("p a n -> p (a n)")[:, 0:n]

        pads = [flat(9, PADW), flat(11, PADW), flat(13, PADW)]
        convs = [flat(15, CONVW), flat(10, CONVW, xo), flat(7, CONVW)]

        MLA_ORDER, MLA_PS = [1, 2, 3, 4, 0], (wa, wb)
        MLA_SCORES = [pj[i][:, :, :].rearrange("p a n -> p (a n)") for i in range(2)]

        raw_full = [sem(f"raw_full{s}") for s in range(RAW_SLOTS)]
        raw_free = [sem(f"raw_free{s}") for s in range(RAW_SLOTS)]
        split_done = sem("split_done")
        split_part = sem("split_part")
        split_used = sem("split_used")
        const_in = sem("const_in")
        x_in = sem("x_in")
        params_in = sem("params_in")
        x_saved = sem("x_saved")
        x_back = [sem(f"x_back{i}") for i in range(4)]
        rows_out = sem("rows_out")
        m0_in = sem("m0_in")
        m_out = sem("m_out_stored")
        rows_in = [sem(f"rows_in{d}") for d in range(2)]
        state_in = [sem(f"state_in{d}") for d in range(2)]
        state_out = [sem(f"state_out{d}") for d in range(2)]
        crows_in = [sem(f"mlstm_rows_in{d}") for d in range(2)]
        cstate_in = [sem(f"mlstm_state_in{d}") for d in range(2)]
        cstate_out = [sem(f"mlstm_state_out{d}") for d in range(2)]
        cache_in = sem("cache_in")
        latent_out = sem("latent_out")
        y_out = sem("y_out")

        s_init = stage("init", "act dve")
        s_ada = stage("ada", "pe dve")
        s_norm = stage("norm")
        s_gate = stage("gates")
        s_gdn = stage("gdn")
        s_mli = stage("mlstm_in", "pe act")
        s_mls = stage("mlstm")
        s_min = stage("mla_in")
        s_mla = stage("mla")
        s_spl = stage("out_split")
        s_out = stage("out")
        s_res = stage("residual")

        block = ctx.enter_context(nc.Block())

        @block.sync
        def _(sp):
            sp.dma_start(con[:, :], io["constants"]).then_inc(const_in, 16)
            sp.dma_start(lvl[:, :, :, :], io["levels"]).then_inc(const_in, 16)
            sp.dma_start(cond_t[:, :, :], io["cond"]).then_inc(const_in, 16)
            sp.dma_start(xo[:, :, :], io["x"]).then_inc(x_in, 16)
            for s in range(RAW_SLOTS):
                sp.sem_inc(raw_free[s], 1)
            per_layer = (ADA_HALVES + STREAM_HALVES) // RAW_SLOTS
            with sp.Fori(0, DEPTH) as l:
                for n, first, src in ((ADA_HALVES, 0, io["w_ada"]),
                                      (STREAM_HALVES, ADA_HALVES // RAW_SLOTS, io["w_stream"])):
                    with sp.Fori(0, n // RAW_SLOTS) as i:
                        turn = sp.snap(l * per_layer + i + first + 1)
                        for s in range(RAW_SLOTS):
                            sp.wait_ge(raw_free[s], turn)
                            sp.dma_start(raw[:, s, :, :].rearrange("p c n -> p (c n)"),
                                         src[l, i * RAW_SLOTS + s, :, :]).then_inc(raw_full[s], 16)

        @block.gpsimd
        def _(pool):
            once = ones.unsqueeze(1).to_broadcast([P, CELLS, P])
            pool.wait_ge(const_in, 48)
            pool.sem_inc(split_used, 2)
            per_layer = (ADA_HALVES + STREAM_HALVES) // RAW_SLOTS
            with pool.Fori(0, DEPTH) as l:
                with pool.Fori(0, STREAM_HALVES // RAW_SLOTS) as i:
                    turn = pool.snap((l * per_layer + i + (ADA_HALVES // RAW_SLOTS + 1)) * 16)
                    done = pool.snap((l * (STREAM_HALVES // RAW_SLOTS) + i) * RAW_SLOTS)
                    for s in range(RAW_SLOTS):
                        pool.wait_ge(split_used, done + s + 1)
                        pool.wait_ge(raw_full[s], turn)
                        nc.gpsimd.tensor_tensor(w_hi[:, s % 2, :, :], raw[:, s, :, :], once, ALU.mult).then_inc(split_part, 1)
                        pool.wait_ge(split_part, done * 2 + 2 * s + 1)
                        nc.gpsimd.tensor_tensor(w_lo[:, s % 2, :, :], raw[:, s, :, :],
                                                w_hi[:, s % 2, :, :].bitcast(F32), ALU.subtract)\
                            .then_inc(split_part, 1)
                        pool.wait_ge(split_part, done * 2 + 2 * s + 2)
                        pool.sem_inc(raw_free[s], 1)
                        pool.sem_inc(split_done, 1)

        @block.tensor
        def _(pe):
            mm = nc.tensor.matmul

            def parts_ready(n):
                pe.wait_ge(split_done, n + 1)

            def project(out, n):
                last = None
                for half in range(2):
                    parts_ready(n + half)
                    for c in range(CELLS):
                        k = half * CELLS + c
                        for a in range(2):
                            hs = slice(a * HALF, (a + 1) * HALF)
                            o = out[:, a, 0:HALF]
                            mm(o, w_hi[:, half, c, :], h_hi[:, k, hs], start=(k == 0), stop=False)
                            mm(o, w_hi[:, half, c, :], h_lo[:, k, hs], start=False, stop=False)
                            last = mm(o, w_lo[:, half, c, :], h_hi[:, k, hs], start=False, stop=(k == KT - 1))
                    if half == 0:
                        last.then_inc(split_used, 1)
                return last

            def used_and(B, last, n, label):
                last.then_inc(split_used, 1)
                pe.wait_ge(split_used, n + 2)
                B.did(pe.nop(), label)

            class Ahead:

                def __init__(self, B, n, tiles):
                    self.B, self.n, self.tiles, self.at = B, n, tiles, 0

                def cells(self, count):
                    for _ in range(count):
                        j, k = divmod(self.at, KT)
                        if j == self.tiles:
                            break
                        if k == 0 and j >= 2:
                            self.B.wait("act", f"ahead taken{j - 2}")
                        half, c = divmod(k, CELLS)
                        if c == 0:
                            parts_ready(self.n + (2 * j + half))
                        for a in range(2):
                            hs, o = slice(a * HALF, (a + 1) * HALF), pj[j % 2][:, a, 0:HALF]
                            mm(o, w_hi[:, half, c, :], h_hi[:, k, hs], start=(k == 0), stop=False)
                            mm(o, w_hi[:, half, c, :], h_lo[:, k, hs], start=False, stop=False)
                            last = mm(o, w_lo[:, half, c, :], h_hi[:, k, hs], start=False, stop=(k == KT - 1))
                        if c == CELLS - 1:
                            last.then_inc(split_used, 1)
                        self.at += 1

                def finish(self):
                    self.cells(self.tiles * KT - self.at)

            def each_tile(out, lhs, rhs):
                last = None
                for t in range(TILES):
                    last = mm(T(out, t), T(lhs, t), T(rhs, t), start=True, stop=True)
                return last

            def transposed(out, src):
                last = None
                for t in range(TILES):
                    last = nc.tensor.transpose(T(out, t), T(src, t), ident)
                return last

            def column_sums(out, src, first=True, last=True):
                mm(out[:, 0:512], ones, src[:, 0:512], start=first, stop=last)
                return mm(out[:, 512:TOK], ones, src[:, 512:TOK], start=first, stop=last)

            def halved_sums(out, src):
                mm(out[:, 0, 0:HALF], ones, src[:, 0:HALF], start=True, stop=True)
                return mm(out[:, 1, 0:HALF], ones, src[:, HALF:TOK], start=True, stop=True)

            pe.wait_ge(const_in, 48)
            with pe.Fori(0, DEPTH) as l:
                per_layer = (ADA_HALVES + STREAM_HALVES) // RAW_SLOTS

                def ada_turn(i):
                    B = s_ada.body("pe", pe, l * ADA_PAIRS + i)
                    turn = pe.snap((l * per_layer + i * (2 * KT // RAW_SLOTS) + 1) * 16)

                    def group(j, ks):
                        for k in ks:
                            s, use = k % RAW_SLOTS, (j * KT + k) // RAW_SLOTS
                            pe.wait_ge(raw_full[s], turn + 16 * use)
                            for a in range(2):
                                last = mm((wa, wb)[j][0:2, a * 512:(a + 1) * 512], cond[:, k, :],
                                          raw[:, s, 4 * a:4 * a + 4, :].rearrange("p c n -> p (c n)"),
                                          start=(k == 0), stop=(k == KT - 1))
                            last.then_inc(raw_free[s], 1)

                    def turned(j):
                        B.wait("dve", f"rows{j}")
                        B.did(pe.nop())
                        for c in range(ADA_TILES):
                            last = nc.tensor.transpose(pj[0][:, 0, (j * ADA_TILES + c) * 2:(j * ADA_TILES + c + 1) * 2],
                                                       flat(13 + 2 * j, ADA_COLS)[0:2, c * P:(c + 1) * P], con[0:2, 0:2])
                        B.did(last, f"turned{j}")

                    group(0, range(KT))
                    group(1, range(KT // 2))
                    turned(0)
                    group(1, range(KT // 2, KT))
                    turned(1)
                    B.end()

                pe.wait_ge(s_init.sems["dve"], s_init.total["dve"])
                with pe.Fori(0, ADA_PAIRS - 1) as i:
                    ada_turn(i)
                N = s_norm.body("pe", pe, l)
                N.wait("dve", f"squares{KT - 1}")
                N.did(halved_sums(pj[1], wt(8)), "sum")
                ada_turn(ADA_PAIRS - 1)

                layer0 = pe.snap(l * STREAM_HALVES)
                last = None
                for k in range(KT):
                    half, c = divmod(k, CELLS)
                    if c == 0:
                        parts_ready(layer0 + half)
                    N.wait("dve", f"h{k}")
                    for a in range(2):
                        hs, o = slice(a * HALF, (a + 1) * HALF), pj[0][:, a, 0:HALF]
                        mm(o, w_hi[:, half, c, :], h_hi[:, k, hs], start=(k == 0), stop=False)
                        mm(o, w_hi[:, half, c, :], h_lo[:, k, hs], start=False, stop=False)
                        last = mm(o, w_lo[:, half, c, :], h_hi[:, k, hs], start=False, stop=(k == KT - 1))
                    if k == CELLS - 1:
                        last.then_inc(split_used, 1)
                used_and(N, last, layer0 + 2, "gates")
                N.end()

                B = s_gate.body("pe", pe, l)
                for j in range(4):
                    B.wait("act", "log" if j < 2 else f"ahead taken{j - 2}")
                    project(pj[j % 2], layer0 + (2 * j + 2)).then_inc(split_used, 1)
                for n, (label, src) in enumerate((("cum", 10), ("cum", 12), ("beta", 14), ("aF", 0), ("aB", 1))):
                    B.wait("dve", label)
                    if n in (0, 2, 3, 4):
                        B.did(pe.nop())
                    for t in range(TILES):
                        last = nc.tensor.transpose(wb[:, (n * TILES + t) * 8:(n * TILES + t + 1) * 8],
                                                   W[0:8, src, t * P:(t + 1) * P], con[0:8, 0:8])
                    B.did(last, f"columns{n}")
                B.end()

                with pe.Fori(0, H_A) as h:
                    B = s_gdn.body("pe", pe, l * H_A + h)
                    ahead = Ahead(B, pe.snap(l * STREAM_HALVES + h * 8 + (STREAM["gates"] + 8)), 4)
                    ahead.cells(12)
                    B.wait("act", "q squared")
                    B.did(column_sums(wa, wt(9)), "q sum")
                    ahead.cells(4)
                    B.wait("act", "k squared")
                    B.did(column_sums(wb, wt(11)), "k sum")
                    ahead.cells(8)
                    B.wait("dve", "k normed")
                    B.did(transposed(wa, wt(1)), "k turned")
                    ahead.cells(8)
                    B.wait("dve", "v silu")
                    B.did(transposed(wb, wt(4)), "v turned")
                    for d in range(2):
                        B.wait("dve", f"kb{d}")
                        B.wait("act", "v turned taken")
                        B.did(each_tile(wa, wt(1), wt(14)), f"kk{d}")
                        B.did(each_tile(wb, wt(1), wt(0)), f"qk{d}")
                        ahead.cells(2)
                        for v in range(LEVELS):
                            B.wait("dve", f"level{d}{v}")
                            last = None
                            for t in range(TILES):
                                last = mm(T(wa, t), T(lvt[v % 2], t), ident if v == 0 else T(wt(10), t),
                                          start=True, stop=True)
                            B.did(last, f"ld{d}{v}")
                            if v:
                                B.wait("act", f"ld taken{d}{v}")
                                if v < LEVELS - 1:
                                    B.did(each_tile(wb, wt(11), wt(13)), f"dld{d}{v}")
                                B.did(each_tile(wa, wt(13), wt(11)), f"dldT{d}{v}")
                            ahead.cells(1 + v % 2)
                        B.wait("dve", f"inverse{d}")
                        B.wait("dve", f"kbg{d}")
                        B.did(each_tile(wa, wt(15), wt(11)), f"wT{d}")
                        B.wait("act", f"wT taken{d}")
                        B.wait("dve", f"kdec{d}")
                        order = [0, 1, 2, 3, 4] if d == 0 else [0, 4, 3, 2, 1]
                        for n, t in enumerate(order):
                            st = state[:, min(n, 1), 0:P]
                            last = mm(wa[:, 0:P], T(wt(11), t), T(wt(14), t), start=True, stop=(n == 0))
                            if n == 1:
                                pe.wait_ge(state_in[d], (l * H_A + h + 1) * 16)
                            if n:
                                if n > 1:
                                    B.wait("dve", f"state{d}{n - 1}")
                                last = mm(wa[:, 0:P], T(wt(12), t), st, start=False, stop=True)
                            B.did(last, f"vnew{d}{n}")
                            if n:
                                mm(wa[:, 512:512 + P], st, T(wt(13), t), start=True, stop=False)
                            B.wait("act", f"vnew taken{d}{n}")
                            last = mm(wa[:, 512:512 + P], T(wt(9), t), T(wt(16), t), start=(n == 0), stop=True)
                            B.did(last, f"o{d}{n}")
                            B.did(mm(wb[:, 0:P], T(wt(10), t), T(wt(9), t), start=True, stop=True), f"kv{d}{n}")
                            ahead.cells(1)
                            if n == TILES - 1:
                                ahead.cells((3 + d) * KT - ahead.at)
                            B.wait("dve", f"o taken{d}{n}")
                    B.wait("act", "o squared")
                    B.did(column_sums(wa, wt(6)), "o sum")
                    B.end()

                B = s_mli.body("pe", pe, l)
                n0_ = pe.snap(l * STREAM_HALVES + (STREAM["gates"] + STREAM["gdn"] + 8))
                used_and(B, project(pj[0], n0_), n0_ + 2, "z")
                B.end()
                with pe.Fori(0, H_C) as h:
                    B = s_mls.body("pe", pe, l * H_C + h)
                    ahead = Ahead(B, pe.snap(l * STREAM_HALVES + h * 10 + (STREAM["gates"] + STREAM["gdn"] + 10)), 5)
                    ahead.cells(4)
                    B.wait("act", "k taken")
                    B.did(transposed(wa, wt(1)), "k turned")
                    B.wait("act", "v taken")
                    B.did(transposed(wb, wt(2)), "v turned")
                    ahead.cells(12)
                    for d in range(2):
                        B.wait("dve", "v turned taken")
                        B.wait("act", "k turned taken")
                        if d:
                            B.wait("dve", "hB ready")
                        B.did(each_tile(wa, wt(1), wt(0)), f"qk{d}")
                        ahead.cells(4)
                        B.wait("dve", f"s{d}")
                        order = [0, 1, 2, 3, 4] if d == 0 else [0, 4, 3, 2, 1]
                        for n, t in enumerate(order):
                            if n:
                                if n == 1:
                                    B.wait("dve", f"n rep{d}")
                                else:
                                    B.wait("dve", f"state{d}{n - 1}")
                                mm(wa[:, 0:P], state[:, 1, 0:P], T(wt(10), t), start=True, stop=False)
                            mm(wa[:, 0:P], T(wt(4), t), T(wt(9), t), start=(n == 0), stop=True)
                            if n:
                                mm(wa[:, 512:512 + P], state[:, 1, P:2 * P], T(wt(10), t), start=True, stop=False)
                            B.did(mm(wa[:, 512:512 + P], ones, T(wt(9), t), start=(n == 0), stop=True), f"numden{d}{n}")
                            mm(wb[:, 0:P], T(wt(11), t), T(wt(4), t), start=True, stop=True)
                            B.did(mm(wb[:, P:2 * P], T(wt(11), t), ones, start=True, stop=True), f"kv{d}{n}")
                            ahead.cells(4 + 2 * d)
                            B.wait("dve", f"h taken{d}{n}")
                    ahead.finish()
                    B.wait("act", "h squared")
                    B.did(column_sums(wa, wt(6)), "h sum")
                    B.end()

                B = s_min.body("pe", pe, l)
                n0_ = pe.snap(l * STREAM_HALVES + (STREAM["gates"] + STREAM["gdn"] + STREAM["mlstm"]))
                for j in range(5, 15):
                    if j >= 7:
                        B.wait("act", f"taken{j - 2}")
                    used_and(B, project(pj[j % 2], n0_ + 2 * j), n0_ + 2 * j + 2, f"tile{j}")
                for k in range(Q_TILES):
                    B.wait("act", f"cq squared{k}")
                    B.did(column_sums(wa, wt(10 + k), k == 0, k == Q_TILES - 1), f"cq sum{k}")
                for k in range(KV_TILES):
                    B.wait("act", f"ckv squared{k}")
                    B.did(column_sums(wb, wt(14 + k), k == 0, k == KV_TILES - 1), f"ckv sum{k}")
                B.wait("dve", "roped")
                B.wait("act", "cq logged")
                mm(wa[:, 0:512], con[:, C_FOLD:C_FOLD + P], W[:, 7, 0:512], start=True, stop=True)
                B.did(mm(wa[:, 512:TOK], con[:, C_FOLD:C_FOLD + P], W[:, 7, 512:TOK], start=True, stop=True), "key pe")
                B.end()

                with pe.Fori(0, H_B) as h:
                    B = s_mla.body("pe", pe, l * H_B + h)
                    n0_ = pe.snap(l * STREAM_HALVES + h * 2
                                  + (STREAM["gates"] + STREAM["gdn"] + STREAM["mlstm"] + STREAM["mla_in"]))
                    cqn = [(h_hi[:, k, :], h_lo[:, k, :]) for k in range(Q_TILES)]
                    kvh = h_hi[:, 4:7, :].rearrange("p a n -> p (a n)")
                    kvl = h_lo[:, 4:7, :].rearrange("p a n -> p (a n)")

                    def three(out, hi, lo, xh, xl, first, last):
                        mm(out, hi, xh, start=first, stop=False)
                        mm(out, hi, xl, start=False, stop=False)
                        return mm(out, lo, xh, start=False, stop=last)

                    parts_ready(n0_)
                    for which in range(2):
                        for k in range(Q_TILES):
                            for a in range(2):
                                hs = slice(a * HALF, (a + 1) * HALF)
                                last = three(pj[which][:, a, 0:HALF], w_hi[:, 0, 2 * k + which, :],
                                             w_lo[:, 0, 2 * k + which, :], cqn[k][0][:, hs], cqn[k][1][:, hs],
                                             k == 0, k == Q_TILES - 1)
                        if which == 0:
                            B.did(last, "q nope")
                    used_and(B, last, n0_ + 1, "q pe")
                    parts_ready(n0_ + 1)
                    B.wait("act", "q nope taken")
                    for k in range(KV_TILES):
                        for a in range(2):
                            at = k * KEYS + a * (KEYS // 2)
                            last = three(pj[0][:, a, 0:KEYS // 2], w_hi[:, 1, 2 * k, :], w_lo[:, 1, 2 * k, :],
                                         kvh[:, at:at + KEYS // 2], kvl[:, at:at + KEYS // 2],
                                         k == 0, k == KV_TILES - 1)
                    B.did(last, "k nope")
                    B.wait("dve", "q pe roped")
                    for t in range(KEYS // P):
                        o = pj[1][:, t // 3, (t % 3) * P:(t % 3 + 1) * P]
                        for k in range(KV_TILES):
                            at = k * KEYS + t * P
                            last = three(o, kvh[:, at:at + P], kvl[:, at:at + P], w_hi[:, 1, 2 * k + 1, :],
                                         w_lo[:, 1, 2 * k + 1, :], k == 0, k == KV_TILES - 1)
                    used_and(B, last, n0_ + 2, "v")
                    qn, qp, kn, kp, vt = wt(0), wt(1), flat(2, KEYS), flat(8, KEYS), flat(4, KEYS)

                    def scores(m):
                        t = MLA_ORDER[m]
                        if m == 1:
                            B.wait("act", "v taken")
                        if m >= 2:
                            B.wait("act", f"exp{m - 2}")
                        spans = [(0, CTX, 0)] if t == 0 else [(CTX, TOK, 0), (TOK, KEYS, 512)]
                        for a, b, o in spans:
                            mm(MLA_SCORES[m % 2][:, o:o + b - a], T(qn, t), kn[:, a:b], start=True, stop=False)
                            last = mm(MLA_SCORES[m % 2][:, o:o + b - a], T(qp, t), kp[:, a:b], start=False, stop=True)
                        B.did(last, f"scores{m}")

                    def turned(m):
                        t = MLA_ORDER[m]
                        B.wait("dve", f"normed{m}")
                        for j in range(1 if t == 0 else TILES):
                            last = nc.tensor.transpose(T(MLA_PS[m % 2], j), T(wt(6 + 4 * (m % 2)), j), ident)
                        B.did(last, f"turned{m}")

                    def output(m):
                        t = MLA_ORDER[m]
                        nk, k0 = (1, 0) if t == 0 else (TILES, 1)
                        B.wait("act", f"turned taken{m}")
                        if m >= 2:
                            B.wait("dve", f"o taken{m - 2}")
                        for j in range(nk):
                            last = mm(MLA_PS[m % 2][:, 768:768 + P], T(vt, k0 + j), T(wt(7 + 4 * (m % 2)), j),
                                      start=(j == 0), stop=(j == nk - 1))
                        B.did(last, f"o{m}")

                    B.wait("act", "k nope taken")
                    for m in range(TILES + 1):
                        if m < TILES:
                            scores(m)
                        if m >= 2:
                            output(m - 2)
                        if m >= 1:
                            turned(m - 1)
                    output(TILES - 1)
                    B.end()

                B = s_spl.body("pe", pe, l)
                B.did(pe.nop())
                B.end()
                with pe.Fori(0, KT // 2) as f:
                    B = s_out.body("pe", pe, l * (KT // 2) + f)
                    n0_ = pe.snap(l * STREAM_HALVES + f * 4 + (STREAM_HALVES - STREAM["out"]))
                    used_and(B, project(pj[0], n0_), n0_ + 2, "first")
                    used_and(B, project(pj[1], n0_ + 2), n0_ + 2 + 2, "second")
                    B.end()
                B = s_res.body("pe", pe, l)
                B.did(halved_sums(pj[0], wt(8)), "sum")
                B.leave()

        @block.scalar
        def _(act):
            A = nc.scalar.activation
            act.preload_act_table_set("natural_log_exp_and_others")
            def sigmoid(B, out, src, label):
                B.link(A(out, src, ACT.Exp, scale=-1.0))
                B.link(A(out, out, ACT.Ln, bias=1.0))
                B.did(A(out, out, ACT.Exp, scale=-1.0), label)

            def take(B, n, j, dst):
                act.wait_ge(split_used, n + (2 * j + 4))
                B.did(A(halves(dst), pj[j % 2][:, :, 0:HALF], ACT.Copy), f"ahead taken{j}")

            def rsqrt(B, out, src, tmp, scale, label, post=1.0, mid=None):
                B.link(A(tmp, src, ACT.Ln, bias=cst[:, 0:1], scale=scale), mid)
                B.link(A(out, tmp, ACT.Exp, scale=-0.5, bias=(cst[:, 1:2] if post != 1.0 else 0.0)), label)

            act.wait_ge(const_in, 48)
            B = s_init.body("act", act, None)
            B.wait("dve", "eps")
            B.link(A(cond[:, :, :], cond_t[:, :, :], ACT.Exp, scale=-1.0), "cond exp")
            B.end()
            with act.Fori(0, DEPTH) as l:
                act.dma_start(prm[:, :], io["params"][l, :, :]).then_inc(params_in, 16)
                act.dma_start(m0[:, :], io["m0"][l, :, :]).then_inc(m0_in, 16)
                act.wait_ge(x_in, 16)
                act.dma_start(x_kept, xo[:, :, :]).then_inc(x_saved, 16)

                B = s_norm.body("act", act, l)
                for k in range(KT):
                    if k >= 4:
                        B.wait("dve", f"squares{max(k - 4, 1)}")
                    B.did(A(wt(k % 4), xo[:, k, :], ACT.Square), f"square{k}")
                B.wait("pe", "sum")
                rsqrt(B, halves(wt(5)), pj[1][:, :, 0:HALF], halves(wt(4)), 1.0 / D_MODEL, "rstd")
                for k in range(KT):
                    B.wait("dve", f"u{k}")
                    B.did(A(h_hi[:, k, :], wt(6 + k % 4), ACT.Copy), f"hi{k}")
                B.end()

                B = s_gate.body("act", act, l)
                g = PRM["gates"]
                act.wait_ge(params_in, (l + 1) * 16)
                xx = W[0:8, 0:2, :]
                B.link(A(colt[0:8, 0, 0:1], prm[0:8, g:g + 1], ACT.Exp), "exp a_log")

                def gate(at):
                    return pj[0][at:at + 8, :, 0:HALF]
                B.did(A(halves(W[0:8, 0, :]), gate(0), ACT.Identity, bias=prm[0:8, g + 1:g + 2]))
                B.did(A(halves(W[0:8, 1, :]), gate(96), ACT.Identity, bias=prm[0:8, g + 3:g + 4]))
                B.did(A(halves(W[0:8, 15, :]), gate(64), ACT.Identity, bias=prm[0:8, g + 2:g + 3]), "i")
                B.link(A(halves(W[0:8, 14, :]), gate(32), ACT.Exp, scale=-1.0), "beta exp")
                B.link(A(W[0:8, 1, :], W[0:8, 1, :], ACT.Copy, scale=-1.0), "x")
                B.link(A(W[0:8, 2:4, :], xx, ACT.Abs))
                B.link(A(W[0:8, 2:4, :], W[0:8, 2:4, :], ACT.Exp, scale=-1.0))
                B.link(A(W[0:8, 2:4, :], W[0:8, 2:4, :], ACT.Ln, bias=1.0), "log")
                act.wait_ge(x_saved, (l + 1) * 16)
                n0_ = act.snap(l * STREAM_HALVES + STREAM["gates"])
                take(B, n0_, 0, xt(4))
                take(B, n0_, 1, xt(5))
                B.wait("dve", "wi")
                B.link(A(W[0:8, 6:8, :], W[0:8, 6:8, :], ACT.Exp), "wi exp")
                B.wait("dve", "em")
                B.link(A(W[0:8, 8:10, :], W[0:8, 8:10, :], ACT.Exp, scale=-1.0), "em exp")
                for d in range(2):
                    hs = slice(4 * d, 4 * d + 4)
                    act.dma_start(rows[0, hs, :], W[hs, 10 + 2 * d, :]).then_inc(rows_out, 16)
                    act.dma_start(rows[1, hs, :], W[hs, 14, :]).then_inc(rows_out, 16)
                    act.dma_start(rows[2, hs, :], W[hs, 2 + d, :]).then_inc(rows_out, 16)
                    act.dma_start(rows[3, hs, :], W[hs, 6 + d, :]).then_inc(rows_out, 16)
                    act.dma_start(rows[4, hs, :], W[hs, 8 + d, :]).then_inc(rows_out, 16)
                    act.dma_start(io["new_m"][l, d, :, :], mout[hs, d:d + 1]).then_inc(rows_out, 16)
                take(B, n0_, 2, xt(6))
                take(B, n0_, 3, xt(7))
                B.wait("pe", "columns4")
                B.link(A(tokc[:, :, :, :].rearrange("p k t h -> p (k t h)"), wb[:, 0:5 * TILES * 8], ACT.Copy))
                act.wait_ge(rows_out, (l + 1) * (12 * 16))
                B.did(act.nop())
                B.end()

                with act.Fori(0, H_A) as h:
                    B = s_gdn.body("act", act, l * H_A + h)
                    now = act.snap((l * H_A + h + 1) * 16)
                    n0_ = act.snap(l * STREAM_HALVES + h * 8 + (STREAM["gates"] + 8))
                    act.dma_start(state[:, 1, 0:P], io["state_gdn"][l, 0, h, :, :]).then_inc(state_in[0], 16)
                    for tile, kind in ((row_g[0], 0), (row_beta[0], 1)):
                        act.dma_start(tile, rows[kind, bass.ds(h, 1), :].partition_broadcast(P)).then_inc(rows_in[0], 16)
                    B.wait("dve", "zeros")
                    for i in range(3):
                        B.did(A(pads[i][:, 2:2 + CTX], xt(4 + i)[:, 0:CTX], ACT.Copy))
                        B.did(A(pads[i][:, 6 + CTX:6 + TOK], xt(4 + i)[:, CTX:TOK], ACT.Copy), f"{'qkv'[i]} padded")
                    for i in range(2):
                        B.wait("dve", f"{'qk'[i]} conv")
                        sigmoid(B, pads[i][:, 0:CONVW], convs[i], f"{'qk'[i]} sigmoid")
                    B.wait("dve", "q silu")
                    B.did(A(wt(9), wt(0), ACT.Square), "q squared")
                    B.wait("dve", "v conv")
                    sigmoid(B, pads[2][:, 0:CONVW], convs[2], "v sigmoid")
                    B.wait("dve", "k silu")
                    B.did(A(wt(11), wt(1), ACT.Square), "k squared")
                    B.wait("pe", "q sum")
                    rsqrt(B, wt(10), wa[:, 0:TOK], wt(10), 1.0, "q rstd", DK_SCALE)
                    B.wait("pe", "k sum")
                    rsqrt(B, wt(12), wb[:, 0:TOK], wt(12), 1.0, "k rstd")
                    for tile, kind in ((row_g[1], 0), (row_beta[1], 1)):
                        act.dma_start(tile, rows[kind, bass.ds(h + 4, 1), :].partition_broadcast(P)).then_inc(rows_in[1], 16)
                    sigmoid(B, xt(9), xt(7), "z sigmoid")
                    B.wait("pe", "k turned")
                    B.did(A(wt(2), wa[:, 0:TOK], ACT.Copy))
                    B.wait("pe", "v turned")
                    B.did(A(wt(3), wb[:, 0:TOK], ACT.Copy), "v turned taken")
                    B.wait("act", "v padded")
                    take(B, n0_, 0, xt(4))
                    take(B, n0_, 1, xt(5))
                    for d in range(2):
                        act.wait_ge(rows_in[d], (l * H_A + h + 1) * 32)
                        B.wait("dve", f"cols{d}")
                        B.did(A(wt(8), row_g[d], ACT.Exp), f"eg{d}")
                        B.did(A(colt[:, 2, :], colt[:, 0, :], ACT.Exp), f"eg col{d}")
                        B.did(A(colt[:, 5, :], colt[:, 4, :], ACT.Exp), f"kdec col{d}")
                        B.wait("dve", f"gap{d}")
                        B.did(A(wt(7), wt(7), ACT.Exp), f"decay{d}")
                        for v in range(1, LEVELS):
                            B.wait("pe", f"ld{d}{v}")
                            B.did(A(wt(13), wa[:, 0:TOK], ACT.Copy), f"ld taken{d}{v}")
                        B.wait("pe", f"wT{d}")
                        B.did(A(wt(12), wa[:, 0:TOK], ACT.Copy, scale=-1.0), f"wT taken{d}")
                        for n in range(TILES):
                            t = n if d == 0 or n == 0 else TILES - n
                            B.wait("pe", f"vnew{d}{n}")
                            B.did(A(T(wt(9), t), wa[:, 0:P], ACT.Copy), f"vnew taken{d}{n}")
                            if n == 0:
                                B.wait("dve", f"state{d}0")
                                act.dma_start(io["new_gdn"][l, d, h, :, :], state[:, 0, 0:P]).then_inc(state_out[d], 16)
                        if d == 1:
                            B.wait("dve", "z ready")
                        take(B, n0_, 2 + d, xt(6 + d))
                        if d == 0:
                            B.wait("dve", f"state0{TILES - 1}")
                            act.dma_start(state[:, 1, 0:P], io["state_gdn"][l, 1, h, :, :]).then_inc(state_in[1], 16)
                    B.wait("dve", "o whole")
                    B.did(A(wt(6), wt(4), ACT.Square), "o squared")
                    B.wait("pe", "o sum")
                    rsqrt(B, wt(7), wa[:, 0:TOK], wt(7), 1.0 / P, "o rstd")
                    for d in range(2):
                        act.wait_ge(state_out[d], now)
                    B.did(act.nop())
                    B.end()

                B = s_mli.body("act", act, l)
                B.wait("pe", "z")
                B.did(A(halves(xt(8)), pj[0][:, :, 0:HALF], ACT.Copy))
                B.end()
                with act.Fori(0, H_C) as h:
                    B = s_mls.body("act", act, l * H_C + h)
                    n0_ = act.snap(l * STREAM_HALVES + h * 10 + (STREAM["gates"] + STREAM["gdn"] + 10))
                    for d in range(1):
                        act.dma_start(state[:, 1, 0:P], io["state_c"][l, d, h, :, :]).then_inc(cstate_in[d], 16)
                        act.dma_start(n0[:, :], io["state_n"][l, d, h, :, :]).then_inc(cstate_in[d], 16)
                        for j in range(3):
                            act.dma_start(wt(5 + j), rows[2 + j, bass.ds(h + 4 * d, 1), :].partition_broadcast(P))\
                                .then_inc(crows_in[d], 16)
                    B.did(A(wt(1), xt(5), ACT.Copy), "k taken")
                    B.did(A(wt(2), xt(6), ACT.Copy), "v taken")
                    B.did(A(wt(0), xt(4), ACT.Copy, scale=DK_SCALE), "q taken")
                    B.wait("pe", "k turned")
                    B.did(A(wt(3), wa[:, 0:TOK], ACT.Copy), "k turned taken")
                    for d in range(2):
                        B.wait("dve", f"gap{d}")
                        B.did(A(wt(8), wt(8), ACT.Exp), f"decay{d}")
                        B.did(A(colt[:, 5, :], colt[:, 4, :], ACT.Exp), f"wk col{d}")
                        if d == 0:
                            sigmoid(B, wt(13), xt(7), "o sigmoid")
                            sigmoid(B, wt(15), xt(8), "z sigmoid")
                            B.wait("act", "q taken")
                            take(B, n0_, 0, xt(4))
                            take(B, n0_, 1, xt(5))
                        B.wait("dve", f"state{d}0")
                        act.dma_start(io["new_c"][l, d, h, :, :], state[:, 0, 0:P]).then_inc(cstate_out[d], 16)
                        act.dma_start(io["new_n"][l, d, h, :, :], state[:, 0, P:P + 1]).then_inc(cstate_out[d], 16)
                        if d == 0:
                            B.wait("dve", "hB ready")
                            act.dma_start(state[:, 1, 0:P], io["state_c"][l, 1, h, :, :]).then_inc(cstate_in[1], 16)
                            act.dma_start(n0[:, :], io["state_n"][l, 1, h, :, :]).then_inc(cstate_in[1], 16)
                            for j in range(3):
                                act.dma_start(wt(5 + j), rows[2 + j, bass.ds(h + 4, 1), :].partition_broadcast(P))\
                                    .then_inc(crows_in[1], 16)
                    B.wait("dve", "oz ready")
                    for j in range(2, 5):
                        take(B, n0_, j, xt(4 + j))
                    B.wait("dve", "h whole")
                    B.did(A(wt(6), wt(12), ACT.Square), "h squared")
                    B.wait("pe", "h sum")
                    rsqrt(B, wt(7), wa[:, 0:TOK], wt(7), 1.0 / P, "h rstd")
                    for d in range(2):
                        act.wait_ge(cstate_out[d], (l * H_C + h + 1) * 32)
                    B.did(act.nop())
                    B.end()

                B = s_min.body("act", act, l)
                act.dma_start(flat(15, 2 * P), io["cache_ckv"][l, :, :]).then_inc(cache_in, 16)
                kp = flat(8, KEYS)
                for a in range(2):
                    act.dma_start(kp[64 * a:64 * a + 64, TOK:KEYS], io["cache_kr"][l, :, :]).then_inc(cache_in, 16)
                for j in range(5):
                    B.did(A(wt(j), xt(4 + j), ACT.Copy), f"taken{j}")
                for j in range(5, 15):
                    B.wait("pe", f"tile{j}")
                    if j < 7:
                        B.did(A(halves(wt(j)), pj[j % 2][:, :, 0:HALF], ACT.Copy), f"taken{j}")
                    else:
                        if j >= 9:
                            B.wait("dve", f"zb{j - 2}")
                        e, x = wt(10 + 2 * (j % 2)), wt(11 + 2 * (j % 2))
                        B.link(A(halves(x), pj[j % 2][:, :, 0:HALF], ACT.Copy), f"taken{j}")
                        sigmoid(B, e, x, f"zb sigmoid{j}")
                act.dma_start(io["new_kr"][l, :, :], W[0:64, 6, 0:CTX]).then_inc(latent_out, 16)
                act.wait_ge(cache_in, (l + 1) * 48)
                B.wait("dve", "zb14")
                B.wait("dve", "cache split")
                for k in range(Q_TILES):
                    B.did(A(wt(10 + k), wt(k), ACT.Square), f"cq squared{k}")
                for k in range(KV_TILES):
                    B.did(A(wt(14 + k), wt(4 + k), ACT.Square), f"ckv squared{k}")
                B.wait("pe", f"cq sum{Q_TILES - 1}")
                rsqrt(B, wt(10), wa[:, 0:TOK], wt(10), 1.0 / (Q_TILES * P), "cq rstd", mid="cq logged")
                B.wait("pe", f"ckv sum{KV_TILES - 1}")
                rsqrt(B, wt(11), wb[:, 0:TOK], wt(11), 1.0 / (KV_TILES * P), "ckv rstd")
                B.wait("pe", "key pe")
                B.did(A(kp[:, 0:TOK], wa[:, 0:TOK], ACT.Copy), "key pe taken")
                B.wait("dve", "ckv normed")
                act.dma_start(io["new_ckv"][l, :, :, :], W[:, 4:6, 0:CTX]).then_inc(latent_out, 16)
                act.wait_ge(latent_out, (l + 1) * 32)
                B.did(act.nop())
                B.end()

                with act.Fori(0, H_B) as h:
                    B = s_mla.body("act", act, l * H_B + h)
                    B.wait("pe", "q nope")
                    B.did(A(halves(wt(0)), pj[0][:, :, 0:HALF], ACT.Copy), "q nope taken")
                    B.wait("pe", "k nope")
                    B.did(A(halves(flat(2, KEYS)), pj[0][:, :, 0:KEYS // 2], ACT.Copy), "k nope taken")
                    B.wait("pe", "v")
                    B.did(A(halves(flat(4, KEYS)), pj[1][:, :, 0:KEYS // 2], ACT.Copy), "v taken")
                    for m in range(TILES + 1):
                        if m < TILES:
                            t = MLA_ORDER[m]
                            nk = P if t == 0 else TOK
                            B.wait("dve", f"max{m}")
                            if m >= 2:
                                B.wait("pe", f"turned{m - 2}")
                            B.did(A(W[:, 6 + 4 * (m % 2), 0:nk], MLA_SCORES[m % 2][:, 0:nk], ACT.Exp,
                                    bias=mxs[:, 1, t:t + 1], scale=SM_SCALE, accum_out=mxs[:, 2, t:t + 1]), f"exp{m}")
                        if m >= 1:
                            t = MLA_ORDER[m - 1]
                            nk = P if t == 0 else TOK
                            B.wait("pe", f"turned{m - 1}")
                            if m >= 3:
                                B.wait("pe", f"o{m - 3}")
                            B.did(A(W[:, 7 + 4 * ((m - 1) % 2), 0:nk], MLA_PS[(m - 1) % 2][:, 0:nk], ACT.Copy),
                                  f"turned taken{m - 1}")
                    B.end()

                B = s_spl.body("act", act, l)
                for k in range(H_B):
                    B.did(A(h_hi[:, k, :], xo[:, H_A + k, :], ACT.Copy), f"hi{k}")
                B.end()
                with act.Fori(0, KT // 2) as f:
                    B = s_out.body("act", act, l * (KT // 2) + f)
                    for j, name in enumerate(("first", "second")):
                        B.wait("pe", name)
                        B.did(A(halves(wt(j)), pj[j][:, :, 0:HALF], ACT.Square), f"square{j}")
                    B.end()

                B = s_res.body("act", act, l)
                for k in range(4):
                    act.dma_start(wt(10 + k), x_kept[:, k, :]).then_inc(x_back[k], 16)
                B.wait("pe", "sum")
                rsqrt(B, halves(wt(5)), pj[0][:, :, 0:HALF], halves(wt(4)), 1.0 / D_MODEL, "rstd")
                for k in range(4, KT):
                    B.wait("dve", f"added{k - 4}")
                    act.dma_start(wt(10 + k % 4), x_kept[:, k, :]).then_inc(x_back[k % 4], 16)
                B.end()
            act.dma_start(io["y"], xo[:, :, :]).then_inc(y_out, 16)
            act.wait_ge(y_out, 16)

        @block.vector
        def _(dve):
            V = nc.vector
            tt, ts, stt = V.tensor_tensor, V.tensor_scalar, V.scalar_tensor_tensor

            def sigmoid_from_exp(B, ap, label=None):
                B.link(ts(ap, ap, 1.0, None, ALU.add))
                B.link(V.reciprocal(ap, ap), label)

            B = s_init.body("dve", dve, None)
            B.did(V.memset(cst[:, 0:1], EPS))
            B.did(V.memset(cst[:, 1:2], math.log(DK_SCALE)), "eps")
            dve.wait_ge(const_in, 48)
            B.wait("act", "cond exp")
            sigmoid_from_exp(B, cond[:, :, :])
            B.link(tt(cond[:, :, :], cond[:, :, :], cond_t[:, :, :], ALU.mult))
            B.end()
            with dve.Fori(0, DEPTH) as l:
                dve.wait_ge(params_in, (l + 1) * 16)
                dve.sem_inc(s_init.passed, 1)
                def par(name, n):
                    return prm[:, PRM[name]:PRM[name] + n]

                N = s_norm.body("dve", dve, l)
                N.wait("act", "square1")
                N.link(tt(wt(8), wt(0), wt(1), ALU.add), "squares1")
                for k in range(2, KT):
                    N.wait("act", f"square{k}")
                    N.link(tt(wt(8), wt(8), wt(k % 4), ALU.add), f"squares{k}")

                def ada_turn(i):
                    B = s_ada.body("dve", dve, l * ADA_PAIRS + i)
                    b = PRM["b_ada"]
                    used = dve.snap(l * per_layer + i * (2 * KT // RAW_SLOTS) + 1)
                    for j in range(2):
                        dve.wait_ge(raw_free[RAW_SLOTS - 1], used + (j + 1) * (KT // RAW_SLOTS))
                        B.did(V.tensor_copy(flat(13 + 2 * j, ADA_COLS)[0:2, :], (wa, wb)[j][0:2, :]), f"rows{j}")
                        B.wait("pe", f"turned{j}")
                        at = (2 * i + j) * ADA_TILES
                        B.did(tt(mod[:, bass.ds(at, ADA_TILES), :],
                                 pj[0][:, 0, j * 2 * ADA_TILES:(j + 1) * 2 * ADA_TILES].rearrange("p (a b) -> p a b", b=2),
                                 prm[:, bass.ds(at + b, ADA_TILES)].unsqueeze(2).to_broadcast([P, ADA_TILES, 2]), ALU.add))
                    B.end()

                per_layer = (ADA_HALVES + STREAM_HALVES) // RAW_SLOTS
                dve.sem_inc(s_norm.passed, 1)
                with dve.Fori(0, ADA_PAIRS - 1) as i:
                    ada_turn(i)
                dve.wait_ge(x_saved, (l + 1) * 16)
                N.wait("act", "rstd")
                for k in range(KT):
                    N.did(tt(xo[:, k, :], xo[:, k, :], wt(5), ALU.mult), f"scaled{k}")
                ada_turn(ADA_PAIRS - 1)

                N.link(stt(mul[:, :, :], mod[:, KT:2 * KT, :], 1.0,
                           par("g_pre", KT).unsqueeze(2).to_broadcast([P, KT, 2]), ALU.add, ALU.mult))
                for k in range(KT + 1):
                    if k < KT:
                        u = wt(6 + k % 4)
                        N.did(ts(u[:, 0:CTX], xo[:, k, 0:CTX], mul[:, k, 0:1], mod[:, k, 0:1], ALU.mult, ALU.add))
                        N.link(ts(u[:, CTX:TOK], xo[:, k, CTX:TOK], mul[:, k, 1:2], mod[:, k, 1:2], ALU.mult, ALU.add),
                               f"u{k}")
                    if k:
                        N.wait("act", f"hi{k - 1}")
                        N.did(tt(h_lo[:, k - 1, :], wt(6 + (k - 1) % 4), h_hi[:, k - 1, :].bitcast(F32), ALU.subtract),
                              f"h{k - 1}")
                N.end()

                B = s_gate.body("dve", dve, l)
                resF, resB = W[0:8, 6:8, :], W[0:8, 8:10, :]
                B.did(V.memset(resF, 1.0))
                B.link(V.memset(resB, 1.0))
                B.did(V.memset(resF.rearrange("p a (t c) -> p (a t) c", c=P)[:, :, 0:1], 0.0))
                B.link(V.memset(resB.rearrange("p a (t c) -> p (a t) c", c=P)[:, :, P - 1:P], 0.0))
                B.wait("act", "exp a_log")
                B.link(ts(colt[0:8, 1, 0:1], colt[0:8, 0, 0:1], -1.0, None, ALU.mult))
                B.wait("act", "beta exp")
                sigmoid_from_exp(B, W[0:8, 14, :], "beta")
                B.wait("act", "log")
                B.link(stt(W[0:8, 4:6, :], W[0:8, 0:2, :], 0.0, W[0:8, 2:4, :], ALU.max, ALU.add))
                B.did(ts(W[0:8, 4, :], W[0:8, 4, :], colt[0:8, 1, 0:1], None, ALU.mult))
                B.link(ts(W[0:8, 5, :], W[0:8, 5, :], -1.0, None, ALU.mult))

                def fl(a):
                    return W[0:8, a:a + 2, :].rearrange("p a n -> p (a n)")
                B.did(V.tensor_tensor_scan(fl(10), fl(6), fl(4), 0.0, ALU.mult, ALU.add))
                B.link(V.tensor_tensor_scan(fl(12)[:, ::-1], fl(8)[:, ::-1], fl(4)[:, ::-1], 0.0,
                                            ALU.mult, ALU.add), "cum")
                B.did(tt(W[0:8, 0, :], W[0:8, 15, :], W[0:8, 11, :], ALU.subtract), "aF")
                B.did(tt(W[0:8, 1, :], W[0:8, 15, :], W[0:8, 13, :], ALU.subtract), "aB")
                B.link(V.memset(W[0:8, 4:6, :], 0.0))
                d0F, d0B = W[0:8, 4, :], W[0:8, 5, :]
                B.did(V.tensor_copy(tiled(d0F)[:, 2:5, 0:1], tiled(W[0:8, 11, :])[:, 1:4, P - 1:P]))
                B.link(V.tensor_copy(tiled(d0B)[:, 1:4, P - 1:P], tiled(W[0:8, 13, :])[:, 2:5, 0:1]))
                dve.wait_ge(m0_in, (l + 1) * 16)
                MF, MB = W[0:8, 2, :], W[0:8, 3, :]
                scan = V.tensor_tensor_scan
                B.did(scan(MF[:, 0:CTX], d0F[:, 0:CTX], W[0:8, 0, 0:CTX], 0.0, ALU.add, ALU.max))
                B.did(scan(MF[:, CTX:TOK], d0F[:, CTX:TOK], W[0:8, 0, CTX:TOK], m0[:, 0:1], ALU.add, ALU.max))
                B.did(scan(MB[:, 0:CTX][:, ::-1], d0B[:, 0:CTX][:, ::-1], W[0:8, 1, 0:CTX][:, ::-1], 0.0,
                           ALU.add, ALU.max))
                B.link(scan(MB[:, CTX:TOK][:, ::-1], d0B[:, CTX:TOK][:, ::-1], W[0:8, 1, CTX:TOK][:, ::-1],
                            m0[:, 0:1], ALU.add, ALU.max))
                B.did(V.memset(mprev[:, :, 0:1], 0.0))
                B.did(V.tensor_copy(mprev[:, 0, 1:2], m0[:, :]))
                B.did(V.tensor_copy(mprev[:, 1, 4:5], m0[:, :]))
                B.did(tt(mprev[:, 0, 2:5].unsqueeze(2), tiled(MF)[:, 1:4, P - 1:P],
                         tiled(W[0:8, 11, :])[:, 1:4, P - 1:P], ALU.add))
                B.did(tt(mprev[:, 1, 1:4].unsqueeze(2), tiled(MB)[:, 2:5, 0:1],
                         tiled(W[0:8, 13, :])[:, 2:5, 0:1], ALU.add))
                B.did(tt(mout[:, 0:1], MF[:, P - 1:P], W[0:8, 11, P - 1:P], ALU.add))
                B.link(tt(mout[:, 1:2], MB[:, 0:1], W[0:8, 13, 0:1], ALU.add))
                for d, M in ((0, MF), (1, MB)):
                    B.did(tt(tiled(W[0:8, 6 + d, :]), mprev[:, d, :].unsqueeze(2).to_broadcast([8, TILES, P]),
                             tiled(M), ALU.subtract), "wi")
                for d, M in ((0, MF), (1, MB)):
                    B.did(tt(W[0:8, 8 + d, :], M, W[0:8, 11 + 2 * d, :], ALU.add), "em")
                B.end()

                with dve.Fori(0, H_A) as h:
                    B = s_gdn.body("dve", dve, l * H_A + h)
                    for pad in pads:
                        B.did(V.memset(pad[:, 0:2], 0.0))
                        B.did(V.memset(pad[:, 2 + CTX:6 + CTX], 0.0))
                        B.did(V.memset(pad[:, 6 + TOK:8 + TOK], 0.0), "zeros")
                    cw = PRM["conv"]
                    for i in range(3):
                        B.link(ts(hcw[:, i, :], prm[:, bass.ds(h * CONV_K + (cw + i * H_A * CONV_K), CONV_K)],
                                  1.0, None, ALU.mult))

                    def conv(i):
                        x, cv = "qkv"[i], convs[i]
                        B.wait("act", f"{x} padded")
                        B.link(ts(cv, pads[i][:, 0:CONVW], hcw[:, i, 0:1], None, ALU.mult))
                        for j in range(1, CONV_K):
                            B.link(stt(cv, pads[i][:, j:j + CONVW], hcw[:, i, j:j + 1], cv, ALU.mult, ALU.add),
                                   f"{x} conv" if j == CONV_K - 1 else None)

                    def silu(i, y):
                        x, cv = "qkv"[i], convs[i]
                        B.wait("act", f"{x} sigmoid")
                        B.did(tt(y[:, 0:CTX], cv[:, 0:CTX], pads[i][:, 0:CTX], ALU.mult))
                        B.link(tt(y[:, CTX:TOK], cv[:, CTX + 4:CONVW], pads[i][:, CTX + 4:CONVW], ALU.mult), f"{x} silu")

                    conv(0)
                    conv(1)
                    silu(0, wt(0))
                    conv(2)
                    silu(1, wt(1))
                    silu(2, wt(4))
                    B.wait("act", "q rstd")
                    B.did(tt(wt(0), wt(0), wt(10), ALU.mult), "q normed")
                    B.wait("act", "k rstd")
                    B.link(tt(wt(1), wt(1), wt(12), ALU.mult), "k normed")
                    B.wait("act", "z sigmoid")
                    B.link(tt(xt(8), xt(7), xt(9), ALU.mult), "z ready")
                    B.wait("act", "v turned taken")
                    for d in range(2):
                        dve.wait_ge(rows_in[d], (l * H_A + h + 1) * 32)
                        last_at = P - 1 if d == 0 else 0
                        B.did(ts(colt[:, 0, :], tokc[:, d, :, bass.ds(h + 4 * d, 1)].rearrange("p t o -> p (t o)"), 1.0, None, ALU.mult))
                        B.link(ts(colt[:, 1, :], tokc[:, 2, :, bass.ds(h + 4 * d, 1)].rearrange("p t o -> p (t o)"), 1.0, None, ALU.mult))
                        B.link(tt(colt[:, 4, :].unsqueeze(2), tiled(row_g[d])[:, :, last_at:last_at + 1],
                                  colt[:, 0, :].unsqueeze(2), ALU.subtract), f"cols{d}")
                        B.did(tt(wt(14), wt(1), row_beta[d], ALU.mult), f"kb{d}")
                        B.link(tt(tiled(wt(7)), tiled(row_g[d]), over_cols(colt[:, 0, :]), ALU.subtract))
                        B.link(tt(tiled(wt(7)), tiled(wt(7)), over_tiles(neg(d)), ALU.add), f"gap{d}")
                        B.wait("act", f"decay{d}")
                        B.wait("pe", f"kk{d}")
                        B.link(tt(wt(9), wa[:, 0:TOK], wt(7), ALU.mult))
                        D, DT = wt(10), wt(11)

                        def blocks(v, label=None):
                            B.link(tt(tiled(lvt[v % 2]), tiled(wt(9)), over_tiles(lvl[:, d, v, :]), ALU.mult), label)
                        blocks(0, f"level{d}0")
                        B.wait("pe", f"qk{d}")
                        B.did(tt(wt(16), wb[:, 0:TOK], wt(7), ALU.mult))
                        B.link(tt(tiled(DT), over_tiles(ident), tiled(lvt[0]), ALU.subtract))
                        blocks(1)
                        B.wait("pe", f"ld{d}0")
                        B.link(tt(tiled(D), over_tiles(ident), tiled(wa[:, 0:TOK]), ALU.subtract), f"level{d}1")
                        for v in range(1, LEVELS):
                            if v < LEVELS - 1:
                                blocks(v + 1)
                                B.wait("pe", f"dld{d}{v}")
                                B.did(tt(D, D, wb[:, 0:TOK], ALU.subtract))
                            B.wait("pe", f"dldT{d}{v}")
                            B.link(tt(DT, DT, wa[:, 0:TOK], ALU.subtract),
                                   f"inverse{d}" if v == LEVELS - 1 else f"level{d}{v + 1}")
                        B.wait("act", f"kdec col{d}")
                        B.link(tt(colt[:, 3, :], colt[:, 1, :], colt[:, 2, :], ALU.mult))
                        B.did(tt(tiled(wt(14)), tiled(wt(3)), over_cols(colt[:, 1, :]), ALU.mult))
                        B.did(tt(tiled(wt(15)), tiled(wt(2)), over_cols(colt[:, 3, :]), ALU.mult), f"kbg{d}")
                        B.wait("act", f"wT taken{d}")
                        B.did(tt(wt(13), wt(0), wt(8), ALU.mult))
                        B.did(tt(tiled(wt(10)), tiled(wt(2)), over_cols(colt[:, 5, :]), ALU.mult), f"kdec{d}")
                        for n in range(TILES):
                            t = n if d == 0 or n == 0 else TILES - n
                            B.wait("pe", f"kv{d}{n}")
                            if n == 0:
                                B.link(V.tensor_copy(state[:, 0, 0:P], wb[:, 0:P]), f"state{d}0")
                            else:
                                e = t * P + last_at
                                B.link(stt(state[:, 1, 0:P], state[:, 1, 0:P], W[:, 8, e:e + 1], wb[:, 0:P],
                                           ALU.mult, ALU.add), f"state{d}{n}")
                            if d == 0:
                                B.link(V.tensor_copy(T(wt(4), t), wa[:, 512:512 + P]), f"o taken{d}{n}")
                            else:
                                B.link(tt(T(wt(4), t), T(wt(4), t), wa[:, 512:512 + P], ALU.add), f"o taken{d}{n}")
                        if d == 0:
                            dve.wait_ge(state_out[0], (l * H_A + h + 1) * 16)
                    B.did(V.memset(cst[:, 2:3], 0.0), "o whole")
                    B.wait("act", "o rstd")
                    B.link(stt(wt(4), wt(4), par("gdn_norm", 1), wt(7), ALU.mult, ALU.mult))
                    B.did(tt(xo[:, bass.ds(h, 1), :].rearrange("p a n -> p (a n)"), wt(4), xt(8), ALU.mult))
                    B.end()

                with dve.Fori(0, H_C) as h:
                    B = s_mls.body("dve", dve, l * H_C + h)
                    B.wait("pe", "v turned")
                    B.did(V.tensor_copy(wt(4), wb[:, 0:TOK]), "v turned taken")
                    for d in range(2):
                        last_at = P - 1 if d == 0 else 0
                        dve.wait_ge(crows_in[d], (l * H_C + h + 1) * 48)
                        dve.wait_ge(cstate_in[d], (l * H_C + h + 1) * 32)
                        B.did(ts(state[:, 1, P:2 * P], ones, n0[:, 0:1], None, ALU.mult), f"n rep{d}")
                        B.link(ts(colt[:, 0, :], tokc[:, 3 + d, :, bass.ds(h + 4 * d, 1)].rearrange("p t o -> p (t o)"), 1.0, None, ALU.mult))
                        B.did(tt(colt[:, 4, :].unsqueeze(2), colt[:, 0, :].unsqueeze(2),
                                 tiled(wt(5))[:, :, last_at:last_at + 1], ALU.subtract))
                        B.link(tt(tiled(wt(8)), over_cols(colt[:, 0, :]), tiled(wt(5)), ALU.subtract))
                        B.link(tt(tiled(wt(8)), tiled(wt(8)), over_tiles(neg(d)), ALU.add), f"gap{d}")
                        B.wait("act", "q taken")
                        B.did(tt(wt(10), wt(0), wt(6), ALU.mult))
                        B.wait("act", f"wk col{d}")
                        B.did(tt(tiled(wt(11)), tiled(wt(3)), over_cols(colt[:, 5, :]), ALU.mult))
                        B.wait("pe", f"qk{d}")
                        B.link(tt(wt(9), wa[:, 0:TOK], wt(8), ALU.mult), f"s{d}")
                        for n in range(TILES):
                            t = n if d == 0 or n == 0 else TILES - n
                            B.wait("pe", f"kv{d}{n}")
                            if n == 0:
                                B.link(V.tensor_copy(state[:, 0, :], wb[:, 0:2 * P]), f"state{d}0")
                            else:
                                e = t * P + last_at
                                B.link(stt(state[:, 1, :], state[:, 1, :], W[:, 6, e:e + 1], wb[:, 0:2 * P],
                                           ALU.mult, ALU.add), f"state{d}{n}")
                            q = W[:, 16, 0:P]
                            B.link(stt(q, wa[:, 512:512 + P], -1.0, T(wt(7), t), ALU.mult, ALU.max))
                            B.link(tt(q, q, wa[:, 512:512 + P], ALU.max))
                            B.link(V.reciprocal(q, q))
                            if d == 0:
                                B.link(tt(T(wt(12), t), wa[:, 0:P], q, ALU.mult), f"h taken{d}{n}")
                            else:
                                B.link(tt(q, wa[:, 0:P], q, ALU.mult), f"h taken{d}{n}")
                                B.link(tt(T(wt(12), t), T(wt(12), t), q, ALU.add))
                        if d == 0:
                            dve.wait_ge(cstate_out[0], (l * H_C + h + 1) * 32)
                            B.did(V.memset(cst[:, 2:3], 0.0), "hB ready")
                            B.wait("act", "z sigmoid")
                            B.link(tt(wt(14), xt(8), wt(15), ALU.mult), "oz ready")
                            B.did(tt(wt(14), wt(14), wt(13), ALU.mult))
                    B.did(V.memset(cst[:, 2:3], 0.0), "h whole")
                    B.wait("act", "h rstd")
                    B.link(stt(wt(12), wt(12), par("mlstm_norm", 1), wt(7), ALU.mult, ALU.mult))
                    B.did(tt(xo[:, bass.ds(h + (H_A + H_B), 1), :].rearrange("p a n -> p (a n)"), wt(12), wt(14), ALU.mult))
                    B.end()

                B = s_min.body("dve", dve, l)
                kvh = h_hi[:, 4:7, :].rearrange("p a n -> p (a n)")
                kvl = h_lo[:, 4:7, :].rearrange("p a n -> p (a n)")
                for j in range(7, 15):
                    e, x = wt(10 + 2 * (j % 2)), wt(11 + 2 * (j % 2))
                    B.wait("act", f"zb sigmoid{j}")
                    B.did(tt(xo[:, H_A + j - 7, :], x, e, ALU.mult), f"zb{j}")
                B.wait("pe", "tile14")
                dve.wait_ge(cache_in, (l + 1) * 48)
                for k in range(KV_TILES):
                    s = slice(k * KEYS + TOK, (k + 1) * KEYS)
                    c = flat(15, 2 * P)[:, k * P:(k + 1) * P]
                    B.link(V.tensor_copy(kvh[:, s], c))
                    B.did(tt(kvl[:, s], c, kvh[:, s].bitcast(F32), ALU.subtract), "cache split")
                B.link(tt(wt(7), wt(6), con[:, C_ROPE:C_ROPE + TOK], ALU.mult), "roped")
                B.wait("act", "cq rstd")
                for k in range(Q_TILES):
                    B.link(stt(wt(k), wt(k), par("q_norm", 4)[:, k:k + 1], wt(10), ALU.mult, ALU.mult))
                    B.link(V.tensor_copy(h_hi[:, k, :], wt(k)))
                    B.did(tt(h_lo[:, k, :], wt(k), h_hi[:, k, :].bitcast(F32), ALU.subtract))
                B.wait("act", "ckv rstd")
                for k in range(KV_TILES):
                    B.link(stt(wt(4 + k), wt(4 + k), par("kv_norm", 2)[:, k:k + 1], wt(11), ALU.mult, ALU.mult),
                           "ckv normed")
                for k in range(KV_TILES):
                    s = slice(k * KEYS, k * KEYS + TOK)
                    B.link(V.tensor_copy(kvh[:, s], wt(4 + k)))
                    B.did(tt(kvl[:, s], wt(4 + k), kvh[:, s].bitcast(F32), ALU.subtract))
                B.end()

                with dve.Fori(0, H_B) as h:
                    B = s_mla.body("dve", dve, l * H_B + h)
                    for m in range(2):
                        src = xo[:, 12 * m:12 * m + 4, bass.ds(h * STRIP, STRIP)]
                        hi, lo = (x[:, 8 + 4 * m:12 + 4 * m, bass.ds(h * STRIP, STRIP)] for x in (h_hi, h_lo))
                        B.link(ts(hi, src, 1.0, None, ALU.mult))
                        B.did(tt(lo, src, hi.bitcast(F32), ALU.subtract))
                    B.wait("pe", "q pe")
                    B.did(tt(halves(wt(1)), pj[1][:, :, 0:HALF], halves(con[:, C_ROPE:C_ROPE + TOK]), ALU.mult), "q pe roped")

                    def taken(m):
                        t = MLA_ORDER[m]
                        B.wait("pe", f"o{m}")
                        o = xo[:, bass.ds(h + H_A, 1), t * P:(t + 1) * P].rearrange("p a n -> p (a n)")
                        B.did(tt(o, o, MLA_PS[m % 2][:, 768:768 + P], ALU.mult), f"o taken{m}")

                    for m in range(TILES):
                        t = MLA_ORDER[m]
                        nk = P if t == 0 else TOK
                        B.wait("pe", f"scores{m}")
                        B.link(V.reduce_max(mxs[:, 0, t:t + 1], MLA_SCORES[m % 2][:, 0:nk], AX))
                        B.link(ts(mxs[:, 1, t:t + 1], mxs[:, 0, t:t + 1], -SM_SCALE, None, ALU.mult), f"max{m}")
                        if m >= 2:
                            taken(m - 2)
                        B.wait("act", f"exp{m}")
                        B.link(V.reciprocal(mxs[:, 3, t:t + 1], mxs[:, 2, t:t + 1]))
                        p = W[:, 6 + 4 * (m % 2), 0:nk]
                        B.link(ts(p, p, mxs[:, 3, t:t + 1], None, ALU.mult), f"normed{m}")
                    taken(TILES - 2)
                    taken(TILES - 1)
                    B.end()

                B = s_spl.body("dve", dve, l)
                B.did(V.memset(wt(8), 0.0))
                for k in range(H_B):
                    B.wait("act", f"hi{k}")
                    B.did(tt(h_lo[:, k, :], xo[:, H_A + k, :], h_hi[:, k, :].bitcast(F32), ALU.subtract))
                B.end()
                with dve.Fori(0, KT // 2) as f:
                    B = s_out.body("dve", dve, l * (KT // 2) + f)
                    for j in range(2):
                        B.wait("act", f"square{j}")
                        B.did(ts(xo[:, bass.ds(2 * f + j, 1), :].rearrange("p a (b n) -> p (a b) n", b=2),
                                 pj[j][:, :, 0:HALF], 1.0, None, ALU.mult))
                        B.link(tt(wt(8), wt(8), wt(j), ALU.add))
                    B.end()

                B = s_res.body("dve", dve, l)
                B.link(tt(mul[:, :, :], mod[:, 2 * KT:3 * KT, :],
                          par("g_post", KT).unsqueeze(2).to_broadcast([P, KT, 2]), ALU.mult))
                B.wait("act", "rstd")
                for k in range(KT):
                    u, x = wt(6 + k % 2), wt(10 + k % 4)
                    B.link(tt(u, xo[:, k, :], wt(5), ALU.mult))
                    dve.wait_ge(x_back[k % 4], (l * (KT // 4) + (k // 4 + 1)) * 16)
                    B.did(stt(xo[:, k, 0:CTX], u[:, 0:CTX], mul[:, k, 0:1], x[:, 0:CTX], ALU.mult, ALU.add))
                    B.did(stt(xo[:, k, CTX:TOK], u[:, CTX:TOK], mul[:, k, 1:2], x[:, CTX:TOK], ALU.mult, ALU.add),
                          f"added{k}")
                B.end()


def column_tiles(w, picks):
    depth, rows_, _ = w.shape
    w = np.concatenate([w, np.zeros((depth, rows_, 1), w.dtype)], axis=2)
    w = w[:, :, np.concatenate(picks)]
    w = w.reshape(depth, rows_ // (CELLS * P), CELLS, P, len(picks), P)
    return w.transpose(0, 4, 1, 3, 2, 5).reshape(depth, -1, P, CELLS * P)


def small_cells(w, picks):
    depth, rows_, _ = w.shape
    w = w[:, :, np.concatenate(picks)].reshape(depth, rows_ // P, P, len(picks) // 2, 2, P)
    w = w.transpose(0, 3, 2, 1, 4, 5).reshape(depth, len(picks) // 2, P, -1)
    fill = np.zeros(w.shape[:3] + (CELLS * P - w.shape[3],), w.dtype)
    return np.concatenate([w, fill], axis=3)


def swapped(first):
    at = np.arange(64)
    return np.concatenate([first + at, first + (at // 32) * 32 + (at % 32 + 16) % 32])


def constants():
    con = np.zeros((P, C_WIDTH), np.float32)
    j, i = np.arange(P)[:, None], np.arange(P)[None, :]
    con[:, C_ID:C_ID + P] = np.eye(P)
    con[:, C_ONE:C_ONE + P] = 1
    con[:, C_NEG:C_NEG + P] = np.where(i >= j, 0, NEG)
    con[:, C_NEG + P:C_NEG + 2 * P] = np.where(i <= j, 0, NEG)
    con[:, C_FOLD:C_FOLD + P] = i % 64 == j % 64
    inv = np.float32(10000.0) ** (-np.arange(0, 32, 2, dtype=np.float32) / np.float32(32))
    at = np.arange(LAT)
    angle = np.concatenate([(at // 64).astype(np.float32)[None] * np.tile(inv, 2)[:, None],
                            (at % 64).astype(np.float32)[None] * np.tile(inv, 2)[:, None]])
    sign = np.where(np.arange(64) % 32 < 16, -1, 1)[:, None]
    con[:64, C_ROPE:C_ROPE + CTX] = 1
    con[:64, C_ROPE + CTX:] = np.cos(angle)
    con[64:, C_ROPE + CTX:] = np.sin(angle) * sign
    lvl = np.zeros((P, 2, LEVELS, P), np.float32)
    for v in range(LEVELS):
        b = 1 << v
        pair = i // (2 * b) == j // (2 * b)
        lvl[:, 0, v] = pair & (i // b % 2 == 1) & (j // b % 2 == 0)
        lvl[:, 1, v] = pair & (i // b % 2 == 0) & (j // b % 2 == 1)
    return con, lvl.astype(np.float16)


def features_first(x):
    return x.T.reshape(-1, P, x.shape[0]).transpose(1, 0, 2)


def kernel(x_prompt, x_sample, cache_mla_ckv, cache_mla_krope, state_gdn, state_mlstm_c,
           state_mlstm_n, state_mlstm_m, c, c_ctx, w_ada, b_ada, g_pre, g_post, w_in,
           gdn_conv, gdn_a_log, gdn_dt_bias, gdn_norm, mla_q_norm, mla_kv_norm,
           mla_w_uq, mla_w_ukv, mlstm_b_i, mlstm_b_f, mlstm_norm, w_out):
    import concourse.bacc as bacc
    from concourse.bass_utils import run_bass_kernel_spmd

    con, lvl = constants()
    L = DEPTH

    def cols(a, n):
        return a.reshape(L, n, P).transpose(0, 2, 1)

    at = np.cumsum([0, 512, 512, 512, 512, 8, 8, 512, 256, 64, 1024, 512, 512, 512, 512, 512, 8, 8])
    qa, ka, va, za, ga, ba, cq, ckv, kr, zb, qc, kc, vc, oc, zc, ic, fc = at[:17]

    def tile(first, n=0):
        return first + n * P + np.arange(P)
    gates = np.full(P, -1)
    for quadrant, first in enumerate((ga, ba, ic, fc)):
        gates[32 * quadrant:32 * quadrant + 8] = first + np.arange(8)
    picks = [gates]
    for h in range(H_A):
        picks += [tile(x, h) for x in (qa, ka, va, za)]
    for h in range(H_C):
        picks += [tile(x, h) for x in (qc, kc, vc, oc, zc)]
    picks += [tile(cq, n) for n in range(4)] + [tile(ckv, n) for n in range(2)] + [swapped(kr)]
    picks += [tile(zb, n) for n in range(8)]
    uq = small_cells(mla_w_uq, sum([[h * 192 + np.arange(P), swapped(h * 192 + P)] for h in range(H_B)], []))
    ukv = small_cells(mla_w_ukv, sum([[h * 256 + np.arange(P), h * 256 + P + np.arange(P)] for h in range(H_B)], []))
    heads = np.stack([uq, ukv], axis=2).reshape(L, 2 * H_B, P, CELLS * P)
    rows_ = np.concatenate([tile(0, n) for n in list(range(4, 12)) + list(range(4)) + list(range(12, 16))])
    stream = np.concatenate([column_tiles(w_in, picks), heads,
                             column_tiles(w_out[:, rows_], [tile(0, f) for f in range(KT)])], axis=1)
    params = np.zeros((L, P, PRM_WIDTH), np.float32)

    def put(name, a):
        params[:, :a.shape[1], PRM[name]:PRM[name] + a.shape[2]] = a
    put("b_ada", cols(b_ada, 48))
    put("g_pre", cols(g_pre, KT))
    put("g_post", cols(g_post, KT))
    put("conv", gdn_conv.reshape(L, CONV_K, 12, P).transpose(0, 3, 2, 1).reshape(L, P, 12 * CONV_K))
    put("gdn_norm", gdn_norm[:, :, None])
    put("q_norm", cols(mla_q_norm, 4))
    put("kv_norm", cols(mla_kv_norm, 2))
    put("mlstm_norm", mlstm_norm[:, :, None])
    put("gates", np.stack([a.reshape(L, 8) for a in (gdn_a_log, gdn_dt_bias, mlstm_b_i, mlstm_b_f)], axis=2))

    arrays = {
        "constants": con, "levels": lvl, "params": params,
        "x": features_first(np.concatenate([x_prompt[0], x_sample[0]], axis=0)),
        "cond": np.stack([c_ctx.reshape(KT, P).T, c[0].reshape(KT, P).T], axis=2),
        "w_ada": w_ada.reshape(L, KT, P, ADA_GROUPS, ADA_COLS).transpose(0, 3, 1, 2, 4).reshape(L, ADA_HALVES, P, ADA_COLS),
        "w_stream": stream,
        "state_gdn": state_gdn[0], "state_c": state_mlstm_c[0], "state_n": state_mlstm_n[0][..., None],
        "m0": state_mlstm_m[0].reshape(L, 8, 1),
        "cache_ckv": cache_mla_ckv[0].transpose(0, 2, 1).reshape(L, 2, P, PAST).transpose(0, 2, 1, 3).reshape(L, P, 2 * PAST),
        "cache_kr": cache_mla_krope[0].transpose(0, 2, 1),
    }
    arrays = {n: np.ascontiguousarray(a) for n, a in arrays.items()}
    outs = {"y": (P, KT, TOK), "new_ckv": (L, P, 2, CTX), "new_kr": (L, 64, CTX),
            "new_gdn": (L, 2, H_A, P, P), "new_c": (L, 2, H_C, P, P), "new_n": (L, 2, H_C, P, 1),
            "new_m": (L, 2, H_C, 1)}

    book = {}
    for _ in range(2):
        nc = bacc.Bacc("TRN2", target_bir_lowering=False, num_devices=1)
        io = {n: nc.dram_tensor(f"in_{n}", a.shape, F16 if n == "levels" else F32, kind="ExternalInput").ap()
              for n, a in arrays.items()}
        io.update({n: nc.dram_tensor(f"out_{n}", s, F32, kind="ExternalOutput").ap() for n, s in outs.items()})
        build(nc, io, book)
    r = run_bass_kernel_spmd(nc, [{f"in_{n}": a for n, a in arrays.items()}], core_ids=[0])
    got = {n: r.results[0][f"out_{n}"] for n in outs}
    y = got["y"].transpose(2, 1, 0).reshape(TOK, D_MODEL)
    return (y[None, :CTX], y[None, CTX:],
            got["new_ckv"].transpose(0, 3, 2, 1).reshape(1, L, CTX, 2 * P),
            got["new_kr"].transpose(0, 2, 1)[None],
            got["new_gdn"][None], got["new_c"][None], got["new_n"][None, ..., 0], got["new_m"][None, ..., 0])
```

```python
import math
from contextlib import ExitStack

import numpy as np
import concourse.bass as bass
from concourse import mybir

F32 = mybir.dt.float32
F32R = mybir.dt.float32r
F16 = mybir.dt.float16
ACT = mybir.ActivationFunctionType
ALU = mybir.AluOpType
AX = mybir.AxisListType.X

P = 128
DEPTH, D_MODEL, CTX, LAT = 2, 2048, 128, 512
TOK = CTX + LAT
TILES = TOK // P
STRIP = TOK // 8
HALF = TOK // 2
KT = D_MODEL // P
H_A, H_B, H_C = 4, 8, 4
Q_TILES, KV_TILES = 4, 2
PAST = 128
KEYS = TOK + PAST
EPS = 1e-6
CONV_K = 5
PADW = TOK + 8
CONVW = TOK + 4
SM_SCALE = float((128 + 64) ** -0.5)
DK_SCALE = float(P ** -0.5)
NEG = -1.0e30
LEVELS = 7

ADA_COLS = 1024
ADA_GROUPS = 3 * D_MODEL // ADA_COLS
ADA_HALVES = ADA_GROUPS * KT
ADA_PAIRS = ADA_GROUPS // 2
ADA_TILES = ADA_COLS // P
STREAM = dict(gates=2, gdn=8 * H_A, mlstm=10 * H_C, mla_in=30, mla=2 * H_B, out=2 * KT)
STREAM_HALVES = sum(STREAM.values())
CELLS = 8
RAW_SLOTS = 4

C_ID, C_ONE, C_NEG, C_FOLD, C_ROPE = 0, 128, 256, 512, 640
C_WIDTH = C_ROPE + TOK
PRM = {}
_at = 0
for _n, _w in (("b_ada", 48), ("g_pre", 16), ("g_post", 16), ("conv", 12 * CONV_K), ("gdn_norm", 1),
               ("q_norm", 4), ("kv_norm", 2), ("mlstm_norm", 1), ("gates", 4)):
    PRM[_n] = _at
    _at += _w
PRM_WIDTH = _at


class Stage:

    def __init__(self, name, sems, passed, book):
        self.name, self.sems, self.passed = name, sems, passed
        self.book = book.setdefault(name, {e: {} for e in sems})
        self.total = {e: self.book[e].get("", 1) for e in sems}

    def body(self, me, eng, turn):
        return Body(self, me, eng, turn)


class Body:

    def __init__(self, stage, me, eng, turn):
        self.stage, self.me, self.eng, self.n = stage, me, eng, 0
        self.base = {e: 0 if turn is None else eng.snap(turn * stage.total[e]) for e in stage.sems}
        self.seen = {}

    def value(self, who, n):
        return self.base[who] + n

    def did(self, ins, label=None):
        ins.then_inc(self.stage.sems[self.me], 1)
        self.n += 1
        if label:
            self.stage.book[self.me][label] = self.n
        return ins

    def link(self, ins, label=None):
        self.did(ins, label)
        self.eng.wait_ge(self.stage.sems[self.me], self.value(self.me, self.n))

    def wait(self, who, label):
        n = self.stage.book[who].get(label, 1)
        if self.seen.get(who, 0) < n:
            self.seen[who] = n
            self.eng.wait_ge(self.stage.sems[who], self.value(who, n))

    def note(self):
        self.stage.book[self.me][""] = self.n

    def leave(self):
        self.note()
        self.eng.sem_inc(self.stage.passed, 1)

    def end(self):
        self.note()
        for who in self.stage.sems:
            n = self.n if who == self.me else self.stage.total[who]
            self.eng.wait_ge(self.stage.sems[who], self.value(who, n))
        self.eng.sem_inc(self.stage.passed, 1)


def build(nc, io, book):
    ctx = ExitStack()
    with ctx:
        def sb(name, shape, dt=F32):
            return ctx.enter_context(nc.sbuf_tensor(name, shape, dt))

        def ps(name, shape):
            return ctx.enter_context(nc.psum_tensor(name, shape, F32))

        def sem(name):
            return ctx.enter_context(nc.semaphore(name))

        def stage(name, engines="pe act dve"):
            return Stage(name, {e: sem(f"{name}_{e}_steps") for e in engines.split()}, sem(f"{name}_passed"), book)

        h_hi = sb("h_hi", [P, KT, TOK], F32R)
        h_lo = sb("h_lo", [P, KT, TOK], F32R)
        xo = sb("xo", [P, KT, TOK])
        raw = sb("raw", [P, RAW_SLOTS, CELLS, P])
        w_hi = sb("w_hi", [P, 2, CELLS, P], F32R)
        w_lo = sb("w_lo", [P, 2, CELLS, P], F32R)
        W = sb("work", [P, 17, TOK])
        con = sb("constants", [P, C_WIDTH])
        lvl = sb("level_masks", [P, 2, LEVELS, P], F16)
        prm = sb("parameters", [P, PRM_WIDTH])
        cond = sb("cond", [P, KT, 2])
        cond_t = sb("cond_t", [P, KT, 2])
        mod = sb("mod", [P, 3 * KT, 2])
        mul = sb("mul", [P, KT, 2])
        tokc = sb("token_columns", [P, 5, TILES, 8])
        colt = sb("column_temps", [P, 12, TILES])
        hcw = sb("head_conv", [P, 3, CONV_K])
        state = sb("state", [P, 2, 2 * P])
        mxs = sb("row_sums", [P, 4, TILES])
        mprev = sb("m_prev", [8, 2, TILES])
        m0 = sb("m0", [8, 1])
        mout = sb("m_out", [8, 2])
        n0 = sb("n0", [P, 1])
        cst = sb("small_constants", [P, 3])

        pj = [ps(f"projection{i}", [P, 2, 512]) for i in range(2)]
        wa = ps("wa", [P, 1024])
        wb = ps("wb", [P, 1024])

        rows = nc.dram_tensor("rows", [5, 8, TOK], F32, kind="Internal").ap()
        x_kept = nc.dram_tensor("x_kept", [P, KT, TOK], F32, kind="Internal").ap()

        ident = con[:, C_ID:C_ID + P]
        ones = con[:, C_ONE:C_ONE + P]

        def neg(d):
            return con[:, C_NEG + d * P:C_NEG + (d + 1) * P]

        def tiled(ap):
            return ap.rearrange("p (t c) -> p t c", c=P)

        def over_tiles(ap):
            return ap.unsqueeze(1).to_broadcast([P, TILES, P])

        def over_cols(ap):
            return ap.unsqueeze(2).to_broadcast([P, TILES, P])

        def halves(ap):
            return ap.rearrange("p (a n) -> p a n", a=2)

        def wt(i):
            return W[:, i, :]

        def xt(i):
            return xo[:, i, :]

        KB, DECAY, KK, QK = [wt(14), xt(14)], [wt(7), wt(15)], [wt(9), xt(12)], [wt(16), xt(13)]
        INV, INV_T, LEVEL, PROD = [wt(10), xt(14)], [wt(11), xt(15)], [wt(12), xt(9)], [wt(13), wt(15)]
        row_g, row_beta = [wt(5), xt(10)], [wt(6), xt(11)]

        MROWS = [[wt(5), wt(6), wt(7)], [xt(9), xt(10), xt(11)]]

        def T(ap, t):
            return ap[:, t * P:(t + 1) * P]

        def flat(i, n, of=W):
            return of[:, i:i + 2, :].rearrange("p a n -> p (a n)")[:, 0:n]

        pads = [flat(9, PADW), flat(11, PADW), flat(13, PADW)]
        convs = [flat(15, CONVW), flat(10, CONVW, xo), flat(7, CONVW)]

        MLA_ORDER, MLA_PS = [1, 2, 3, 4, 0], (wa, wb)
        MLA_SCORES = [pj[i][:, :, :].rearrange("p a n -> p (a n)") for i in range(2)]

        raw_full = [sem(f"raw_full{s}") for s in range(RAW_SLOTS)]
        raw_free = [sem(f"raw_free{s}") for s in range(RAW_SLOTS)]
        split_done = sem("split_done")
        split_part = sem("split_part")
        split_used = sem("split_used")
        const_in = sem("const_in")
        x_in = sem("x_in")
        params_in = sem("params_in")
        x_saved = sem("x_saved")
        x_back = [sem(f"x_back{i}") for i in range(4)]
        rows_out = sem("rows_out")
        m0_in = sem("m0_in")
        m_out = sem("m_out_stored")
        rows_in = [sem(f"rows_in{d}") for d in range(2)]
        state_in = [sem(f"state_in{d}") for d in range(2)]
        state_out = [sem(f"state_out{d}") for d in range(2)]
        crows_in = [sem(f"mlstm_rows_in{d}") for d in range(2)]
        cstate_in = [sem(f"mlstm_state_in{d}") for d in range(2)]
        cstate_out = [sem(f"mlstm_state_out{d}") for d in range(2)]
        cache_in = sem("cache_in")
        latent_out = sem("latent_out")
        y_out = sem("y_out")

        s_init = stage("init", "act dve")
        s_ada = stage("ada", "pe dve")
        s_norm = stage("norm", "pe act dve pool")
        s_gate = stage("gates")
        s_gdn = stage("gdn")
        s_mli = stage("mlstm_in", "pe act")
        s_mls = stage("mlstm")
        s_min = stage("mla_in")
        s_mla = stage("mla")
        s_spl = stage("out_split", "act dve")
        s_out = stage("out")
        s_res = stage("residual")

        block = ctx.enter_context(nc.Block())

        @block.sync
        def _(sp):
            sp.dma_start(con[:, :], io["constants"]).then_inc(const_in, 16)
            sp.dma_start(lvl[:, :, :, :], io["levels"]).then_inc(const_in, 16)
            sp.dma_start(cond_t[:, :, :], io["cond"]).then_inc(const_in, 16)
            for s in range(RAW_SLOTS):
                sp.sem_inc(raw_free[s], 1)
            per_layer = (ADA_HALVES + STREAM_HALVES) // RAW_SLOTS
            with sp.Fori(0, DEPTH) as l:
                for n, first, src in ((ADA_HALVES, 0, io["w_ada"]),
                                      (STREAM_HALVES, ADA_HALVES // RAW_SLOTS, io["w_stream"])):
                    with sp.Fori(0, n // RAW_SLOTS) as i:
                        turn = sp.snap(l * per_layer + i + first + 1)
                        for s in range(RAW_SLOTS):
                            sp.wait_ge(raw_free[s], turn)
                            sp.dma_start(raw[:, s, :, :].rearrange("p c n -> p (c n)"),
                                         src[l, i * RAW_SLOTS + s, :, :]).then_inc(raw_full[s], 16)

        @block.gpsimd
        def _(pool):
            once = ones.unsqueeze(1).to_broadcast([P, CELLS, P])
            pool.wait_ge(const_in, 48)
            pool.sem_inc(split_used, 2)
            per_layer = (ADA_HALVES + STREAM_HALVES) // RAW_SLOTS
            with pool.Fori(0, DEPTH) as l:
                N = s_norm.body("pool", pool, l)
                N.wait("act", "square1")
                N.link(nc.gpsimd.tensor_tensor(wt(8), wt(0), wt(1), ALU.add), "squares1")
                for k in range(2, KT):
                    N.wait("act", f"square{k}")
                    N.link(nc.gpsimd.tensor_tensor(wt(8), wt(8), wt(k % 4), ALU.add), f"squares{k}")
                N.leave()
                with pool.Fori(0, STREAM_HALVES // RAW_SLOTS) as i:
                    turn = pool.snap((l * per_layer + i + (ADA_HALVES // RAW_SLOTS + 1)) * 16)
                    done = pool.snap((l * (STREAM_HALVES // RAW_SLOTS) + i) * RAW_SLOTS)
                    for s in range(RAW_SLOTS):
                        pool.wait_ge(split_used, done + s + 1)
                        pool.wait_ge(raw_full[s], turn)
                        nc.gpsimd.tensor_tensor(w_hi[:, s % 2, :, :], raw[:, s, :, :], once, ALU.mult).then_inc(split_part, 1)
                        pool.wait_ge(split_part, done * 2 + 2 * s + 1)
                        nc.gpsimd.tensor_tensor(w_lo[:, s % 2, :, :], raw[:, s, :, :],
                                                w_hi[:, s % 2, :, :].bitcast(F32), ALU.subtract)\
                            .then_inc(split_part, 1)
                        pool.wait_ge(split_part, done * 2 + 2 * s + 2)
                        pool.sem_inc(raw_free[s], 1)
                        pool.sem_inc(split_done, 1)

        @block.tensor
        def _(pe):
            mm = nc.tensor.matmul

            def parts_ready(n):
                pe.wait_ge(split_done, n + 1)

            def project(out, n, second=None):
                last = None
                for half in range(2):
                    parts_ready(n + half)
                    if half and second:
                        second()
                    for c in range(CELLS):
                        k = half * CELLS + c
                        tile = (k + CELLS) % KT if second else k
                        for a in range(2):
                            hs = slice(a * HALF, (a + 1) * HALF)
                            o = out[:, a, 0:HALF]
                            mm(o, w_hi[:, half, c, :], h_hi[:, tile, hs], start=(k == 0), stop=False)
                            mm(o, w_hi[:, half, c, :], h_lo[:, tile, hs], start=False, stop=False)
                            last = mm(o, w_lo[:, half, c, :], h_hi[:, tile, hs], start=False, stop=(k == KT - 1))
                    if half == 0:
                        last.then_inc(split_used, 1)
                return last

            def used_and(B, last, n, label):
                last.then_inc(split_used, 1)
                pe.wait_ge(split_used, n + 2)
                B.did(pe.nop(), label)

            class Ahead:

                def __init__(self, B, n, tiles):
                    self.B, self.n, self.tiles, self.at = B, n, tiles, 0

                def cells(self, count):
                    for _ in range(count):
                        j, k = divmod(self.at, KT)
                        if j == self.tiles:
                            break
                        if k == 0 and j >= 2:
                            self.B.wait("act", f"ahead taken{j - 2}")
                        half, c = divmod(k, CELLS)
                        if c == 0:
                            parts_ready(self.n + (2 * j + half))
                        for a in range(2):
                            hs, o = slice(a * HALF, (a + 1) * HALF), pj[j % 2][:, a, 0:HALF]
                            mm(o, w_hi[:, half, c, :], h_hi[:, k, hs], start=(k == 0), stop=False)
                            mm(o, w_hi[:, half, c, :], h_lo[:, k, hs], start=False, stop=False)
                            last = mm(o, w_lo[:, half, c, :], h_hi[:, k, hs], start=False, stop=(k == KT - 1))
                        if c == CELLS - 1:
                            last.then_inc(split_used, 1)
                        self.at += 1

                def finish(self):
                    self.cells(self.tiles * KT - self.at)

            def each_tile(out, lhs, rhs):
                last = None
                for t in range(TILES):
                    last = mm(T(out, t), T(lhs, t), T(rhs, t), start=True, stop=True)
                return last

            def transposed(out, src):
                last = None
                for t in range(TILES):
                    last = nc.tensor.transpose(T(out, t), T(src, t), ident)
                return last

            def column_sums(out, src, first=True, last=True):
                mm(out[:, 0:512], ones, src[:, 0:512], start=first, stop=last)
                return mm(out[:, 512:TOK], ones, src[:, 512:TOK], start=first, stop=last)

            def halved_sums(out, src):
                mm(out[:, 0, 0:HALF], ones, src[:, 0:HALF], start=True, stop=True)
                return mm(out[:, 1, 0:HALF], ones, src[:, HALF:TOK], start=True, stop=True)

            pe.wait_ge(const_in, 48)
            with pe.Fori(0, DEPTH) as l:
                per_layer = (ADA_HALVES + STREAM_HALVES) // RAW_SLOTS

                def ada_turn(i):
                    B = s_ada.body("pe", pe, l * ADA_PAIRS + i)
                    turn = pe.snap((l * per_layer + i * (2 * KT // RAW_SLOTS) + 1) * 16)

                    def group(j, ks):
                        for k in ks:
                            s, use = k % RAW_SLOTS, (j * KT + k) // RAW_SLOTS
                            pe.wait_ge(raw_full[s], turn + 16 * use)
                            for a in range(2):
                                last = mm((wa, wb)[j][0:2, a * 512:(a + 1) * 512], cond[:, k, :],
                                          raw[:, s, 4 * a:4 * a + 4, :].rearrange("p c n -> p (c n)"),
                                          start=(k == 0), stop=(k == KT - 1))
                            last.then_inc(raw_free[s], 1)

                    def turned(j):
                        B.wait("dve", f"rows{j}")
                        B.did(pe.nop())
                        for c in range(ADA_TILES):
                            last = nc.tensor.transpose(pj[0][:, 0, (j * ADA_TILES + c) * 2:(j * ADA_TILES + c + 1) * 2],
                                                       flat(13 + 2 * j, ADA_COLS)[0:2, c * P:(c + 1) * P], con[0:2, 0:2])
                        B.did(last, f"turned{j}")

                    group(0, range(KT))
                    group(1, range(KT // 2))
                    turned(0)
                    group(1, range(KT // 2, KT))
                    turned(1)
                    B.end()

                pe.wait_ge(s_init.sems["dve"], s_init.total["dve"])
                with pe.Fori(0, ADA_PAIRS - 1) as i:
                    ada_turn(i)
                N = s_norm.body("pe", pe, l)
                N.wait("pool", f"squares{KT - 1}")
                N.did(halved_sums(pj[1], wt(8)), "sum")
                ada_turn(ADA_PAIRS - 1)

                layer0 = pe.snap(l * STREAM_HALVES)
                last = None
                for k in range(KT):
                    half, c = divmod(k, CELLS)
                    if c == 0:
                        parts_ready(layer0 + half)
                    N.wait("dve", f"h{k}")
                    for a in range(2):
                        hs, o = slice(a * HALF, (a + 1) * HALF), pj[1][:, a, 0:HALF]
                        mm(o, w_hi[:, half, c, :], h_hi[:, k, hs], start=(k == 0), stop=False)
                        mm(o, w_hi[:, half, c, :], h_lo[:, k, hs], start=False, stop=False)
                        last = mm(o, w_lo[:, half, c, :], h_hi[:, k, hs], start=False, stop=(k == KT - 1))
                    if k == CELLS - 1:
                        last.then_inc(split_used, 1)
                used_and(N, last, layer0 + 2, "gates")
                N.leave()

                B = s_gate.body("pe", pe, l)
                for j in range(4):
                    if j:
                        B.wait("act", "log" if j == 1 else f"ahead taken{j - 2}")
                    project(pj[j % 2], layer0 + (2 * j + 2)).then_inc(split_used, 1)
                for n, (label, src) in enumerate((("cum", 10), ("cum", 12), ("beta", 14), ("aF", 0), ("aB", 1))):
                    B.wait("dve", label)
                    if n in (0, 2, 3, 4):
                        B.did(pe.nop())
                    for t in range(TILES):
                        last = nc.tensor.transpose(wb[:, (n * TILES + t) * 8:(n * TILES + t + 1) * 8],
                                                   W[0:8, src, t * P:(t + 1) * P], con[0:8, 0:8])
                    B.did(last, f"columns{n}")
                B.wait("act", "ahead taken3")
                B.leave()

                with pe.Fori(0, H_A) as h:
                    B = s_gdn.body("pe", pe, l * H_A + h)
                    ahead = Ahead(B, pe.snap(l * STREAM_HALVES + h * 8 + (STREAM["gates"] + 8)), 4)
                    ahead.cells(24)
                    B.wait("act", "q squared")
                    B.did(column_sums(wa, wt(9)), "q sum")
                    ahead.cells(4)
                    B.wait("act", "k squared")
                    B.did(column_sums(wb, wt(11)), "k sum")
                    ahead.cells(4)
                    B.wait("dve", "k normed")
                    B.did(transposed(wa, wt(1)), "k turned")
                    ahead.cells(1)
                    B.wait("dve", "v silu")
                    B.did(transposed(wb, wt(4)), "v turned")
                    ahead.cells(5)
                    B.wait("act", "v turned taken")
                    for d in range(2):
                        B.wait("dve", f"kb{d}")
                        if d:
                            B.wait("dve", "kk decayed0")
                        B.did(each_tile(wa, wt(1), KB[d]), f"kk{d}")
                        if d:
                            B.wait("dve", "qk decayed0")
                        B.did(each_tile(wb, wt(1), wt(0)), f"qk{d}")
                        ahead.cells(2 + d)
                    for v in range(LEVELS):
                        for d in range(2):
                            B.wait("dve", f"level{d}{v}")
                            for t in range(TILES):
                                last = mm(T((wa, wb)[d], t), T(LEVEL[d], t), ident if v == 0 else T(INV[d], t),
                                          start=True, stop=True)
                            B.did(last, f"ld{d}{v}")
                        ahead.cells(1 if v < 2 else 0)
                        if 0 < v < LEVELS - 1:
                            for d in range(2):
                                B.wait("act", f"ld taken{d}{v}")
                                B.did(each_tile((wa, wb)[d], INV_T[d], PROD[d]), f"dld{d}{v}")
                        if v:
                            for d in range(2):
                                B.wait("act", f"ld taken{d}{v}")
                                if v < LEVELS - 1:
                                    B.wait("dve", f"inv{d}{v}")
                                B.did(each_tile((wa, wb)[d], PROD[d], INV_T[d]), f"dldT{d}{v}")
                    for d in range(2):
                        ahead.cells(4 - d)
                        B.wait("dve", "inverse1")
                        B.wait("dve", f"kbg{d}")
                        B.did(each_tile(wa, wt(15), INV_T[d]), f"wT{d}")
                        ahead.cells(1)
                        B.wait("act", f"wT taken{d}")
                        B.wait("dve", f"kdec{d}")
                        order = [0, 1, 2, 3, 4] if d == 0 else [0, 4, 3, 2, 1]
                        for n, t in enumerate(order):
                            st = state[:, min(n, 1), 0:P]
                            last = mm(wa[:, 0:P], T(INV_T[d], t), T(wt(14), t), start=True, stop=(n == 0))
                            if n == 1:
                                pe.wait_ge(state_in[d], (l * H_A + h + 1) * 16)
                            if n:
                                if n > 1:
                                    B.wait("dve", f"state{d}{n - 1}")
                                last = mm(wa[:, 0:P], T(wt(12), t), st, start=False, stop=True)
                            B.did(last, f"vnew{d}{n}")
                            if n:
                                mm(wa[:, 512:512 + P], st, T(wt(13), t), start=True, stop=False)
                            B.wait("act", f"vnew taken{d}{n}")
                            last = mm(wa[:, 512:512 + P], T(wt(9), t), T(QK[d], t), start=(n == 0), stop=True)
                            B.did(last, f"o{d}{n}")
                            B.did(mm(wb[:, 0:P], T(wt(10), t), T(wt(9), t), start=True, stop=True), f"kv{d}{n}")
                            ahead.cells(1 + d)
                            if n == TILES - 1 and d:
                                ahead.finish()
                            B.wait("dve", f"o taken{d}{n}")
                    B.wait("act", "o squared")
                    B.did(column_sums(wa, wt(6)), "o sum")
                    B.wait("act", "ahead taken3")
                    B.leave()

                B = s_mli.body("pe", pe, l)
                n0_ = pe.snap(l * STREAM_HALVES + (STREAM["gates"] + STREAM["gdn"] + 8))
                used_and(B, project(pj[0], n0_), n0_ + 2, "z")
                B.end()
                with pe.Fori(0, H_C) as h:
                    B = s_mls.body("pe", pe, l * H_C + h)
                    ahead = Ahead(B, pe.snap(l * STREAM_HALVES + h * 10 + (STREAM["gates"] + STREAM["gdn"] + 10)), 5)
                    ahead.cells(12)
                    B.wait("act", "k taken")
                    B.did(transposed(wa, wt(1)), "k turned")
                    B.wait("act", "v taken")
                    B.did(transposed(wb, wt(2)), "v turned")
                    ahead.cells(6)
                    for d in range(2):
                        B.wait("dve", "v turned taken")
                        B.wait("act", "k turned taken")
                        if d:
                            B.wait("dve", "hB ready")
                        B.did(each_tile(wa, wt(1), wt(0)), f"qk{d}")
                        ahead.cells(4)
                        B.wait("dve", f"s{d}")
                        order = [0, 1, 2, 3, 4] if d == 0 else [0, 4, 3, 2, 1]
                        for n, t in enumerate(order):
                            if n:
                                if n == 1:
                                    B.wait("dve", f"n rep{d}")
                                else:
                                    B.wait("dve", f"state{d}{n - 1}")
                                mm(wa[:, 0:P], state[:, 1, 0:P], T(wt(10), t), start=True, stop=False)
                            mm(wa[:, 0:P], T(wt(4), t), T(wt(9), t), start=(n == 0), stop=True)
                            if n:
                                mm(wa[:, 512:512 + P], state[:, 1, P:2 * P], T(wt(10), t), start=True, stop=False)
                            B.did(mm(wa[:, 512:512 + P], ones, T(wt(9), t), start=(n == 0), stop=True), f"numden{d}{n}")
                            mm(wb[:, 0:P], T(wt(11), t), T(wt(4), t), start=True, stop=True)
                            B.did(mm(wb[:, P:2 * P], T(wt(11), t), ones, start=True, stop=True), f"kv{d}{n}")
                            ahead.cells(4 + 2 * d)
                            B.wait("dve", f"h taken{d}{n}")
                    ahead.finish()
                    B.wait("act", "h squared")
                    B.did(column_sums(wa, wt(6)), "h sum")
                    B.wait("act", "ahead taken4")
                    B.leave()

                B = s_min.body("pe", pe, l)
                n0_ = pe.snap(l * STREAM_HALVES + (STREAM["gates"] + STREAM["gdn"] + STREAM["mlstm"]))
                for j in range(5, 15):
                    if j >= 7:
                        B.wait("act", f"taken{j - 2}")
                    used_and(B, project(pj[j % 2], n0_ + 2 * j), n0_ + 2 * j + 2, f"tile{j}")
                    if j == 5:
                        B.wait("dve", "cq squares")
                        B.did(column_sums(wa, wt(8)), "cq sum")
                    if j == 7:
                        B.wait("dve", "ckv squares")
                        B.did(column_sums(wb, wt(7)), "ckv sum")
                    if j == 12:
                        B.wait("dve", "roped")
                        mm(wa[:, 0:512], con[:, C_FOLD:C_FOLD + P], W[:, 7, 0:512], start=True, stop=True)
                        B.did(mm(wa[:, 512:TOK], con[:, C_FOLD:C_FOLD + P], W[:, 7, 512:TOK], start=True, stop=True),
                              "key pe")
                B.end()

                with pe.Fori(0, H_B) as h:
                    B = s_mla.body("pe", pe, l * H_B + h)
                    n0_ = pe.snap(l * STREAM_HALVES + h * 2
                                  + (STREAM["gates"] + STREAM["gdn"] + STREAM["mlstm"] + STREAM["mla_in"]))
                    cqn = [(h_hi[:, k, :], h_lo[:, k, :]) for k in range(Q_TILES)]
                    kvh = h_hi[:, 4:7, :].rearrange("p a n -> p (a n)")
                    kvl = h_lo[:, 4:7, :].rearrange("p a n -> p (a n)")

                    def three(out, hi, lo, xh, xl, first, last):
                        mm(out, hi, xh, start=first, stop=False)
                        mm(out, hi, xl, start=False, stop=False)
                        return mm(out, lo, xh, start=False, stop=last)

                    parts_ready(n0_)
                    for which in range(2):
                        for k in range(Q_TILES):
                            for a in range(2):
                                hs = slice(a * HALF, (a + 1) * HALF)
                                last = three(pj[which][:, a, 0:HALF], w_hi[:, 0, 2 * k + which, :],
                                             w_lo[:, 0, 2 * k + which, :], cqn[k][0][:, hs], cqn[k][1][:, hs],
                                             k == 0, k == Q_TILES - 1)
                        if which == 0:
                            B.did(last, "q nope")
                    used_and(B, last, n0_ + 1, "q pe")
                    parts_ready(n0_ + 1)
                    B.wait("act", "q nope taken")
                    for k in range(KV_TILES):
                        for a in range(2):
                            at = k * KEYS + a * (KEYS // 2)
                            last = three(pj[0][:, a, 0:KEYS // 2], w_hi[:, 1, 2 * k, :], w_lo[:, 1, 2 * k, :],
                                         kvh[:, at:at + KEYS // 2], kvl[:, at:at + KEYS // 2],
                                         k == 0, k == KV_TILES - 1)
                    B.did(last, "k nope")
                    B.wait("dve", "q pe roped")
                    for t in range(KEYS // P):
                        o = pj[1][:, t // 3, (t % 3) * P:(t % 3 + 1) * P]
                        for k in range(KV_TILES):
                            at = k * KEYS + t * P
                            last = three(o, kvh[:, at:at + P], kvl[:, at:at + P], w_hi[:, 1, 2 * k + 1, :],
                                         w_lo[:, 1, 2 * k + 1, :], k == 0, k == KV_TILES - 1)
                    used_and(B, last, n0_ + 2, "v")
                    qn, qp, kn, kp, vt = wt(0), wt(1), flat(2, KEYS), flat(8, KEYS), flat(4, KEYS)

                    def scores(m):
                        t = MLA_ORDER[m]
                        if m == 1:
                            B.wait("act", "v taken")
                        if m >= 2:
                            B.wait("act", f"exp{m - 2}")
                        spans = [(0, CTX, 0)] if t == 0 else [(CTX, TOK, 0), (TOK, KEYS, 512)]
                        for a, b, o in spans:
                            mm(MLA_SCORES[m % 2][:, o:o + b - a], T(qn, t), kn[:, a:b], start=True, stop=False)
                            last = mm(MLA_SCORES[m % 2][:, o:o + b - a], T(qp, t), kp[:, a:b], start=False, stop=True)
                        B.did(last, f"scores{m}")

                    def turned(m):
                        t = MLA_ORDER[m]
                        B.wait("dve", f"normed{m}")
                        for j in range(1 if t == 0 else TILES):
                            last = nc.tensor.transpose(T(MLA_PS[m % 2], j), T(wt(6 + 4 * (m % 2)), j), ident)
                        B.did(last, f"turned{m}")

                    def output(m):
                        t = MLA_ORDER[m]
                        nk, k0 = (1, 0) if t == 0 else (TILES, 1)
                        B.wait("act", f"turned taken{m}")
                        if m >= 2:
                            B.wait("dve", f"o taken{m - 2}")
                        for j in range(nk):
                            last = mm(MLA_PS[m % 2][:, 768:768 + P], T(vt, k0 + j), T(wt(7 + 4 * (m % 2)), j),
                                      start=(j == 0), stop=(j == nk - 1))
                        B.did(last, f"o{m}")

                    B.wait("act", "k nope taken")
                    for m in range(TILES + 1):
                        if m < TILES:
                            scores(m)
                        if m >= 2:
                            output(m - 2)
                        if m >= 1:
                            turned(m - 1)
                    output(TILES - 1)
                    B.leave()

                def rest_split():
                    pe.wait_ge(s_spl.sems["dve"], (l + 1) * s_spl.total["dve"])
                with pe.Fori(0, KT // 2) as f:
                    B = s_out.body("pe", pe, l * (KT // 2) + f)
                    n0_ = pe.snap(l * STREAM_HALVES + f * 4 + (STREAM_HALVES - STREAM["out"]))
                    used_and(B, project(pj[0], n0_, rest_split), n0_ + 2, "first")
                    B.wait("dve", "begun")
                    used_and(B, project(pj[1], n0_ + 2, rest_split), n0_ + 2 + 2, "second")
                    B.wait("dve", "taken0")
                    B.leave()
                B = s_res.body("pe", pe, l)
                B.wait("dve", "y squared")
                B.did(halved_sums(pj[0], wt(8)), "sum")
                B.leave()

        @block.scalar
        def _(act):
            A = nc.scalar.activation
            act.preload_act_table_set("natural_log_exp_and_others")
            act.dma_start(xo[:, :, :], io["x"]).then_inc(x_in, 16)
            def sigmoid(B, out, src, label):
                B.link(A(out, src, ACT.Exp, scale=-1.0))
                B.link(A(out, out, ACT.Ln, bias=1.0))
                B.did(A(out, out, ACT.Exp, scale=-1.0), label)

            def take(B, n, j, dst):
                act.wait_ge(split_used, n + (2 * j + 4))
                B.did(A(halves(dst), pj[j % 2][:, :, 0:HALF], ACT.Copy), f"ahead taken{j}")

            def rsqrt(B, out, src, tmp, scale, label, post=1.0):
                B.link(A(tmp, src, ACT.Ln, bias=cst[:, 0:1], scale=scale))
                B.link(A(out, tmp, ACT.Exp, scale=-0.5, bias=(cst[:, 1:2] if post != 1.0 else 0.0)), label)

            act.wait_ge(const_in, 48)
            B = s_init.body("act", act, None)
            B.wait("dve", "eps")
            B.link(A(cond[:, :, :], cond_t[:, :, :], ACT.Exp, scale=-1.0), "cond exp")
            B.end()
            with act.Fori(0, DEPTH) as l:
                act.dma_start(prm[:, :], io["params"][l, :, :]).then_inc(params_in, 16)
                act.dma_start(m0[:, :], io["m0"][l, :, :]).then_inc(m0_in, 16)
                act.wait_ge(x_in, 16)
                act.dma_start(x_kept, xo[:, :, :]).then_inc(x_saved, 16)

                B = s_norm.body("act", act, l)
                for k in range(KT):
                    if k >= 4:
                        B.wait("pool", f"squares{max(k - 4, 1)}")
                    B.did(A(wt(k % 4), xo[:, k, :], ACT.Square), f"square{k}")
                B.wait("pe", "sum")
                rsqrt(B, halves(wt(5)), pj[1][:, :, 0:HALF], halves(wt(4)), 1.0 / D_MODEL, "rstd")
                for k in range(KT):
                    B.wait("dve", f"u{k}")
                    B.did(A(h_hi[:, k, :], wt(6 + k % 4), ACT.Copy), f"hi{k}")
                B.end()

                B = s_gate.body("act", act, l)
                g = PRM["gates"]
                act.wait_ge(params_in, (l + 1) * 16)
                xx = W[0:8, 0:2, :]
                B.link(A(colt[0:8, 0, 0:1], prm[0:8, g:g + 1], ACT.Exp), "exp a_log")

                def gate(at):
                    return pj[1][at:at + 8, :, 0:HALF]
                B.did(A(halves(W[0:8, 0, :]), gate(0), ACT.Identity, bias=prm[0:8, g + 1:g + 2]))
                B.did(A(halves(W[0:8, 1, :]), gate(96), ACT.Identity, bias=prm[0:8, g + 3:g + 4]))
                B.did(A(halves(W[0:8, 15, :]), gate(64), ACT.Identity, bias=prm[0:8, g + 2:g + 3]), "i")
                B.link(A(halves(W[0:8, 14, :]), gate(32), ACT.Exp, scale=-1.0), "beta exp")
                B.link(A(W[0:8, 1, :], W[0:8, 1, :], ACT.Copy, scale=-1.0), "x")
                B.link(A(W[0:8, 2:4, :], xx, ACT.Abs))
                B.link(A(W[0:8, 2:4, :], W[0:8, 2:4, :], ACT.Exp, scale=-1.0))
                B.link(A(W[0:8, 2:4, :], W[0:8, 2:4, :], ACT.Ln, bias=1.0), "log")
                act.wait_ge(x_saved, (l + 1) * 16)
                n0_ = act.snap(l * STREAM_HALVES + STREAM["gates"])
                take(B, n0_, 0, xt(4))
                take(B, n0_, 1, xt(5))
                B.wait("dve", "wi")
                B.link(A(W[0:8, 6:8, :], W[0:8, 6:8, :], ACT.Exp), "wi exp")
                B.wait("dve", "em")
                B.link(A(W[0:8, 8:10, :], W[0:8, 8:10, :], ACT.Exp, scale=-1.0), "em exp")
                for d in range(2):
                    hs = slice(4 * d, 4 * d + 4)
                    act.dma_start(rows[0, hs, :], W[hs, 10 + 2 * d, :]).then_inc(rows_out, 16)
                    act.dma_start(rows[1, hs, :], W[hs, 14, :]).then_inc(rows_out, 16)
                    act.dma_start(rows[2, hs, :], W[hs, 2 + d, :]).then_inc(rows_out, 16)
                    act.dma_start(rows[3, hs, :], W[hs, 6 + d, :]).then_inc(rows_out, 16)
                    act.dma_start(rows[4, hs, :], W[hs, 8 + d, :]).then_inc(rows_out, 16)
                    act.dma_start(io["new_m"][l, d, :, :], mout[hs, d:d + 1]).then_inc(rows_out, 16)
                take(B, n0_, 2, xt(6))
                take(B, n0_, 3, xt(7))
                B.wait("pe", "columns4")
                B.link(A(tokc[:, :, :, :].rearrange("p k t h -> p (k t h)"), wb[:, 0:5 * TILES * 8], ACT.Copy))
                act.wait_ge(rows_out, (l + 1) * (12 * 16))
                B.did(act.nop())
                B.end()

                with act.Fori(0, H_A) as h:
                    B = s_gdn.body("act", act, l * H_A + h)
                    now = act.snap((l * H_A + h + 1) * 16)
                    n0_ = act.snap(l * STREAM_HALVES + h * 8 + (STREAM["gates"] + 8))
                    act.dma_start(state[:, 1, 0:P], io["state_gdn"][l, 0, h, :, :]).then_inc(state_in[0], 16)
                    for tile, kind in ((row_g[0], 0), (row_beta[0], 1)):
                        act.dma_start(tile, rows[kind, bass.ds(h, 1), :].partition_broadcast(P)).then_inc(rows_in[0], 16)
                    B.wait("dve", "zeros")
                    for i in range(3):
                        B.did(A(pads[i][:, 2:2 + CTX], xt(4 + i)[:, 0:CTX], ACT.Copy))
                        B.did(A(pads[i][:, 6 + CTX:6 + TOK], xt(4 + i)[:, CTX:TOK], ACT.Copy), f"{'qkv'[i]} padded")
                    for i in range(2):
                        B.wait("dve", f"{'qk'[i]} conv")
                        sigmoid(B, pads[i][:, 0:CONVW], convs[i], f"{'qk'[i]} sigmoid")
                    B.wait("dve", "q silu")
                    B.did(A(wt(9), wt(0), ACT.Square), "q squared")
                    B.wait("act", "v padded")
                    take(B, n0_, 0, xt(4))
                    B.wait("dve", "v conv")
                    sigmoid(B, pads[2][:, 0:CONVW], convs[2], "v sigmoid")
                    B.wait("dve", "k silu")
                    B.did(A(wt(11), wt(1), ACT.Square), "k squared")
                    B.wait("pe", "q sum")
                    rsqrt(B, wt(10), wa[:, 0:TOK], wt(10), 1.0, "q rstd", DK_SCALE)
                    B.wait("pe", "k sum")
                    rsqrt(B, wt(12), wb[:, 0:TOK], wt(12), 1.0, "k rstd")
                    for tile, kind in ((row_g[1], 0), (row_beta[1], 1)):
                        act.dma_start(tile, rows[kind, bass.ds(h + 4, 1), :].partition_broadcast(P)).then_inc(rows_in[1], 16)
                    sigmoid(B, xt(9), xt(7), "z sigmoid")
                    take(B, n0_, 1, xt(5))
                    B.wait("pe", "k turned")
                    B.did(A(wt(2), wa[:, 0:TOK], ACT.Copy))
                    B.wait("pe", "v turned")
                    B.did(A(wt(3), wb[:, 0:TOK], ACT.Copy), "v turned taken")
                    for d in range(2):
                        B.wait("dve", f"cols{d}")
                        B.did(A(colt[:, 6 * d + 2, :], colt[:, 6 * d, :], ACT.Exp))
                        B.did(A(colt[:, 6 * d + 5, :], colt[:, 6 * d + 4, :], ACT.Exp), f"kdec col{d}")
                        B.wait("dve", f"gap{d}")
                        B.did(A(DECAY[d], DECAY[d], ACT.Exp), f"decay{d}")
                    for v in range(1, LEVELS):
                        for d in range(2):
                            B.wait("pe", f"ld{d}{v}")
                            B.did(A(PROD[d], (wa, wb)[d][:, 0:TOK], ACT.Copy), f"ld taken{d}{v}")
                    for d in range(2):
                        act.wait_ge(rows_in[d], (l * H_A + h + 1) * 32)
                        if d:
                            B.wait("dve", f"o taken0{TILES - 1}")
                        B.did(A(wt(8), row_g[d], ACT.Exp), f"eg{d}")
                        B.wait("pe", f"wT{d}")
                        B.did(A(wt(12), wa[:, 0:TOK], ACT.Copy, scale=-1.0), f"wT taken{d}")
                        for n in range(TILES):
                            t = n if d == 0 or n == 0 else TILES - n
                            B.wait("pe", f"vnew{d}{n}")
                            B.did(A(T(wt(9), t), wa[:, 0:P], ACT.Copy), f"vnew taken{d}{n}")
                            if n == 0:
                                B.wait("dve", f"state{d}0")
                                act.dma_start(io["new_gdn"][l, d, h, :, :], state[:, 0, 0:P]).then_inc(state_out[d], 16)
                        if d == 1:
                            B.wait("dve", "z ready")
                        take(B, n0_, 2 + d, xt(6 + d))
                        if d == 0:
                            B.wait("dve", f"state0{TILES - 1}")
                            act.dma_start(state[:, 1, 0:P], io["state_gdn"][l, 1, h, :, :]).then_inc(state_in[1], 16)
                    B.wait("dve", "o whole")
                    B.did(A(wt(6), wt(4), ACT.Square), "o squared")
                    B.wait("pe", "o sum")
                    rsqrt(B, wt(7), wa[:, 0:TOK], wt(7), 1.0 / P, "o rstd")
                    for d in range(2):
                        act.wait_ge(state_out[d], now)
                    B.did(act.nop())
                    B.end()

                B = s_mli.body("act", act, l)
                B.wait("pe", "z")
                B.did(A(halves(xt(8)), pj[0][:, :, 0:HALF], ACT.Copy))
                B.end()
                with act.Fori(0, H_C) as h:
                    B = s_mls.body("act", act, l * H_C + h)
                    n0_ = act.snap(l * STREAM_HALVES + h * 10 + (STREAM["gates"] + STREAM["gdn"] + 10))
                    act.dma_start(state[:, 1, 0:P], io["state_c"][l, 0, h, :, :]).then_inc(cstate_in[0], 16)
                    act.dma_start(n0[:, :], io["state_n"][l, 0, h, :, :]).then_inc(cstate_in[0], 16)
                    for d in range(2):
                        for j in range(3):
                            act.dma_start(MROWS[d][j], rows[2 + j, bass.ds(h + 4 * d, 1), :].partition_broadcast(P))\
                                .then_inc(crows_in[d], 16)
                    B.did(A(wt(1), xt(5), ACT.Copy), "k taken")
                    B.did(A(wt(2), xt(6), ACT.Copy), "v taken")
                    B.did(A(wt(0), xt(4), ACT.Copy, scale=DK_SCALE), "q taken")
                    B.wait("pe", "k turned")
                    B.did(A(wt(3), wa[:, 0:TOK], ACT.Copy), "k turned taken")
                    for d in range(2):
                        B.wait("dve", f"gap{d}")
                        B.did(A(wt(8), wt(8), ACT.Exp), f"decay{d}")
                        B.did(A(colt[:, 5, :], colt[:, 4, :], ACT.Exp), f"wk col{d}")
                        if d == 0:
                            sigmoid(B, wt(13), xt(7), "o sigmoid")
                            sigmoid(B, wt(15), xt(8), "z sigmoid")
                            B.wait("act", "q taken")
                            take(B, n0_, 0, xt(4))
                            take(B, n0_, 1, xt(5))
                        B.wait("dve", f"state{d}0")
                        act.dma_start(io["new_c"][l, d, h, :, :], state[:, 0, 0:P]).then_inc(cstate_out[d], 16)
                        act.dma_start(io["new_n"][l, d, h, :, :], state[:, 0, P:P + 1]).then_inc(cstate_out[d], 16)
                        if d == 0:
                            B.wait("dve", "hB ready")
                            act.dma_start(state[:, 1, 0:P], io["state_c"][l, 1, h, :, :]).then_inc(cstate_in[1], 16)
                            act.dma_start(n0[:, :], io["state_n"][l, 1, h, :, :]).then_inc(cstate_in[1], 16)
                    B.wait("dve", "oz ready")
                    for j in range(2, 5):
                        take(B, n0_, j, xt(4 + j))
                    B.wait("dve", "h whole")
                    B.did(A(wt(6), wt(12), ACT.Square), "h squared")
                    B.wait("pe", "h sum")
                    rsqrt(B, wt(7), wa[:, 0:TOK], wt(7), 1.0 / P, "h rstd")
                    for d in range(2):
                        act.wait_ge(cstate_out[d], (l * H_C + h + 1) * 32)
                    B.did(act.nop())
                    B.end()

                B = s_min.body("act", act, l)
                act.dma_start(flat(15, 2 * P), io["cache_ckv"][l, :, :]).then_inc(cache_in, 16)
                kp = flat(8, KEYS)
                for a in range(2):
                    act.dma_start(kp[64 * a:64 * a + 64, TOK:KEYS], io["cache_kr"][l, :, :]).then_inc(cache_in, 16)
                def squared(k, src, label):
                    B.did(A(wt(14 + 2 * (k % 2)), src, ACT.Square), label)
                for k in range(2):
                    squared(k, xt(4 + k), f"cq squared{k}")
                for j in range(5):
                    B.did(A(wt(j), xt(4 + j), ACT.Copy), f"taken{j}")
                for k in range(2, Q_TILES):
                    B.wait("dve", "cq added")
                    squared(k, xt(4 + k), f"cq squared{k}")

                for j in range(5, 15):
                    B.wait("pe", f"tile{j}")
                    if j < 7:
                        B.link(A(halves(wt(j)), pj[j % 2][:, :, 0:HALF], ACT.Copy), f"taken{j}")
                    else:
                        if j >= 9:
                            B.wait("dve", f"zb{j - 2}")
                        e, x = wt(10 + 2 * (j % 2)), wt(11 + 2 * (j % 2))
                        B.link(A(halves(x), pj[j % 2][:, :, 0:HALF], ACT.Copy), f"taken{j}")
                        sigmoid(B, e, x, f"zb sigmoid{j}")
                    if j == 5:
                        B.wait("dve", "cq squares")
                        for k in range(KV_TILES):
                            squared(k, wt(4 + k), f"ckv squared{k}")
                    if j == 6:
                        act.dma_start(io["new_kr"][l, :, :], W[0:64, 6, 0:CTX]).then_inc(latent_out, 16)
                        B.wait("pe", "cq sum")
                        B.wait("dve", "ckv squares")
                        rsqrt(B, wt(14), wa[:, 0:TOK], wt(14), 1.0 / (Q_TILES * P), "cq rstd")
                    if j == 8:
                        B.wait("pe", "ckv sum")
                        rsqrt(B, wt(16), wb[:, 0:TOK], wt(16), 1.0 / (KV_TILES * P), "ckv rstd")
                B.wait("dve", "ckv normed")
                act.dma_start(io["new_ckv"][l, :, :, :], W[:, 4:6, 0:CTX]).then_inc(latent_out, 16)
                for k in range(Q_TILES):
                    B.did(A(h_hi[:, k, :], wt(k), ACT.Copy), f"latent hi{k}")
                for k in range(KV_TILES):
                    at = k * KEYS
                    B.did(A(h_hi[:, 4:7, :].rearrange("p a n -> p (a n)")[:, at:at + TOK], wt(4 + k), ACT.Copy),
                          f"latent hi{Q_TILES + k}")
                B.wait("pe", "key pe")
                B.link(A(kp[:, 0:TOK], wa[:, 0:TOK], ACT.Copy), "key pe taken")
                act.wait_ge(cache_in, (l + 1) * 48)
                act.wait_ge(latent_out, (l + 1) * 32)
                B.did(act.nop())
                B.end()

                with act.Fori(0, H_B) as h:
                    B = s_mla.body("act", act, l * H_B + h)
                    B.wait("pe", "q nope")
                    B.did(A(halves(wt(0)), pj[0][:, :, 0:HALF], ACT.Copy), "q nope taken")
                    B.wait("pe", "k nope")
                    B.did(A(halves(flat(2, KEYS)), pj[0][:, :, 0:KEYS // 2], ACT.Copy), "k nope taken")
                    B.wait("pe", "v")
                    B.did(A(halves(flat(4, KEYS)), pj[1][:, :, 0:KEYS // 2], ACT.Copy), "v taken")
                    for m in range(TILES + 1):
                        if m < TILES:
                            t = MLA_ORDER[m]
                            nk = P if t == 0 else TOK
                            B.wait("dve", f"max{m}")
                            if m >= 2:
                                B.wait("pe", f"turned{m - 2}")
                            B.did(A(W[:, 6 + 4 * (m % 2), 0:nk], MLA_SCORES[m % 2][:, 0:nk], ACT.Exp,
                                    bias=mxs[:, 1, t:t + 1], scale=SM_SCALE, accum_out=mxs[:, 2, t:t + 1]), f"exp{m}")
                        if m >= 1:
                            t = MLA_ORDER[m - 1]
                            nk = P if t == 0 else TOK
                            B.wait("pe", f"turned{m - 1}")
                            if m >= 3:
                                B.wait("pe", f"o{m - 3}")
                            B.did(A(W[:, 7 + 4 * ((m - 1) % 2), 0:nk], MLA_PS[(m - 1) % 2][:, 0:nk], ACT.Copy),
                                  f"turned taken{m - 1}")
                    B.end()

                B = s_spl.body("act", act, l)
                for k in range(H_B):
                    B.did(A(h_hi[:, k, :], xo[:, H_A + k, :], ACT.Copy), f"hi{k}")
                B.end()
                with act.Fori(0, KT // 2) as f:
                    B = s_out.body("act", act, l * (KT // 2) + f)
                    for j, name in enumerate(("first", "second")):
                        B.wait("pe", name)
                        B.did(A(halves(wt(j)), pj[j][:, :, 0:HALF], ACT.Square), f"square{j}")
                    B.end()

                B = s_res.body("act", act, l)
                for k in range(4):
                    act.dma_start(wt(10 + k), x_kept[:, k, :]).then_inc(x_back[k], 16)
                B.wait("pe", "sum")
                rsqrt(B, halves(wt(5)), pj[0][:, :, 0:HALF], halves(wt(4)), 1.0 / D_MODEL, "rstd")
                for k in range(4, KT + 4):
                    B.wait("dve", f"added{k - 4}")
                    if k < KT:
                        act.dma_start(wt(10 + k % 4), x_kept[:, k, :]).then_inc(x_back[k % 4], 16)
                    if k % 4 == 3:
                        act.dma_start(io["y"][:, k - 7:k - 3, :], xo[:, k - 7:k - 3, :]).then_inc(y_out, 16)
                act.wait_ge(y_out, (l + 1) * (KT // 4 * 16))
                B.did(act.nop())
                B.end()

        @block.vector
        def _(dve):
            V = nc.vector
            tt, ts, stt = V.tensor_tensor, V.tensor_scalar, V.scalar_tensor_tensor

            def sigmoid_from_exp(B, ap, label=None):
                B.link(ts(ap, ap, 1.0, None, ALU.add))
                B.link(V.reciprocal(ap, ap), label)

            B = s_init.body("dve", dve, None)
            B.did(V.memset(cst[:, 0:1], EPS))
            B.did(V.memset(cst[:, 1:2], math.log(DK_SCALE)), "eps")
            dve.wait_ge(const_in, 48)
            B.wait("act", "cond exp")
            sigmoid_from_exp(B, cond[:, :, :])
            B.link(tt(cond[:, :, :], cond[:, :, :], cond_t[:, :, :], ALU.mult))
            B.end()
            with dve.Fori(0, DEPTH) as l:
                dve.wait_ge(params_in, (l + 1) * 16)
                dve.sem_inc(s_init.passed, 1)
                def par(name, n):
                    return prm[:, PRM[name]:PRM[name] + n]

                N = s_norm.body("dve", dve, l)
                def ada_turn(i):
                    B = s_ada.body("dve", dve, l * ADA_PAIRS + i)
                    b = PRM["b_ada"]
                    used = dve.snap(l * per_layer + i * (2 * KT // RAW_SLOTS) + 1)
                    for j in range(2):
                        dve.wait_ge(raw_free[RAW_SLOTS - 1], used + (j + 1) * (KT // RAW_SLOTS))
                        B.did(V.tensor_copy(flat(13 + 2 * j, ADA_COLS)[0:2, :], (wa, wb)[j][0:2, :]), f"rows{j}")
                        B.wait("pe", f"turned{j}")
                        at = (2 * i + j) * ADA_TILES
                        B.did(tt(mod[:, bass.ds(at, ADA_TILES), :],
                                 pj[0][:, 0, j * 2 * ADA_TILES:(j + 1) * 2 * ADA_TILES].rearrange("p (a b) -> p a b", b=2),
                                 prm[:, bass.ds(at + b, ADA_TILES)].unsqueeze(2).to_broadcast([P, ADA_TILES, 2]), ALU.add))
                    B.end()

                per_layer = (ADA_HALVES + STREAM_HALVES) // RAW_SLOTS
                with dve.Fori(0, ADA_PAIRS - 1) as i:
                    ada_turn(i)
                dve.wait_ge(x_saved, (l + 1) * 16)
                N.wait("act", "rstd")
                for k in range(KT):
                    N.did(tt(xo[:, k, :], xo[:, k, :], wt(5), ALU.mult), f"scaled{k}")
                ada_turn(ADA_PAIRS - 1)

                N.link(stt(mul[:, :, :], mod[:, KT:2 * KT, :], 1.0,
                           par("g_pre", KT).unsqueeze(2).to_broadcast([P, KT, 2]), ALU.add, ALU.mult))
                for k in range(KT + 1):
                    if k < KT:
                        u = wt(6 + k % 4)
                        N.did(ts(u[:, 0:CTX], xo[:, k, 0:CTX], mul[:, k, 0:1], mod[:, k, 0:1], ALU.mult, ALU.add))
                        N.link(ts(u[:, CTX:TOK], xo[:, k, CTX:TOK], mul[:, k, 1:2], mod[:, k, 1:2], ALU.mult, ALU.add),
                               f"u{k}")
                    if k:
                        N.wait("act", f"hi{k - 1}")
                        N.did(tt(h_lo[:, k - 1, :], wt(6 + (k - 1) % 4), h_hi[:, k - 1, :].bitcast(F32), ALU.subtract),
                              f"h{k - 1}")
                N.end()

                B = s_gate.body("dve", dve, l)
                resF, resB = W[0:8, 6:8, :], W[0:8, 8:10, :]
                B.did(V.memset(resF, 1.0))
                B.link(V.memset(resB, 1.0))
                B.did(V.memset(resF.rearrange("p a (t c) -> p (a t) c", c=P)[:, :, 0:1], 0.0))
                B.link(V.memset(resB.rearrange("p a (t c) -> p (a t) c", c=P)[:, :, P - 1:P], 0.0))
                B.wait("act", "exp a_log")
                B.link(ts(colt[0:8, 1, 0:1], colt[0:8, 0, 0:1], -1.0, None, ALU.mult))
                B.wait("act", "beta exp")
                sigmoid_from_exp(B, W[0:8, 14, :], "beta")
                B.wait("act", "log")
                B.link(stt(W[0:8, 4:6, :], W[0:8, 0:2, :], 0.0, W[0:8, 2:4, :], ALU.max, ALU.add))
                B.did(ts(W[0:8, 4, :], W[0:8, 4, :], colt[0:8, 1, 0:1], None, ALU.mult))
                B.link(ts(W[0:8, 5, :], W[0:8, 5, :], -1.0, None, ALU.mult))

                def fl(a):
                    return W[0:8, a:a + 2, :].rearrange("p a n -> p (a n)")
                B.did(V.tensor_tensor_scan(fl(10), fl(6), fl(4), 0.0, ALU.mult, ALU.add))
                B.link(V.tensor_tensor_scan(fl(12)[:, ::-1], fl(8)[:, ::-1], fl(4)[:, ::-1], 0.0,
                                            ALU.mult, ALU.add), "cum")
                B.did(tt(W[0:8, 0, :], W[0:8, 15, :], W[0:8, 11, :], ALU.subtract), "aF")
                B.did(tt(W[0:8, 1, :], W[0:8, 15, :], W[0:8, 13, :], ALU.subtract), "aB")
                B.link(V.memset(W[0:8, 4:6, :], 0.0))
                d0F, d0B = W[0:8, 4, :], W[0:8, 5, :]
                B.did(V.tensor_copy(tiled(d0F)[:, 2:5, 0:1], tiled(W[0:8, 11, :])[:, 1:4, P - 1:P]))
                B.link(V.tensor_copy(tiled(d0B)[:, 1:4, P - 1:P], tiled(W[0:8, 13, :])[:, 2:5, 0:1]))
                dve.wait_ge(m0_in, (l + 1) * 16)
                MF, MB = W[0:8, 2, :], W[0:8, 3, :]
                scan = V.tensor_tensor_scan
                B.did(scan(MF[:, 0:CTX], d0F[:, 0:CTX], W[0:8, 0, 0:CTX], 0.0, ALU.add, ALU.max))
                B.did(scan(MF[:, CTX:TOK], d0F[:, CTX:TOK], W[0:8, 0, CTX:TOK], m0[:, 0:1], ALU.add, ALU.max))
                B.did(scan(MB[:, 0:CTX][:, ::-1], d0B[:, 0:CTX][:, ::-1], W[0:8, 1, 0:CTX][:, ::-1], 0.0,
                           ALU.add, ALU.max))
                B.link(scan(MB[:, CTX:TOK][:, ::-1], d0B[:, CTX:TOK][:, ::-1], W[0:8, 1, CTX:TOK][:, ::-1],
                            m0[:, 0:1], ALU.add, ALU.max))
                B.did(V.memset(mprev[:, :, 0:1], 0.0))
                B.did(V.tensor_copy(mprev[:, 0, 1:2], m0[:, :]))
                B.did(V.tensor_copy(mprev[:, 1, 4:5], m0[:, :]))
                B.did(tt(mprev[:, 0, 2:5].unsqueeze(2), tiled(MF)[:, 1:4, P - 1:P],
                         tiled(W[0:8, 11, :])[:, 1:4, P - 1:P], ALU.add))
                B.did(tt(mprev[:, 1, 1:4].unsqueeze(2), tiled(MB)[:, 2:5, 0:1],
                         tiled(W[0:8, 13, :])[:, 2:5, 0:1], ALU.add))
                B.did(tt(mout[:, 0:1], MF[:, P - 1:P], W[0:8, 11, P - 1:P], ALU.add))
                B.link(tt(mout[:, 1:2], MB[:, 0:1], W[0:8, 13, 0:1], ALU.add))
                for d, M in ((0, MF), (1, MB)):
                    B.did(tt(tiled(W[0:8, 6 + d, :]), mprev[:, d, :].unsqueeze(2).to_broadcast([8, TILES, P]),
                             tiled(M), ALU.subtract), "wi")
                for d, M in ((0, MF), (1, MB)):
                    B.did(tt(W[0:8, 8 + d, :], M, W[0:8, 11 + 2 * d, :], ALU.add), "em")
                B.end()

                with dve.Fori(0, H_A) as h:
                    B = s_gdn.body("dve", dve, l * H_A + h)
                    for pad in pads:
                        B.did(V.memset(pad[:, 0:2], 0.0))
                        B.did(V.memset(pad[:, 2 + CTX:6 + CTX], 0.0))
                        B.did(V.memset(pad[:, 6 + TOK:8 + TOK], 0.0), "zeros")
                    cw = PRM["conv"]
                    for i in range(3):
                        B.link(ts(hcw[:, i, :], prm[:, bass.ds(h * CONV_K + (cw + i * H_A * CONV_K), CONV_K)],
                                  1.0, None, ALU.mult))

                    def conv(i):
                        x, cv = "qkv"[i], convs[i]
                        B.wait("act", f"{x} padded")
                        B.link(ts(cv, pads[i][:, 0:CONVW], hcw[:, i, 0:1], None, ALU.mult))
                        for j in range(1, CONV_K):
                            B.link(stt(cv, pads[i][:, j:j + CONVW], hcw[:, i, j:j + 1], cv, ALU.mult, ALU.add),
                                   f"{x} conv" if j == CONV_K - 1 else None)

                    def silu(i, y):
                        x, cv = "qkv"[i], convs[i]
                        B.wait("act", f"{x} sigmoid")
                        B.did(tt(y[:, 0:CTX], cv[:, 0:CTX], pads[i][:, 0:CTX], ALU.mult))
                        B.link(tt(y[:, CTX:TOK], cv[:, CTX + 4:CONVW], pads[i][:, CTX + 4:CONVW], ALU.mult), f"{x} silu")

                    conv(0)
                    conv(1)
                    silu(0, wt(0))
                    conv(2)
                    silu(1, wt(1))
                    silu(2, wt(4))
                    B.wait("act", "q rstd")
                    B.did(tt(wt(0), wt(0), wt(10), ALU.mult), "q normed")
                    B.wait("act", "k rstd")
                    B.link(tt(wt(1), wt(1), wt(12), ALU.mult), "k normed")
                    B.wait("act", "z sigmoid")
                    B.link(tt(xt(8), xt(7), xt(9), ALU.mult), "z ready")
                    B.wait("act", "v turned taken")
                    for d in range(2):
                        last_at = P - 1 if d == 0 else 0
                        dve.wait_ge(rows_in[d], (l * H_A + h + 1) * 32)
                        c = 6 * d
                        B.did(ts(colt[:, c, :], tokc[:, d, :, bass.ds(h + 4 * d, 1)].rearrange("p t o -> p (t o)"), 1.0, None, ALU.mult))
                        B.link(ts(colt[:, c + 1, :], tokc[:, 2, :, bass.ds(h + 4 * d, 1)].rearrange("p t o -> p (t o)"), 1.0, None, ALU.mult))
                        B.link(tt(colt[:, c + 4, :].unsqueeze(2), tiled(row_g[d])[:, :, last_at:last_at + 1],
                                  colt[:, c, :].unsqueeze(2), ALU.subtract), f"cols{d}")
                        B.did(tt(KB[d], wt(1), row_beta[d], ALU.mult), f"kb{d}")
                        B.link(tt(tiled(DECAY[d]), tiled(row_g[d]), over_cols(colt[:, c, :]), ALU.subtract))
                        B.link(tt(tiled(DECAY[d]), tiled(DECAY[d]), over_tiles(neg(d)), ALU.add), f"gap{d}")
                    for d in range(2):
                        B.wait("act", f"decay{d}")
                        B.wait("pe", f"kk{d}")
                        B.link(tt(KK[d], wa[:, 0:TOK], DECAY[d], ALU.mult), f"kk decayed{d}")
                        B.wait("pe", f"qk{d}")
                        B.link(tt(QK[d], wb[:, 0:TOK], DECAY[d], ALU.mult), f"qk decayed{d}")

                    def blocks(d, v, label=None):
                        B.link(tt(tiled(LEVEL[d]), tiled(KK[d]), over_tiles(lvl[:, d, v, :]), ALU.mult), label)
                    for d in range(2):
                        blocks(d, 0, f"level{d}0")
                        B.link(tt(tiled(INV_T[d]), over_tiles(ident), tiled(LEVEL[d]), ALU.subtract))
                    for d in range(2):
                        B.wait("pe", f"ld{d}0")
                        blocks(d, 1)
                        B.link(tt(tiled(INV[d]), over_tiles(ident), tiled((wa, wb)[d][:, 0:TOK]), ALU.subtract), f"level{d}1")
                    for v in range(1, LEVELS):
                        if v < LEVELS - 1:
                            for d in range(2):
                                B.wait("pe", f"ld{d}{v}")
                                blocks(d, v + 1)
                            for d in range(2):
                                B.wait("pe", f"dld{d}{v}")
                                B.link(tt(INV[d], INV[d], (wa, wb)[d][:, 0:TOK], ALU.subtract), f"inv{d}{v}")
                        for d in range(2):
                            B.wait("pe", f"dldT{d}{v}")
                            B.link(tt(INV_T[d], INV_T[d], (wa, wb)[d][:, 0:TOK], ALU.subtract),
                                   f"inverse{d}" if v == LEVELS - 1 else f"level{d}{v + 1}")
                    for d in range(2):
                        last_at = P - 1 if d == 0 else 0
                        c = 6 * d
                        B.wait("act", f"kdec col{d}")
                        B.link(tt(colt[:, c + 3, :], colt[:, c + 1, :], colt[:, c + 2, :], ALU.mult))
                        B.did(tt(tiled(wt(14)), tiled(wt(3)), over_cols(colt[:, c + 1, :]), ALU.mult))
                        B.did(tt(tiled(wt(15)), tiled(wt(2)), over_cols(colt[:, c + 3, :]), ALU.mult), f"kbg{d}")
                        B.wait("act", f"eg{d}")
                        B.did(tt(wt(13), wt(0), wt(8), ALU.mult))
                        B.did(tt(tiled(wt(10)), tiled(wt(2)), over_cols(colt[:, c + 5, :]), ALU.mult), f"kdec{d}")
                        for n in range(TILES):
                            t = n if d == 0 or n == 0 else TILES - n
                            B.wait("pe", f"kv{d}{n}")
                            if n == 0:
                                B.link(V.tensor_copy(state[:, 0, 0:P], wb[:, 0:P]), f"state{d}0")
                            else:
                                e = t * P + last_at
                                B.link(stt(state[:, 1, 0:P], state[:, 1, 0:P], W[:, 8, e:e + 1], wb[:, 0:P],
                                           ALU.mult, ALU.add), f"state{d}{n}")
                            if d == 0:
                                B.link(V.tensor_copy(T(wt(4), t), wa[:, 512:512 + P]), f"o taken{d}{n}")
                            else:
                                B.link(tt(T(wt(4), t), T(wt(4), t), wa[:, 512:512 + P], ALU.add), f"o taken{d}{n}")
                        if d == 0:
                            dve.wait_ge(state_out[0], (l * H_A + h + 1) * 16)
                    B.did(V.memset(cst[:, 2:3], 0.0), "o whole")
                    B.wait("act", "o rstd")
                    B.link(stt(wt(4), wt(4), par("gdn_norm", 1), wt(7), ALU.mult, ALU.mult))
                    B.did(tt(xo[:, bass.ds(h, 1), :].rearrange("p a n -> p (a n)"), wt(4), xt(8), ALU.mult))
                    B.end()

                with dve.Fori(0, H_C) as h:
                    B = s_mls.body("dve", dve, l * H_C + h)
                    B.wait("pe", "v turned")
                    B.did(V.tensor_copy(wt(4), wb[:, 0:TOK]), "v turned taken")
                    for d in range(2):
                        last_at = P - 1 if d == 0 else 0
                        dve.wait_ge(crows_in[d], (l * H_C + h + 1) * 48)
                        B.link(ts(colt[:, 0, :], tokc[:, 3 + d, :, bass.ds(h + 4 * d, 1)].rearrange("p t o -> p (t o)"), 1.0, None, ALU.mult))
                        B.did(tt(colt[:, 4, :].unsqueeze(2), colt[:, 0, :].unsqueeze(2),
                                 tiled(MROWS[d][0])[:, :, last_at:last_at + 1], ALU.subtract))
                        B.link(tt(tiled(wt(8)), over_cols(colt[:, 0, :]), tiled(MROWS[d][0]), ALU.subtract))
                        B.link(tt(tiled(wt(8)), tiled(wt(8)), over_tiles(neg(d)), ALU.add), f"gap{d}")
                        B.wait("act", "q taken")
                        B.did(tt(wt(10), wt(0), MROWS[d][1], ALU.mult))
                        B.wait("act", f"wk col{d}")
                        B.did(tt(tiled(wt(11)), tiled(wt(3)), over_cols(colt[:, 5, :]), ALU.mult))
                        B.wait("pe", f"qk{d}")
                        B.link(tt(wt(9), wa[:, 0:TOK], wt(8), ALU.mult), f"s{d}")
                        dve.wait_ge(cstate_in[d], (l * H_C + h + 1) * 32)
                        B.did(ts(state[:, 1, P:2 * P], ones, n0[:, 0:1], None, ALU.mult), f"n rep{d}")
                        for n in range(TILES):
                            t = n if d == 0 or n == 0 else TILES - n
                            B.wait("pe", f"kv{d}{n}")
                            if n == 0:
                                B.link(V.tensor_copy(state[:, 0, :], wb[:, 0:2 * P]), f"state{d}0")
                            else:
                                e = t * P + last_at
                                B.link(stt(state[:, 1, :], state[:, 1, :], MROWS[d][1][:, e:e + 1], wb[:, 0:2 * P],
                                           ALU.mult, ALU.add), f"state{d}{n}")
                            q = W[:, 16, 0:P]
                            B.link(stt(q, wa[:, 512:512 + P], -1.0, T(MROWS[d][2], t), ALU.mult, ALU.max))
                            B.link(tt(q, q, wa[:, 512:512 + P], ALU.max))
                            B.link(V.reciprocal(q, q))
                            if d == 0:
                                B.link(tt(T(wt(12), t), wa[:, 0:P], q, ALU.mult), f"h taken{d}{n}")
                            else:
                                B.link(tt(q, wa[:, 0:P], q, ALU.mult), f"h taken{d}{n}")
                                B.link(tt(T(wt(12), t), T(wt(12), t), q, ALU.add))
                        if d == 0:
                            dve.wait_ge(cstate_out[0], (l * H_C + h + 1) * 32)
                            B.did(V.memset(cst[:, 2:3], 0.0), "hB ready")
                            B.wait("act", "z sigmoid")
                            B.link(tt(wt(14), xt(8), wt(15), ALU.mult), "oz ready")
                            B.did(tt(wt(14), wt(14), wt(13), ALU.mult))
                    B.did(V.memset(cst[:, 2:3], 0.0), "h whole")
                    B.wait("act", "h rstd")
                    B.link(stt(wt(12), wt(12), par("mlstm_norm", 1), wt(7), ALU.mult, ALU.mult))
                    B.did(tt(xo[:, bass.ds(h + (H_A + H_B), 1), :].rearrange("p a n -> p (a n)"), wt(12), wt(14), ALU.mult))
                    B.end()

                B = s_min.body("dve", dve, l)
                kvh = h_hi[:, 4:7, :].rearrange("p a n -> p (a n)")
                kvl = h_lo[:, 4:7, :].rearrange("p a n -> p (a n)")
                B.wait("act", "cq squared1")
                B.link(tt(wt(8), wt(14), wt(16), ALU.add), "cq added")
                for k in range(2, Q_TILES):
                    B.wait("act", f"cq squared{k}")
                    B.link(tt(wt(8), wt(8), wt(14 + 2 * (k % 2)), ALU.add), "cq squares")
                B.wait("act", "ckv squared1")
                B.link(tt(wt(7), wt(14), wt(16), ALU.add), "ckv squares")
                for j in range(7, 15):
                    e, x = wt(10 + 2 * (j % 2)), wt(11 + 2 * (j % 2))
                    B.wait("act", f"zb sigmoid{j}")
                    B.did(tt(xo[:, H_A + j - 7, :], x, e, ALU.mult), f"zb{j}")
                    if j == 7:
                        B.wait("act", "cq rstd")
                        for k in range(Q_TILES):
                            B.did(stt(wt(k), wt(k), par("q_norm", 4)[:, k:k + 1], wt(14), ALU.mult, ALU.mult))
                    if j == 9:
                        B.wait("act", "ckv rstd")
                        for k in range(KV_TILES):
                            B.link(stt(wt(4 + k), wt(4 + k), par("kv_norm", 2)[:, k:k + 1], wt(16), ALU.mult, ALU.mult),
                                   "ckv normed")
                        B.link(tt(wt(7), wt(6), con[:, C_ROPE:C_ROPE + TOK], ALU.mult), "roped")
                B.wait("pe", "tile14")
                dve.wait_ge(cache_in, (l + 1) * 48)
                for k in range(KV_TILES):
                    s = slice(k * KEYS + TOK, (k + 1) * KEYS)
                    c = flat(15, 2 * P)[:, k * P:(k + 1) * P]
                    B.link(V.tensor_copy(kvh[:, s], c))
                    B.did(tt(kvl[:, s], c, kvh[:, s].bitcast(F32), ALU.subtract))
                for k in range(Q_TILES):
                    B.wait("act", f"latent hi{k}")
                    B.did(tt(h_lo[:, k, :], wt(k), h_hi[:, k, :].bitcast(F32), ALU.subtract))
                for k in range(KV_TILES):
                    s = slice(k * KEYS, k * KEYS + TOK)
                    B.wait("act", f"latent hi{Q_TILES + k}")
                    B.did(tt(kvl[:, s], wt(4 + k), kvh[:, s].bitcast(F32), ALU.subtract))
                B.end()

                with dve.Fori(0, H_B) as h:
                    B = s_mla.body("dve", dve, l * H_B + h)
                    B.wait("pe", "q pe")
                    B.did(tt(halves(wt(1)), pj[1][:, :, 0:HALF], halves(con[:, C_ROPE:C_ROPE + TOK]), ALU.mult), "q pe roped")
                    for m in range(2):
                        src = xo[:, 12 * m:12 * m + 4, bass.ds(h * STRIP, STRIP)]
                        hi, lo = (x[:, 8 + 4 * m:12 + 4 * m, bass.ds(h * STRIP, STRIP)] for x in (h_hi, h_lo))
                        B.link(ts(hi, src, 1.0, None, ALU.mult))
                        B.did(tt(lo, src, hi.bitcast(F32), ALU.subtract))

                    def taken(m):
                        t = MLA_ORDER[m]
                        B.wait("pe", f"o{m}")
                        o = xo[:, bass.ds(h + H_A, 1), t * P:(t + 1) * P].rearrange("p a n -> p (a n)")
                        B.did(tt(o, o, MLA_PS[m % 2][:, 768:768 + P], ALU.mult), f"o taken{m}")

                    for m in range(TILES):
                        t = MLA_ORDER[m]
                        nk = P if t == 0 else TOK
                        B.wait("pe", f"scores{m}")
                        B.link(V.reduce_max(mxs[:, 0, t:t + 1], MLA_SCORES[m % 2][:, 0:nk], AX))
                        B.link(ts(mxs[:, 1, t:t + 1], mxs[:, 0, t:t + 1], -SM_SCALE, None, ALU.mult), f"max{m}")
                        if m >= 2:
                            taken(m - 2)
                        B.wait("act", f"exp{m}")
                        B.link(V.reciprocal(mxs[:, 3, t:t + 1], mxs[:, 2, t:t + 1]))
                        p = W[:, 6 + 4 * (m % 2), 0:nk]
                        B.link(ts(p, p, mxs[:, 3, t:t + 1], None, ALU.mult), f"normed{m}")
                    taken(TILES - 2)
                    taken(TILES - 1)
                    B.end()

                B = s_spl.body("dve", dve, l)
                B.did(V.memset(wt(8), 0.0))
                for k in range(H_B):
                    B.wait("act", f"hi{k}")
                    B.did(tt(h_lo[:, k, :], xo[:, H_A + k, :], h_hi[:, k, :].bitcast(F32), ALU.subtract))
                B.end()
                with dve.Fori(0, KT // 2) as f:
                    B = s_out.body("dve", dve, l * (KT // 2) + f)
                    B.did(V.memset(cst[:, 2:3], 0.0), "begun")
                    for j in range(2):
                        B.wait("act", f"square{j}")
                        B.did(ts(xo[:, bass.ds(2 * f + j, 1), :].rearrange("p a (b n) -> p (a b) n", b=2),
                                 pj[j][:, :, 0:HALF], 1.0, None, ALU.mult), f"taken{j}")
                        B.link(tt(wt(8), wt(8), wt(j), ALU.add))
                    B.end()

                B = s_res.body("dve", dve, l)
                B.did(V.memset(cst[:, 2:3], 0.0), "y squared")
                B.link(tt(mul[:, :, :], mod[:, 2 * KT:3 * KT, :],
                          par("g_post", KT).unsqueeze(2).to_broadcast([P, KT, 2]), ALU.mult))
                B.wait("act", "rstd")
                for k in range(KT):
                    u, x = wt(6 + k % 2), wt(10 + k % 4)
                    B.link(tt(u, xo[:, k, :], wt(5), ALU.mult))
                    dve.wait_ge(x_back[k % 4], (l * (KT // 4) + (k // 4 + 1)) * 16)
                    B.did(stt(xo[:, k, 0:CTX], u[:, 0:CTX], mul[:, k, 0:1], x[:, 0:CTX], ALU.mult, ALU.add))
                    B.did(stt(xo[:, k, CTX:TOK], u[:, CTX:TOK], mul[:, k, 1:2], x[:, CTX:TOK], ALU.mult, ALU.add),
                          f"added{k}")
                B.end()


def column_tiles(w, picks):
    depth, rows_, _ = w.shape
    w = np.concatenate([w, np.zeros((depth, rows_, 1), w.dtype)], axis=2)
    w = w[:, :, np.concatenate(picks)]
    w = w.reshape(depth, rows_ // (CELLS * P), CELLS, P, len(picks), P)
    return w.transpose(0, 4, 1, 3, 2, 5).reshape(depth, -1, P, CELLS * P)


def small_cells(w, picks):
    depth, rows_, _ = w.shape
    w = w[:, :, np.concatenate(picks)].reshape(depth, rows_ // P, P, len(picks) // 2, 2, P)
    w = w.transpose(0, 3, 2, 1, 4, 5).reshape(depth, len(picks) // 2, P, -1)
    fill = np.zeros(w.shape[:3] + (CELLS * P - w.shape[3],), w.dtype)
    return np.concatenate([w, fill], axis=3)


def swapped(first):
    at = np.arange(64)
    return np.concatenate([first + at, first + (at // 32) * 32 + (at % 32 + 16) % 32])


def constants():
    con = np.zeros((P, C_WIDTH), np.float32)
    j, i = np.arange(P)[:, None], np.arange(P)[None, :]
    con[:, C_ID:C_ID + P] = np.eye(P)
    con[:, C_ONE:C_ONE + P] = 1
    con[:, C_NEG:C_NEG + P] = np.where(i >= j, 0, NEG)
    con[:, C_NEG + P:C_NEG + 2 * P] = np.where(i <= j, 0, NEG)
    con[:, C_FOLD:C_FOLD + P] = i % 64 == j % 64
    inv = np.float32(10000.0) ** (-np.arange(0, 32, 2, dtype=np.float32) / np.float32(32))
    at = np.arange(LAT)
    angle = np.concatenate([(at // 64).astype(np.float32)[None] * np.tile(inv, 2)[:, None],
                            (at % 64).astype(np.float32)[None] * np.tile(inv, 2)[:, None]])
    sign = np.where(np.arange(64) % 32 < 16, -1, 1)[:, None]
    con[:64, C_ROPE:C_ROPE + CTX] = 1
    con[:64, C_ROPE + CTX:] = np.cos(angle)
    con[64:, C_ROPE + CTX:] = np.sin(angle) * sign
    lvl = np.zeros((P, 2, LEVELS, P), np.float32)
    for v in range(LEVELS):
        b = 1 << v
        pair = i // (2 * b) == j // (2 * b)
        lvl[:, 0, v] = pair & (i // b % 2 == 1) & (j // b % 2 == 0)
        lvl[:, 1, v] = pair & (i // b % 2 == 0) & (j // b % 2 == 1)
    return con, lvl.astype(np.float16)


def features_first(x):
    return x.T.reshape(-1, P, x.shape[0]).transpose(1, 0, 2)


def kernel(x_prompt, x_sample, cache_mla_ckv, cache_mla_krope, state_gdn, state_mlstm_c,
           state_mlstm_n, state_mlstm_m, c, c_ctx, w_ada, b_ada, g_pre, g_post, w_in,
           gdn_conv, gdn_a_log, gdn_dt_bias, gdn_norm, mla_q_norm, mla_kv_norm,
           mla_w_uq, mla_w_ukv, mlstm_b_i, mlstm_b_f, mlstm_norm, w_out):
    import concourse.bacc as bacc
    from concourse.bass_utils import run_bass_kernel_spmd

    con, lvl = constants()
    L = DEPTH

    def cols(a, n):
        return a.reshape(L, n, P).transpose(0, 2, 1)

    at = np.cumsum([0, 512, 512, 512, 512, 8, 8, 512, 256, 64, 1024, 512, 512, 512, 512, 512, 8, 8])
    qa, ka, va, za, ga, ba, cq, ckv, kr, zb, qc, kc, vc, oc, zc, ic, fc = at[:17]

    def tile(first, n=0):
        return first + n * P + np.arange(P)
    gates = np.full(P, -1)
    for quadrant, first in enumerate((ga, ba, ic, fc)):
        gates[32 * quadrant:32 * quadrant + 8] = first + np.arange(8)
    picks = [gates]
    for h in range(H_A):
        picks += [tile(x, h) for x in (qa, ka, va, za)]
    for h in range(H_C):
        picks += [tile(x, h) for x in (qc, kc, vc, oc, zc)]
    picks += [tile(cq, n) for n in range(4)] + [tile(ckv, n) for n in range(2)] + [swapped(kr)]
    picks += [tile(zb, n) for n in range(8)]
    uq = small_cells(mla_w_uq, sum([[h * 192 + np.arange(P), swapped(h * 192 + P)] for h in range(H_B)], []))
    ukv = small_cells(mla_w_ukv, sum([[h * 256 + np.arange(P), h * 256 + P + np.arange(P)] for h in range(H_B)], []))
    heads = np.stack([uq, ukv], axis=2).reshape(L, 2 * H_B, P, CELLS * P)
    rows_ = np.concatenate([tile(0, n) for n in list(range(4)) + list(range(12, 16)) + list(range(4, 12))])
    stream = np.concatenate([column_tiles(w_in, picks), heads,
                             column_tiles(w_out[:, rows_], [tile(0, f) for f in range(KT)])], axis=1)
    params = np.zeros((L, P, PRM_WIDTH), np.float32)

    def put(name, a):
        params[:, :a.shape[1], PRM[name]:PRM[name] + a.shape[2]] = a
    put("b_ada", cols(b_ada, 48))
    put("g_pre", cols(g_pre, KT))
    put("g_post", cols(g_post, KT))
    put("conv", gdn_conv.reshape(L, CONV_K, 12, P).transpose(0, 3, 2, 1).reshape(L, P, 12 * CONV_K))
    put("gdn_norm", gdn_norm[:, :, None])
    put("q_norm", cols(mla_q_norm, 4))
    put("kv_norm", cols(mla_kv_norm, 2))
    put("mlstm_norm", mlstm_norm[:, :, None])
    put("gates", np.stack([a.reshape(L, 8) for a in (gdn_a_log, gdn_dt_bias, mlstm_b_i, mlstm_b_f)], axis=2))

    arrays = {
        "constants": con, "levels": lvl, "params": params,
        "x": features_first(np.concatenate([x_prompt[0], x_sample[0]], axis=0)),
        "cond": np.stack([c_ctx.reshape(KT, P).T, c[0].reshape(KT, P).T], axis=2),
        "w_ada": w_ada.reshape(L, KT, P, ADA_GROUPS, ADA_COLS).transpose(0, 3, 1, 2, 4).reshape(L, ADA_HALVES, P, ADA_COLS),
        "w_stream": stream,
        "state_gdn": state_gdn[0], "state_c": state_mlstm_c[0], "state_n": state_mlstm_n[0][..., None],
        "m0": state_mlstm_m[0].reshape(L, 8, 1),
        "cache_ckv": cache_mla_ckv[0].transpose(0, 2, 1).reshape(L, 2, P, PAST).transpose(0, 2, 1, 3).reshape(L, P, 2 * PAST),
        "cache_kr": cache_mla_krope[0].transpose(0, 2, 1),
    }
    arrays = {n: np.ascontiguousarray(a) for n, a in arrays.items()}
    outs = {"y": (P, KT, TOK), "new_ckv": (L, P, 2, CTX), "new_kr": (L, 64, CTX),
            "new_gdn": (L, 2, H_A, P, P), "new_c": (L, 2, H_C, P, P), "new_n": (L, 2, H_C, P, 1),
            "new_m": (L, 2, H_C, 1)}

    book = {}
    for _ in range(2):
        nc = bacc.Bacc("TRN2", target_bir_lowering=False, num_devices=1)
        io = {n: nc.dram_tensor(f"in_{n}", a.shape, F16 if n == "levels" else F32, kind="ExternalInput").ap()
              for n, a in arrays.items()}
        io.update({n: nc.dram_tensor(f"out_{n}", s, F32, kind="ExternalOutput").ap() for n, s in outs.items()})
        build(nc, io, book)
    r = run_bass_kernel_spmd(nc, [{f"in_{n}": a for n, a in arrays.items()}], core_ids=[0])
    got = {n: r.results[0][f"out_{n}"] for n in outs}
    y = got["y"].transpose(2, 1, 0).reshape(TOK, D_MODEL)
    return (y[None, :CTX], y[None, CTX:],
            got["new_ckv"].transpose(0, 3, 2, 1).reshape(1, L, CTX, 2 * P),
            got["new_kr"].transpose(0, 2, 1)[None],
            got["new_gdn"][None], got["new_c"][None], got["new_n"][None, ..., 0], got["new_m"][None, ..., 0])
```
